# Optimizing a Trainium2 kernel written in Bass

```python
import jax, jax.numpy as jnp
from jax import lax
import numpy as np
import math

D_MODEL = 1024
BATCH = 1
SEQ = 512
DEPTH = 1

MEM_LEN = 256
N_HEADS_MLA = 8
QK_NOPE_DIM = 64
QK_ROPE_DIM = 32
QK_HEAD_DIM = QK_NOPE_DIM + QK_ROPE_DIM
V_HEAD_DIM = 64
Q_LORA_RANK = 3 * D_MODEL // 8
KV_LORA_RANK = D_MODEL // 4
MLA_WIDTH = N_HEADS_MLA * V_HEAD_DIM
CONV_WIDTH = D_MODEL // 2
CONV_K = 3
N_HEADS_MEM = 4
MEM_HEAD_DIM = 128
MEM_WIDTH = N_HEADS_MEM * MEM_HEAD_DIM

N_BRANCH = 3
ROPE_BASE = 10000.0
Q_BLOCK = 128
EPS = 1e-6

IN_SIZES = (Q_LORA_RANK, KV_LORA_RANK, QK_ROPE_DIM,
            CONV_WIDTH, CONV_WIDTH, CONV_WIDTH,
            MEM_WIDTH,
            MLA_WIDTH, CONV_WIDTH, MEM_WIDTH,
            N_BRANCH * D_MODEL)
IN_WIDTH = sum(IN_SIZES)


def rmsnorm(t, g):
    tf = t.astype(jnp.float32)
    tf = tf * lax.rsqrt(jnp.mean(tf * tf, axis=-1, keepdims=True) + EPS)
    return tf.astype(t.dtype) * g

def split_cols(t, sizes):
    return jnp.split(t, np.cumsum(sizes)[:-1].tolist(), axis=-1)

def rope_tables(positions, dtype):
    inv_freq = ROPE_BASE ** (-jnp.arange(0, QK_ROPE_DIM, 2, dtype=jnp.float32) / QK_ROPE_DIM)
    ang = positions.astype(jnp.float32)[..., None] * inv_freq
    return (jnp.cos(ang)[:, :, None, :].astype(dtype),
            jnp.sin(ang)[:, :, None, :].astype(dtype))

def rope_tail(t, cos, sin):
    t_nope, t1, t2 = split_cols(t, (QK_NOPE_DIM, QK_ROPE_DIM // 2, QK_ROPE_DIM // 2))
    return jnp.concatenate([t_nope, t1 * cos - t2 * sin, t2 * cos + t1 * sin], axis=-1)

def blocked_bidirectional_attention(q, k, v):
    B, S, H, Dh = q.shape
    nblk = S // Q_BLOCK
    qb = q.reshape(B, nblk, Q_BLOCK, H, Dh).transpose(1, 0, 2, 3, 4)
    scale = Dh ** -0.5

    def one_block(q_blk):
        s = jnp.einsum('bqhd,bkhd->bhqk', q_blk, k).astype(jnp.float32) * scale
        p = jax.nn.softmax(s, axis=-1).astype(v.dtype)
        return jnp.einsum('bhqk,bkhd->bqhd', p, v)

    out = lax.map(one_block, qb)
    return out.transpose(1, 0, 2, 3, 4).reshape(B, S, H * v.shape[-1])

def centred_short_conv(z, w, b):
    out = lax.conv_general_dilated(
        z, w[:, None, :], window_strides=(1,),
        padding=((CONV_K // 2, CONV_K // 2),),
        dimension_numbers=('NWC', 'WIO', 'NWC'),
        feature_group_count=z.shape[-1])
    return out + b

def hybrid_layer(x, mem, cos, sin, norm_g, w_in, b_gate, q_norm_g, w_uq, kv_norm_g, w_ukv,
                 q_head_g, k_head_g, conv_w, conv_b, mem_norm_g, w_mkv, mem_q_g, mem_k_g,
                 w_br_attn, w_br_conv, w_br_mem, w_out):
    B, S, _ = x.shape
    M = mem.shape[1]
    h = rmsnorm(x, norm_g)
    proj = h @ w_in
    (q_lat, kv_lat, k_pe, c_b, c_c, c_u, q_mem,
     g_attn, g_conv, g_mem, r) = split_cols(proj, IN_SIZES)

    q = (rmsnorm(q_lat, q_norm_g) @ w_uq).reshape(B, S, N_HEADS_MLA, QK_HEAD_DIM)
    kv = (rmsnorm(kv_lat, kv_norm_g) @ w_ukv).reshape(B, S, N_HEADS_MLA, QK_NOPE_DIM + V_HEAD_DIM)
    k_nope, v = split_cols(kv, (QK_NOPE_DIM, V_HEAD_DIM))
    k_rope = jnp.broadcast_to(k_pe[:, :, None, :], (B, S, N_HEADS_MLA, QK_ROPE_DIM))
    k = jnp.concatenate([k_nope, k_rope], axis=-1)
    q = rope_tail(rmsnorm(q, q_head_g), cos, sin)
    k = rope_tail(rmsnorm(k, k_head_g), cos, sin)
    o_attn = blocked_bidirectional_attention(q, k, v) * jax.nn.silu(g_attn)

    o_conv = c_b * centred_short_conv(c_c * c_u, conv_w, conv_b) * jax.nn.silu(g_conv)

    mkv = (rmsnorm(mem, mem_norm_g) @ w_mkv).reshape(B, M, N_HEADS_MEM, 2 * MEM_HEAD_DIM)
    m_k, m_v = split_cols(mkv, (MEM_HEAD_DIM, MEM_HEAD_DIM))
    mq = rmsnorm(q_mem.reshape(B, S, N_HEADS_MEM, MEM_HEAD_DIM), mem_q_g)
    m_k = rmsnorm(m_k, mem_k_g)
    s = jnp.einsum('bshd,bmhd->bhsm', mq, m_k).astype(jnp.float32) * (MEM_HEAD_DIM ** -0.5)
    p = jax.nn.softmax(s, axis=-1).astype(m_v.dtype)
    o_mem = jnp.einsum('bhsm,bmhd->bshd', p, m_v).reshape(B, S, MEM_WIDTH) * jax.nn.silu(g_mem)

    r_attn, r_conv, r_mem = split_cols(jax.nn.sigmoid(r + b_gate), (D_MODEL, D_MODEL, D_MODEL))
    y = r_attn * (o_attn @ w_br_attn) + r_conv * (o_conv @ w_br_conv) + r_mem * (o_mem @ w_br_mem)
    return x + y @ w_out

def first_inputs(seed: int = 0) -> dict:
    key = jax.random.key(seed)
    ks = jax.random.split(key, 24)

    def nrm(k, shape, scale):
        return jax.random.normal(k, shape, jnp.float32) * scale

    def gain(k, shape):
        return 1.0 + 0.1 * jax.random.normal(k, shape, jnp.float32)

    x = nrm(ks[0], (BATCH, SEQ, D_MODEL), 1.0)
    mem = nrm(ks[1], (BATCH, MEM_LEN, D_MODEL), 1.0)
    offset = jax.random.randint(ks[2], (BATCH, 1), 0, 1024, dtype=jnp.int32)
    positions = jnp.arange(SEQ, dtype=jnp.int32)[None, :] + offset
    return {
        'x': x,
        'mem': mem,
        'positions': positions,
        'norm_g': gain(ks[3], (DEPTH, D_MODEL)),
        'w_in': nrm(ks[4], (DEPTH, D_MODEL, IN_WIDTH), D_MODEL ** -0.5),
        'b_gate': nrm(ks[5], (DEPTH, N_BRANCH * D_MODEL), 0.1),
        'q_norm_g': gain(ks[6], (DEPTH, Q_LORA_RANK)),
        'w_uq': nrm(ks[7], (DEPTH, Q_LORA_RANK, N_HEADS_MLA * QK_HEAD_DIM), Q_LORA_RANK ** -0.5),
        'kv_norm_g': gain(ks[8], (DEPTH, KV_LORA_RANK)),
        'w_ukv': nrm(ks[9], (DEPTH, KV_LORA_RANK, N_HEADS_MLA * (QK_NOPE_DIM + V_HEAD_DIM)), KV_LORA_RANK ** -0.5),
        'q_head_g': gain(ks[10], (DEPTH, QK_HEAD_DIM)),
        'k_head_g': gain(ks[11], (DEPTH, QK_HEAD_DIM)),
        'conv_w': nrm(ks[12], (DEPTH, CONV_K, CONV_WIDTH), CONV_K ** -0.5),
        'conv_b': nrm(ks[13], (DEPTH, CONV_WIDTH), 0.1),
        'mem_norm_g': gain(ks[14], (DEPTH, D_MODEL)),
        'w_mkv': nrm(ks[15], (DEPTH, D_MODEL, 2 * MEM_WIDTH), D_MODEL ** -0.5),
        'mem_q_g': gain(ks[16], (DEPTH, MEM_HEAD_DIM)),
        'mem_k_g': gain(ks[17], (DEPTH, MEM_HEAD_DIM)),
        'w_br_attn': nrm(ks[18], (DEPTH, MLA_WIDTH, D_MODEL), MLA_WIDTH ** -0.5),
        'w_br_conv': nrm(ks[19], (DEPTH, CONV_WIDTH, D_MODEL), CONV_WIDTH ** -0.5),
        'w_br_mem': nrm(ks[20], (DEPTH, MEM_WIDTH, D_MODEL), MEM_WIDTH ** -0.5),
        'w_out': nrm(ks[21], (DEPTH, D_MODEL, D_MODEL), D_MODEL ** -0.5),
    }

def first_block(x, mem, positions, norm_g, w_in, b_gate, q_norm_g, w_uq, kv_norm_g, w_ukv,
              q_head_g, k_head_g, conv_w, conv_b, mem_norm_g, w_mkv, mem_q_g, mem_k_g,
              w_br_attn, w_br_conv, w_br_mem, w_out):
    cos, sin = rope_tables(positions, x.dtype)
    for i in range(DEPTH):
        x = hybrid_layer(x, mem, cos, sin, norm_g[i], w_in[i], b_gate[i], q_norm_g[i], w_uq[i],
                         kv_norm_g[i], w_ukv[i], q_head_g[i], k_head_g[i], conv_w[i], conv_b[i],
                         mem_norm_g[i], w_mkv[i], mem_q_g[i], mem_k_g[i],
                         w_br_attn[i], w_br_conv[i], w_br_mem[i], w_out[i])
    return x


HEAD_DIM = 64
N_FOX_HEADS = 8
N_DIL_HEADS = 8
FOX_WIDTH = N_FOX_HEADS * HEAD_DIM
DIL_WIDTH = N_DIL_HEADS * HEAD_DIM
MIX_WIDTH = FOX_WIDTH + DIL_WIDTH
IN_WIDTH_2 = 3 * FOX_WIDTH + N_FOX_HEADS + 3 * DIL_WIDTH
DILATION_PATTERNS = ((128, 1), (512, 4), (2048, 16))
RMS_EPS = 1e-6
NEG_INF = -1e30

PEER_HEADS = 8
PEER_NKEYS = 128
PEER_EXPERTS = PEER_NKEYS * PEER_NKEYS
PEER_TOPK = 16
PEER_QDIM = 256
PEER_HALF = PEER_QDIM // 2
PEER_CHUNK = 128


def rms_norm(x, g):
    xf = x.astype(jnp.float32)
    y = xf * lax.rsqrt(jnp.mean(xf * xf, axis=-1, keepdims=True) + RMS_EPS)
    return (y * g.astype(jnp.float32)).astype(x.dtype)

def split_heads(a, n_heads):
    b, t, _ = a.shape
    return a.reshape(b, t, n_heads, HEAD_DIM).transpose(0, 2, 1, 3)

def merge_heads(a):
    b, h, t, d = a.shape
    return a.transpose(0, 2, 1, 3).reshape(b, t, h * d)

def alibi_slopes(n):
    return 2.0 ** (-8.0 * jnp.arange(1, n + 1, dtype=jnp.float32) / n)

def fox_attention(q, k, v, log_f):
    b, h, t, hd = q.shape
    c = jnp.cumsum(log_f, axis=-1)
    scale = 1.0 / math.sqrt(hd)
    kpos = jnp.arange(t)

    def block(i):
        t0 = i * Q_BLOCK
        qb = lax.dynamic_slice_in_dim(q, t0, Q_BLOCK, axis=2)
        cq = lax.dynamic_slice_in_dim(c, t0, Q_BLOCK, axis=2)
        s = jnp.einsum('bhqd,bhkd->bhqk', qb, k).astype(jnp.float32) * scale
        s = s + cq[..., :, None] - c[:, :, None, :]
        qpos = t0 + jnp.arange(Q_BLOCK)
        mask = kpos[None, :] <= qpos[:, None]
        s = jnp.where(mask, s, NEG_INF)
        p = jax.nn.softmax(s, axis=-1)
        return jnp.einsum('bhqk,bhkd->bhqd', p.astype(v.dtype), v)

    out = lax.map(block, jnp.arange(t // Q_BLOCK))
    return out.transpose(1, 2, 0, 3, 4).reshape(b, h, t, hd)

def dilated_window_branch(q, k, v, window, dilation, slopes):
    b, h, t, hd = q.shape
    n_steps = window // dilation
    sub_len = t // dilation
    nb = -(-sub_len // Q_BLOCK)
    pad = nb * Q_BLOCK - sub_len

    def to_sub(a):
        a = a.reshape(b, h, sub_len, dilation, hd).transpose(0, 1, 3, 2, 4)
        a = jnp.pad(a, ((0, 0), (0, 0), (0, 0), (0, pad), (0, 0)))
        return a.reshape(b, h, dilation, nb, Q_BLOCK, hd)

    qs, ks, vs = to_sub(q), to_sub(k), to_sub(v)

    def with_prev(a):
        prev = jnp.concatenate([jnp.zeros_like(a[:, :, :, :1]), a[:, :, :, :-1]], axis=3)
        return jnp.concatenate([prev, a], axis=4)

    kc, vc = with_prev(ks), with_prev(vs)
    s = jnp.einsum('bhrnqd,bhrnkd->bhrnqk', qs, kc).astype(jnp.float32) / math.sqrt(hd)

    qi = jnp.arange(Q_BLOCK)[:, None] + Q_BLOCK
    ki = jnp.arange(2 * Q_BLOCK)[None, :]
    steps = qi - ki
    band = (steps >= 0) & (steps <= n_steps)
    key_sub = jnp.arange(nb)[:, None, None] * Q_BLOCK - Q_BLOCK + ki[None]
    valid = band[None] & (key_sub >= 0)
    bias = -slopes[:, None, None, None, None] * (dilation * steps).astype(jnp.float32)[None, None, None]
    s = jnp.where(valid, s + bias, NEG_INF)
    lse = jax.nn.logsumexp(s, axis=-1)
    p = jnp.exp(s - lse[..., None])
    o = jnp.einsum('bhrnqk,bhrnkd->bhrnqd', p.astype(vc.dtype), vc)

    def from_sub(a, tail):
        a = a.reshape((b, h, dilation, nb * Q_BLOCK) + tail)[:, :, :, :sub_len]
        a = jnp.swapaxes(a, 2, 3)
        return a.reshape((b, h, t) + tail)

    return from_sub(o, (hd,)), from_sub(lse, ())

def dilated_attention(q, k, v):
    slopes = alibi_slopes(q.shape[1])
    outs, lses = [], []
    for window, dilation in DILATION_PATTERNS:
        o, l = dilated_window_branch(q, k, v, window, dilation, slopes)
        outs.append(o)
        lses.append(l)
    w = jax.nn.softmax(jnp.stack(lses, axis=0), axis=0)
    o = jnp.stack(outs, axis=0).astype(jnp.float32)
    return jnp.sum(w[..., None] * o, axis=0).astype(q.dtype)

def peer_ffn(xn, wq, subkeys, u_table, v_table):
    b, t, d = xn.shape
    xt = xn.reshape(-1, PEER_CHUNK, d)

    def chunk(xc):
        q = (xc @ wq).reshape(PEER_CHUNK, PEER_HEADS, 2, PEER_HALF)
        s = jnp.einsum('chpd,hpkd->chpk', q, subkeys).astype(jnp.float32)
        s1, i1 = lax.top_k(s[:, :, 0], PEER_TOPK)
        s2, i2 = lax.top_k(s[:, :, 1], PEER_TOPK)
        cand = (s1[..., :, None] + s2[..., None, :]).reshape(PEER_CHUNK, PEER_HEADS, PEER_TOPK * PEER_TOPK)
        cidx = (i1[..., :, None] * PEER_NKEYS + i2[..., None, :]).reshape(PEER_CHUNK, PEER_HEADS, PEER_TOPK * PEER_TOPK)
        cs, ci = lax.top_k(cand, PEER_TOPK)
        eidx = jnp.take_along_axis(cidx, ci, axis=-1)
        g = jax.nn.softmax(cs, axis=-1)
        ug = jnp.take(u_table, eidx, axis=0)
        vg = jnp.take(v_table, eidx, axis=0)
        hid = jnp.einsum('cd,chkd->chk', xc, ug).astype(jnp.float32)
        a = jax.nn.gelu(hid, approximate=False) * g
        return jnp.einsum('chk,chkd->cd', a.astype(vg.dtype), vg)

    out = lax.map(chunk, xt)
    return out.reshape(b, t, d)

def second_inputs(seed: int = 0) -> dict:
    key = jax.random.key(seed)
    ks = jax.random.split(key, 14)
    f32 = jnp.float32
    sd = D_MODEL ** -0.5
    x = jax.random.normal(ks[0], (BATCH, SEQ, D_MODEL), f32)
    norm1_g = 1.0 + 0.05 * jax.random.normal(ks[1], (DEPTH, D_MODEL), f32)
    w_in = jnp.concatenate([
        sd * jax.random.normal(ks[2], (DEPTH, D_MODEL, 3 * FOX_WIDTH), f32),
        0.1 * sd * jax.random.normal(ks[3], (DEPTH, D_MODEL, N_FOX_HEADS), f32),
        sd * jax.random.normal(ks[4], (DEPTH, D_MODEL, 3 * DIL_WIDTH), f32),
    ], axis=-1)
    b_forget = 3.0 + 0.1 * jax.random.normal(ks[5], (DEPTH, N_FOX_HEADS), f32)
    w_out = MIX_WIDTH ** -0.5 * jax.random.normal(ks[6], (DEPTH, MIX_WIDTH, D_MODEL), f32)
    norm2_g = 1.0 + 0.05 * jax.random.normal(ks[7], (DEPTH, D_MODEL), f32)
    peer_wq = sd * jax.random.normal(ks[8], (DEPTH, D_MODEL, PEER_HEADS * PEER_QDIM), f32)
    peer_subkeys = PEER_HALF ** -0.5 * jax.random.normal(ks[9], (DEPTH, PEER_HEADS, 2, PEER_NKEYS, PEER_HALF), f32)
    peer_u = sd * jax.random.normal(ks[10], (DEPTH, PEER_EXPERTS, D_MODEL), f32)
    peer_v = (PEER_HEADS ** -0.5) * jax.random.normal(ks[11], (DEPTH, PEER_EXPERTS, D_MODEL), f32)
    normf_g = 1.0 + 0.05 * jax.random.normal(ks[12], (D_MODEL,), f32)
    return {"x": x, "norm1_g": norm1_g, "w_in": w_in, "b_forget": b_forget, "w_out": w_out,
            "norm2_g": norm2_g, "peer_wq": peer_wq, "peer_subkeys": peer_subkeys,
            "peer_u": peer_u, "peer_v": peer_v, "normf_g": normf_g}

def second_block(x, norm1_g, w_in, b_forget, w_out, norm2_g, peer_wq, peer_subkeys, peer_u, peer_v, normf_g):
    h = x
    for layer in range(DEPTH):
        xn = rms_norm(h, norm1_g[layer])
        proj = xn @ w_in[layer]
        o0 = 3 * FOX_WIDTH
        o1 = o0 + N_FOX_HEADS
        fq = split_heads(proj[..., :FOX_WIDTH], N_FOX_HEADS)
        fk = split_heads(proj[..., FOX_WIDTH:2 * FOX_WIDTH], N_FOX_HEADS)
        fv = split_heads(proj[..., 2 * FOX_WIDTH:o0], N_FOX_HEADS)
        log_f = jax.nn.log_sigmoid(proj[..., o0:o1].astype(jnp.float32)
                                   + b_forget[layer].astype(jnp.float32)).transpose(0, 2, 1)
        dq = split_heads(proj[..., o1:o1 + DIL_WIDTH], N_DIL_HEADS)
        dk = split_heads(proj[..., o1 + DIL_WIDTH:o1 + 2 * DIL_WIDTH], N_DIL_HEADS)
        dv = split_heads(proj[..., o1 + 2 * DIL_WIDTH:o1 + 3 * DIL_WIDTH], N_DIL_HEADS)
        fox_out = fox_attention(fq, fk, fv, log_f)
        dil_out = dilated_attention(dq, dk, dv)
        mixed = jnp.concatenate([merge_heads(fox_out), merge_heads(dil_out)], axis=-1)
        h = h + mixed @ w_out[layer]
        xn2 = rms_norm(h, norm2_g[layer])
        h = h + peer_ffn(xn2, peer_wq[layer], peer_subkeys[layer], peer_u[layer], peer_v[layer])
    return rms_norm(h, normf_g)


def setup_inputs(seed=0):
    out = dict(first_inputs(seed))
    for name, value in second_inputs(seed + 1).items():
        if name != "x":
            out[name + "_2"] = value
    return out


def reference(
    x, mem, positions, norm_g, w_in, b_gate, q_norm_g, w_uq, kv_norm_g, w_ukv, q_head_g,
    k_head_g, conv_w, conv_b, mem_norm_g, w_mkv, mem_q_g, mem_k_g, w_br_attn, w_br_conv,
    w_br_mem, w_out, norm1_g_2, w_in_2, b_forget_2, w_out_2, norm2_g_2, peer_wq_2,
    peer_subkeys_2, peer_u_2, peer_v_2, normf_g_2,
):
    x = first_block(
        x, mem, positions, norm_g, w_in, b_gate, q_norm_g, w_uq, kv_norm_g, w_ukv, q_head_g,
        k_head_g, conv_w, conv_b, mem_norm_g, w_mkv, mem_q_g, mem_k_g, w_br_attn, w_br_conv,
        w_br_mem, w_out,
    )
    return second_block(
        x, norm1_g_2, w_in_2, b_forget_2, w_out_2, norm2_g_2, peer_wq_2, peer_subkeys_2,
        peer_u_2, peer_v_2, normf_g_2,
    )


_drawn_inputs = setup_inputs


def setup_inputs(seed=0):
    import zlib

    import numpy as np

    out = dict(_drawn_inputs(seed))
    spreads = {}
    factors = {'q_norm_g': 5.464,
     'kv_norm_g': 4.503,
     'q_head_g': 5.471,
     'k_head_g': 5.435,
     'mem_norm_g': 4.305,
     'mem_q_g': 5.167,
     'mem_k_g': 5.284,
     'conv_b': 3.089,
     'norm1_g_2': 4.041,
     'b_forget_2': 50.408,
     'norm2_g_2': 2.898}
    for name, (base, spread) in spreads.items():
        noise = np.random.default_rng([zlib.crc32(name.encode()), seed]).standard_normal(out[name].shape)
        drawn = base * np.exp(spread * noise) if base else spread * noise
        out[name] = __import__('jax').numpy.asarray(drawn.astype(out[name].dtype))
    for name, factor in factors.items():
        out[name] = (out[name] * factor).astype(out[name].dtype)
    return out
```

```python
from contextlib import ExitStack

import numpy as np

import concourse.bass as bass
from concourse import mybir

F32 = mybir.dt.float32
F32R = mybir.dt.float32r
BF16 = mybir.dt.bfloat16
U32 = mybir.dt.uint32
I32 = mybir.dt.int32
ALU = mybir.AluOpType
ACT = mybir.ActivationFunctionType
AX = mybir.AxisListType

P = 128
D = 1024
KD = D // P
T = 512
TB = T // P
MEM = 256
MB = MEM // P
HEADS = 8
QL, KVL = 3, 2
NOPE, ROPE = 64, 32
QKD = NOPE + ROPE
HALF = ROPE // 2
DH = 64
MEM_HEADS = 4
EPS = 1e-6
ATT2 = 16
TOPK = 16
NG = 64
PEER_HEADS = 8
NKEYS = 128
NEG = -1e30
BIG = 3.0e38

COLS = {}
_n = 0
for _name, _k in (("norm", 8), ("qn", 3), ("kvn", 2), ("qh", 1), ("kh", 1), ("cw", 12), ("cb", 4), ("memn", 8),
                  ("mq", 1), ("mk", 1), ("bg", 24), ("norm1", 8), ("norm2", 8), ("bf", 1), ("invf", 1), ("eps", 1)):
    COLS[_name] = _n
    _n += _k
NCOLS = _n

CN = {}
_n = 0
for _name, _k in (("ident", 128), ("negid", 128), ("ones", 128), ("rot", 128), ("iota", 128), ("iota16", 16),
                  ("msf", 128), ("mtf", 128), ("msd", 512), ("mtd", 512), ("cnt", 512)):
    CN[_name] = _n
    _n += _k
NCONST = _n
NKEEP = CN["msf"]

LOADS = []
PROJ = []
STEPS = []
TEMPS = {}
POST_OF = []


def build_schedule():
    if STEPS:
        return

    def load(kind, i, n):
        LOADS.append((kind, i, n))
        return len(LOADS) - 1

    def proj(kind, i, loads, temp=False):
        n = len(PROJ)
        PROJ.append((kind, i, loads))
        if temp:
            TEMPS[n] = len(TEMPS)
            POST_OF.append(None)
        STEPS.append(("proj", n))
        return n

    posts = [0]

    def post(kind, i, ns):
        posts[0] += 1
        for n in ns:
            POST_OF[TEMPS[n]] = posts[0]
        STEPS.append(("post", kind, i, ns, posts[0]))

    def tile(kind, i, k, m, temp=False):
        return proj(kind, i, [load(kind, i, k * m)], temp)

    def pre_q(h):
        tile("uq", h, QL, QKD)

    def pre_k(h):
        tile("uk", h, KVL, NOPE)

    conv_ns = []

    def conv_part(c):
        conv_ns.append(tile("conv", c, KD, P, True))
        if c % 4 == 3:
            post("conv", c // 4, conv_ns[-4:])

    STEPS.append(("norm", "x"))
    for i in range(QL + KVL):
        tile("lat", i, KD, P)
        if i == 0:
            STEPS.append(("cast",))
    tile("kpe", 0, KD, QKD)
    STEPS.append(("rope_tables",))
    conv_part(0)
    STEPS.append(("norm", "kvl"))
    conv_part(1)
    STEPS.append(("norm", "ql"))
    L = load("uv", 0, KVL * 512)
    for tb in range(TB):
        proj("uv", tb, [L])
    fill = list(range(2, 16))

    def filler(k=1):
        for _ in range(k):
            if fill:
                conv_part(fill.pop(0))

    def prep_mla(h):
        yield lambda: pre_q(h)
        yield lambda: (pre_k(h), STEPS.append(("norm", f"q{h}")))
        yield lambda: STEPS.append(("norm", f"k{h}"))
        yield lambda: STEPS.append(("rope", h, 0))
        yield lambda: STEPS.append(("rope", h, 1))

    for f in prep_mla(0):
        f()
        filler()
    for qb in range(TB):
        STEPS.append(("S", 0, qb))
    filler()
    STEPS.append(("M", 0))
    for h in range(HEADS):
        nxt = prep_mla(h + 1) if h + 1 < HEADS else iter(())

        def more():
            f = next(nxt, None)
            if f:
                f()
        more()
        STEPS.append(("T", h, 0))
        STEPS.append(("T", h, 1))
        more()
        STEPS.append(("PV", h, 0))
        STEPS.append(("T", h, 2))
        more()
        STEPS.append(("PV", h, 1))
        STEPS.append(("T", h, 3))
        more()
        STEPS.append(("PV", h, 2))
        more()
        STEPS.append(("PV", h, 3))
        STEPS.append(("O", h))
        if h + 1 < HEADS:
            filler()
            for qb in range(TB):
                STEPS.append(("S", h + 1, qb))
            filler()
            STEPS.append(("M", h + 1))
    while fill:
        filler()
    STEPS.append(("norm", "mem"))
    for h in range(MEM_HEADS):
        tile("qm", h, KD, P)
    for h in range(MEM_HEADS):
        tile("mk", h, KD, P)
        STEPS.append(("norm", f"mq{h}"))
    Ls = [load("mv", c, 1024) for c in range(4)]
    for tb in range(MB):
        proj("mv", tb, Ls)
    for h in range(MEM_HEADS):
        STEPS.append(("norm", f"mk{h}"))

    def gate(i):
        n = tile("gate", i, KD, P, i < 4)
        if i < 4:
            post("gate", i, [n])

    for h in range(MEM_HEADS):
        a = HEADS + h
        for qb in range(TB):
            STEPS.append(("S", a, qb))
        gate(2 * h)
        STEPS.append(("M", a))
        gate(2 * h + 1)
        for kb in range(MB):
            STEPS.append(("T", a, kb))
        for kb in range(MB):
            STEPS.append(("PV", a, kb))
        STEPS.append(("O", a))
    for i in range(4):
        post("mgate", i, [])
    for f in range(KD):
        for b in range(3):
            L1 = load("rb", 3 * f + b, 12 * P)
            n1 = proj("r", 3 * f + b, [L1], True)
            n2 = proj("br", 3 * f + b, [L1], True)
            post("rb", 3 * f + b, [n1, n2])
    for f in range(KD):
        post("res", f, [tile("wo", f, KD, P, True)])

    STEPS.append(("norm", "x2"))
    post("forget", 0, [tile("wf", 0, KD, 8, True)])
    for g in range(2):
        if g == 0:
            Ls = [load("v2", c, 1024) for c in range(4)]
            for tb in range(TB):
                proj("v2", tb, Ls)

    def qk2(p, s):
        tile("qk2", 2 * p + s, KD, P)

    qk2(0, 0)
    qk2(0, 1)
    for qb in range(TB):
        STEPS.append(("S", 12, qb))
    qk2(1, 0)
    STEPS.append(("M", 12))
    for j in range(ATT2):
        a = 12 + j
        STEPS.append(("T", a, 0))
        STEPS.append(("T", a, 1))
        STEPS.append(("PV", a, 0))
        STEPS.append(("T", a, 2))
        STEPS.append(("PV", a, 1))
        STEPS.append(("T", a, 3))
        STEPS.append(("PV", a, 2))
        STEPS.append(("PV", a, 3))
        STEPS.append(("O", a))
        if j + 1 < ATT2:
            if j % 2 == 0:
                for qb in range(TB):
                    STEPS.append(("S", a + 1, qb))
                if j // 2 + 1 < 8:
                    qk2(j // 2 + 1, 1)
                STEPS.append(("M", a + 1))
            else:
                for qb in range(TB):
                    STEPS.append(("S", a + 1, qb))
                if j == 5:
                    Ls = [load("v2", 4 + c, 1024) for c in range(4)]
                    for tb in range(TB):
                        proj("v2", TB + tb, Ls)
                if j // 2 + 2 < 8:
                    qk2(j // 2 + 2, 0)
                STEPS.append(("M", a + 1))
    for f in range(KD):
        post("res2", f, [tile("wo2", f, KD, P, True)])
    STEPS.append(("norm", "h2"))
    for i in range(2 * PEER_HEADS):
        tile("wq", i, KD, P)


def norm_shape(key):
    if key in ("x", "x2", "h2"):
        return KD, D, T
    if key == "mem":
        return KD, D, MEM
    if key == "ql":
        return QL, QL * P, T
    if key == "kvl":
        return KVL, KVL * P, T
    if key.startswith("mq"):
        return 1, P, T
    if key.startswith("mk"):
        return 1, P, MEM
    return 1, QKD, T


def program(nc, t_in, out):
    build_schedule()
    ctx = ExitStack()
    with ctx:
        def sem(name):
            return ctx.enter_context(nc.semaphore(name))

        SB = 52480
        LOW = 2 * KD * T + NKEEP + NCOLS + NCOLS % 2 + 960 + 3 * T

        def place(name, off, shape, dt):
            with nc.sbuf_tensor(name + "_before", [P, off], F32) if off else ExitStack():
                with nc.sbuf_tensor(name, [P] + shape, dt) as buffer:
                    return buffer

        low = place("low", 0, [LOW], F32)
        blocks = place("blocks", LOW, [SB - LOW], F32)
        dense = place("dense", LOW, [14352], F32)

        def region(off, n, k=None, of=None):
            at, base = (of, LOW) if of is not None else (low, 0) if off < LOW else (blocks, LOW)
            v = at[:, off - base:off - base + n]
            return v if k is None else v.rearrange("p (k n) -> p k n", k=k)

        xT = region(0, 4096, KD)
        hT = region(4096, 4096, KD)
        o = 8192
        const = region(o, NKEEP)
        o += NKEEP
        cols = region(o, NCOLS)
        o += NCOLS + NCOLS % 2
        msf = region(o, 64).bitcast(BF16)
        mtf = region(o + 64, 64).bitcast(BF16)
        msd = region(o + 128, 256).bitcast(BF16)
        mtd = region(o + 384, 256).bitcast(BF16)
        cnt = region(o + 640, 256).bitcast(BF16)
        idb = region(o + 896, 64).bitcast(BF16)
        o += 960
        lists = region(o, 3 * T, 3)
        o += 3 * T
        assert o == LOW
        NW = 5
        ring = region(o, NW * 1536, NW)
        o += NW * 1536
        NE = 6
        ebuf = region(o, NE * T, NE)
        o += NE * T
        sq = region(o, 2 * T, 2)
        o += 2 * T
        rs = region(o, 2 * T, 2)
        o += 2 * T
        dtmp = region(o, T)
        o += T
        PT = region(o, 4 * T, 4)
        o += 4 * T
        VA = region(o, 4096).rearrange("p (t h d) -> p t h d", t=TB, h=HEADS)
        vA_off = o
        o += 4096
        oT = region(o, 12 * T, 12)
        oT_off = o
        o += 12 * T
        R1 = o
        lat = region(o, 6 * T, 6)
        o += 6 * T
        qm1 = region(o, 2 * T, 2)
        o += 2 * T
        km1 = region(o, 2 * T, 2)
        o += 2 * T
        rtmp = region(o, T)
        cosT = region(o + T, T)
        sinT = region(o + 2 * T, T)
        o += 3 * T
        memT = region(o, KD * MEM, KD)
        o += KD * MEM
        mkT = region(o, 4 * MEM, 4)
        o += 4 * MEM
        mv = region(o, MB * T, MB)
        o += MB * T
        mq = region(o, 4 * T, 4)
        o += 4 * T
        mrow = region(o, T)
        o += T
        mx = region(o, 8)
        o += 8
        zsm = region(o, 3 * T, 3)
        o += 3 * T
        memgate = lat[:, 0:4, :]
        cwork = zsm
        zc = region(o, T + 2)
        o += T + 2
        assert o <= SB, o
        yT = region(R1, 4096, KD)
        Q2 = region(R1 + 4096, 4 * T, 4)
        K2 = region(R1 + 4096 + 4 * T, 4 * T, 4)
        VB = region(R1 + 8192, 4096).rearrange("p (t h d) -> p t h d", t=TB, h=HEADS)
        assert R1 + 12288 <= o - (T + 2) - 3 * T - 8 - T
        pq = region(R1, 16 * T, 16)
        sk = region(R1 + 8192, 2048, 16)
        sc = region(vA_off, 4096, 2)
        tk = oT_off
        cand = region(tk, 2048)
        eq = region(tk + 2048, 2048)
        tv = region(tk + 4096, 256, 16)
        ti = region(tk + 4352, 256, 16).bitcast(U32)
        tif = region(tk + 4608, 256)
        cs = region(tk + 4864, 128, 8)
        ci = region(tk + 4992, 128, 8).bitcast(U32)
        ca = region(tk + 5120, 128).bitcast(U32)
        cbf = region(tk + 5248, 256, 2)
        sel = region(tk + 5504, 384, 3)
        ee = region(tk + 5888, 128)
        es = region(tk + 6016, 16)
        stage = region(LOW, 2 * 16384).rearrange("p (s i t) -> p s i t", s=2, i=P)
        ohring = region(LOW + 32768, 2 * 2 * 4 * P).rearrange("p (s w u i) -> p s w u i", s=2, w=2, u=4)
        UR = region(LOW, 4 * 1024, 4, dense)
        VR = region(LOW + 4096, 4 * 1024, 4, dense)
        GR = region(LOW + 8192, 4 * T, 4, dense)
        AF = region(LOW + 10240, 4 * T, 4, dense)
        gf = region(LOW + 12288, D, None, dense)
        fsq = region(LOW + 13312, D, None, dense)
        fss = region(LOW + 14336, 16, None, dense)
        U2 = place("u_split", LOW + 14352, [2, 2, KD, P], F32R)
        V2 = place("v_split", LOW + 14352 + 4096, [4, 2, D], F32R)
        A2 = place("a_split", LOW + 14352 + 12288, [4, 2, T], F32R)
        hh = place("h_high", LOW + 32768 + 2048, [KD, T], F32R)
        hl = place("h_low", 4096, [KD, T], F32R)
        craw = region(oT_off, NCONST - NKEEP)
        pos_i = ebuf[:, 0, :].bitcast(I32)

        ident = const[:, CN["ident"]:CN["ident"] + P]
        negid = const[:, CN["negid"]:CN["negid"] + P]
        ones = const[:, CN["ones"]:CN["ones"] + P]
        rot = const[:, CN["rot"]:CN["rot"] + P]
        iota = const[:, CN["iota"]:CN["iota"] + P]
        iota16 = const[:, CN["iota16"]:CN["iota16"] + 16]

        def col(name, i=0, p0=0, p1=P):
            return cols[p0:p1, COLS[name] + i:COLS[name] + i + 1]

        bank = [ctx.enter_context(nc.psum_tensor(f"bank{i}", [P, T], F32)) for i in range(8)]
        pj = [bank[0], bank[1]]
        ax = [bank[2], bank[7]]
        scb = [bank[3], bank[4], bank[5]]
        ob = bank[6]

        gates = nc.dram_tensor("gates", (NKEYS, P, T), F32, kind="Internal").ap()

        s_x = sem("x_loaded")
        s_par = sem("params_loaded")
        s_const = sem("constants_loaded")
        s_raw = sem("masks_loaded")
        s_mem = sem("mem_loaded")
        s_pos = sem("positions_loaded")
        s_cast = sem("masks_cast")
        s_init = sem("buffers_set")
        s_init2 = sem("second_block_buffers_set")
        s_w = [sem(f"weights_in_slot{i}") for i in range(NW)]
        s_proj = sem("projections_done")
        s_evac = sem("projections_evacuated")
        s_post = sem("post_steps_done")
        s_sq = sem("squares_ready")
        s_squsd = sem("squares_used")
        s_aux = sem("aux_bank_written")
        s_auxfree = [sem("aux_bank0_read"), sem("aux_bank1_read")]
        s_rs = sem("reciprocal_roots_done")
        s_norm = sem("norm_steps_done")
        s_tab = sem("rope_tables_done")
        s_rope = sem("rope_steps_done")
        s_S = sem("score_rows_done")
        s_max = sem("row_maxima_done")
        s_T = sem("score_columns_done")
        s_P = sem("exponentials_done")
        s_Pc = sem("exponentials_counted")
        s_PV = sem("value_products_done")
        s_O = sem("head_outputs_done")
        s_kb = [sem(f"key_bias_in_buffer{i}") for i in range(4)]
        s_fmag = sem("forget_magnitudes_ready")
        s_fch = sem("forget_logs_done")
        s_d = sem("vector_chain")
        s_rc = sem("scalar_chain")
        s_sk = sem("subkeys_loaded")
        s_cos = sem("angles_ready")
        s_qs = sem("key_scores_done")
        s_qe = sem("key_scores_copied")
        s_tk = sem("topk_blocks_done")
        s_sm = sem("rank_differences_ready")
        s_ex = sem("rank_exponentials_done")
        s_lt = sem("lists_transposed")
        s_ltc = sem("lists_copied")
        s_hx = sem("residual_transposed")
        s_hxc = sem("residual_copied")
        s_oh = sem("onehots_ready")
        s_gm = [sem(f"gate_groups_done_bank{i}") for i in range(2)]
        s_ge = [sem(f"gate_groups_copied_bank{i}") for i in range(2)]
        s_gst = [sem(f"gates_stored_stage{i}") for i in range(2)]
        s_u = [sem(f"u_tiles_{i}") for i in range(2)]
        s_v = [sem(f"v_tiles_{i}") for i in range(2)]
        s_g = [sem(f"g_tiles_{i}") for i in range(2)]
        s_hid = sem("hidden_done")
        s_gelu = sem("gelu_done")
        s_act = sem("gated_done")
        s_ahi = sem("gated_high_parts")
        s_alo = sem("gated_low_parts")
        s_uhi = sem("u_high_parts")
        s_ulo = sem("u_low_parts")
        s_vhi = sem("v_high_parts")
        s_vlo = sem("v_low_parts")
        s_hh = sem("h_high_parts")
        s_hl = sem("h_low_parts")
        s_eo = sem("expert_outputs_done")
        s_ea = sem("expert_outputs_added")
        s_gf = sem("final_gain_loaded")
        s_fin = sem("final_rows_ready")
        s_fsq = sem("final_squares_done")
        s_out = sem("output_stored")

        NORMS = [s[1] for s in STEPS if s[0] == "norm"]
        norm_no = {k: i + 1 for i, k in enumerate(NORMS)}
        sq0, n = {}, 0
        for k in NORMS:
            sq0[k] = n
            n += norm_shape(k)[0]
        pi = {(k, i): n for n, (k, i, _) in enumerate(PROJ)}
        auxi, n = {}, 0
        for s in STEPS:
            if s[0] == "norm":
                auxi[("norm", s[1])] = n
                n += 1
            elif s[0] == "rope":
                auxi[("rope",) + s[1:]] = n
                n += 1
            elif s[0] == "M":
                auxi[("M", s[1])] = n
                n += 1
            elif s[0] == "PV" and HEADS <= s[1] < 12 and s[2] == 0:
                auxi[("den", s[1])] = n
                n += 1
        tiles = [s for s in STEPS if s[0] in ("S", "T")]
        tile_no = {s: i for i, s in enumerate(tiles)}
        s_no = {s: i + 1 for i, s in enumerate(x for x in tiles if x[0] == "S")}
        t_no = {s: i + 1 for i, s in enumerate(x for x in tiles if x[0] == "T")}
        pv_no = {s[1:]: i + 1 for i, s in enumerate(x for x in STEPS if x[0] == "PV")}
        cnt_no = {s[1:]: i + 1 for i, s in enumerate(x for x in STEPS if x[0] == "T" and x[1] >= 20)}
        rope_no = {s[1:]: i + 1 for i, s in enumerate(x for x in STEPS if x[0] == "rope")}
        M_no = {s[1]: i + 1 for i, s in enumerate(x for x in STEPS if x[0] == "M")}
        O_no = {s[1]: i + 1 for i, s in enumerate(x for x in STEPS if x[0] == "O")}
        post_no = {s[1:3]: s[4] for s in STEPS if s[0] == "post"}
        last_use = {}
        for n, (_, _, loads) in enumerate(PROJ):
            for L in loads:
                last_use[L] = n

        def n_keys(a):
            return MB if HEADS <= a < 12 else TB

        def q0(a, kb):
            return kb * P if a >= 12 else 0

        def at_least(eng, sem, value):
            if not isinstance(value, int) or value > 0:
                eng.wait_ge(sem, value)

        block = ctx.enter_context(nc.Block())

        @block.sync
        def _(sp):
            sp.dma_start(xT, t_in["xT"]).then_inc(s_x, 16)
            sp.dma_start(cols, t_in["cols"]).then_inc(s_par, 16)
            sp.dma_start(const, t_in["const"][:, 0:NKEEP]).then_inc(s_const, 16)

            def weights(L):
                kind, i, n = LOADS[L]
                if L >= NW:
                    sp.wait_ge(s_proj, last_use[L - NW] + 1)
                sp.dma_start(ring[:, L % NW, 0:n], t_in[kind][i]).then_inc(s_w[L % NW], 16)

            for L in range(len(LOADS)):
                weights(L)
                if L == NW - 1:
                    sp.dma_start(craw, t_in["const"][:, NKEEP:NCONST]).then_inc(s_raw, 16)
                    sp.dma_start(pos_i[NOPE:QKD, :], t_in["pos"].to_broadcast([ROPE, T])).then_inc(s_pos, 16)
                    sp.dma_start(memT, t_in["memT"]).then_inc(s_mem, 16)
            sp.wait_ge(s_O, len(O_no))
            sp.dma_start(sk, t_in["sk"]).then_inc(s_sk, 16)
            for tb in range(TB):
                sp.wait_ge(s_ge[0], 16 * (tb + 1))
                sp.wait_ge(s_ge[1], 16 * (tb + 1))
                for c in range(4):
                    sp.dma_start(gates[32 * c:32 * c + 32, :, tb * P:(tb + 1) * P].rearrange("i j t -> j i t"),
                                 stage[:, tb % 2, 32 * c:32 * c + 32, :]).then_inc(s_gst[tb % 2], 16)
            for i in range(2):
                sp.wait_ge(s_gst[i], 16 * 4 * TB // 2)

            def expert_loads(g, half):
                sl = slice(2 * half, 2 * half + 2)
                at_least(sp, s_ulo, g * 2 - 2)
                sp.dma_start(UR[:, sl], t_in["uT"][bass.ts(g, 2)].rearrange("s p n -> p s n")).then_inc(s_u[half], 16)
                at_least(sp, s_vlo, g * 2 - 2)
                sp.dma_start(VR[:, sl], t_in["v"][bass.ts(g, 2)].rearrange("s p n -> p s n")).then_inc(s_v[half], 16)
                at_least(sp, s_act, g * 2 - 2)
                sp.dma_start(GR[:, sl], gates[bass.ts(g, 2)].rearrange("s p n -> p s n")).then_inc(s_g[half], 16)

            expert_loads(0, 0)
            expert_loads(1, 1)
            sp.dma_start(gf, t_in["gf"].to_broadcast([P, D])).then_inc(s_gf, 16)
            with sp.Fori(1, NG // 2) as it:
                for half in range(2):
                    expert_loads(it * 2 + half, half)
            for tb in range(TB):
                sp.wait_ge(s_fin, tb + 1)
                sp.dma_start(out[tb * P:(tb + 1) * P, :], xT[:, 2 * tb:2 * tb + 2, :]
                             .rearrange("p k n -> p (k n)")).then_inc(s_out, 16)
            sp.wait_ge(s_out, 16 * TB)

        @block.gpsimd
        def _(pool):
            nc.gpsimd.memset(VA, 1.0).then_inc(s_init, 1)
            pool.wait_ge(s_init, 1)
            nc.gpsimd.memset(km1[QKD:P, :, :], 1.0).then_inc(s_init, 1)
            pool.wait_ge(s_init, 2)
            nc.gpsimd.memset(zc[:, 0:T + 2], 0.0).then_inc(s_init, 1)
            pool.wait_ge(s_O, 12)
            nc.gpsimd.memset(Q2[NOPE:QKD, :, :], 0.0).then_inc(s_init2, 1)
            pool.wait_ge(s_init2, 1)
            nc.gpsimd.memset(K2[NOPE:QKD, :, :], 0.0).then_inc(s_init2, 1)
            pool.wait_ge(s_init2, 2)
            nc.gpsimd.memset(K2[QKD:P, :, :], 1.0).then_inc(s_init2, 1)
            pool.wait_ge(s_init2, 3)
            nc.gpsimd.memset(VB, 1.0).then_inc(s_init2, 1)
            pool.wait_ge(s_init2, 4)
            nc.gpsimd.memset(Q2[NOPE:NOPE + 1, :, :], 1.0).then_inc(s_init2, 1)
            for j in range(ATT2):
                a = 12 + j
                if j == 0:
                    pool.wait_ge(s_post, post_no[("forget", 0)])
                if j >= 4:
                    pool.wait_ge(s_T, t_no[("T", a - 4, TB - 1)])
                src = zsm[j:j + 1, 2, :] if j < 8 else t_in["bias"][j - 8:j - 7, :]
                pool.dma_start(K2[NOPE:NOPE + 1, j % 4, :], src).then_inc(s_kb[j % 4], 16)
            pool.wait_ge(s_kb[3], 16 * 4)

            def low_u(e, slot):
                pool.wait_ge(s_uhi, e + 1)
                nc.gpsimd.tensor_tensor(U2[:, slot % 2, 1].rearrange("p k e -> p (k e)"), UR[:, slot, :],
                                        U2[:, slot % 2, 0].rearrange("p k e -> p (k e)").bitcast(F32),
                                        ALU.subtract).then_inc(s_ulo, 1)

            def low_v(e, slot):
                pool.wait_ge(s_vhi, e + 1)
                nc.gpsimd.tensor_tensor(V2[:, slot, 1], VR[:, slot, :], V2[:, slot, 0].bitcast(F32),
                                        ALU.subtract).then_inc(s_vlo, 1)

            def low_parts(e, last):
                for u in range(4):
                    if not last or u < 2:
                        low_u(e + (u + 2), (u + 2) % 4)
                    low_v(e + u, u)

            low_u(0, 0)
            low_u(1, 1)
            with pool.Fori(0, NG // 2 - 1) as it:
                low_parts(it * 4, False)
            low_parts(2 * NG - 4, True)

        @block.tensor
        def _(pe):
            mm = nc.tensor.matmul

            def need_aux(i):
                if i >= 2:
                    pe.wait_ge(s_auxfree[i % 2], i // 2)

            def proj(n):
                kind, i, loads = PROJ[n]
                if n >= 2:
                    pe.wait_ge(s_evac, n - 1)
                for L in loads:
                    pe.wait_ge(s_w[L % NW], 16 * (L // NW + 1))
                ps = pj[n % 2]
                w = ring[:, loads[0] % NW, :]

                def run(nk, m, rhs, N=T, base=0):
                    for k in range(nk):
                        last = mm(ps[0:m, 0:N], w[:, base + k * m:base + (k + 1) * m], rhs(k),
                                  start=(k == 0), stop=(k == nk - 1))
                    return last

                def tok(lhs, nk, chunk):
                    for k in range(nk):
                        L = loads[k // chunk]
                        last = mm(ps[:, :], lhs(k), ring[:, L % NW, (k % chunk) * T:(k % chunk + 1) * T],
                                  start=(k == 0), stop=(k == nk - 1))
                    return last

                if kind in ("lat", "conv", "gate", "qm", "r"):
                    pe.wait_ge(s_norm, norm_no["x"])
                    last = run(KD, P, lambda k: hT[:, k, :])
                elif kind == "kpe":
                    last = run(KD, QKD, lambda k: hT[:, k, :])
                elif kind == "uq":
                    pe.wait_ge(s_norm, norm_no["ql"])
                    last = run(QL, QKD, lambda k: lat[:, k, :])
                elif kind == "uk":
                    pe.wait_ge(s_norm, norm_no["kvl"])
                    last = run(KVL, NOPE, lambda k: lat[:, QL + k, :])
                elif kind == "uv":
                    pe.wait_ge(s_norm, norm_no["kvl"])
                    last = tok(lambda k: lat[:, QL + k, i * P:(i + 1) * P], KVL, KVL)
                elif kind == "mk":
                    pe.wait_ge(s_norm, norm_no["mem"])
                    last = run(KD, P, lambda k: memT[:, k, :], N=MEM)
                elif kind == "mv":
                    pe.wait_ge(s_norm, norm_no["mem"])
                    last = tok(lambda k: memT[:, k, i * P:(i + 1) * P], KD, 2)
                elif kind == "br":
                    b = i % 3
                    pe.wait_ge(s_post, post_no[("mgate", 3)])
                    last = run(4, P, lambda k: oT[:, 4 * b + k, :], base=KD * P)
                elif kind == "wo":
                    pe.wait_ge(s_post, post_no[("rb", 3 * KD - 1)])
                    last = run(KD, P, lambda k: yT[:, k, :])
                elif kind in ("qk2", "wf"):
                    pe.wait_ge(s_norm, norm_no["x2"])
                    last = run(KD, P if kind == "qk2" else 8, lambda k: hT[:, k, :])
                elif kind == "v2":
                    pe.wait_ge(s_norm, norm_no["x2"])
                    tb = i % TB
                    last = tok(lambda k: hT[:, k, tb * P:(tb + 1) * P], KD, 2)
                elif kind == "wo2":
                    pe.wait_ge(s_O, len(O_no))
                    last = run(KD, P, lambda k: oT[:, k, :])
                else:
                    assert kind == "wq"
                    pe.wait_ge(s_norm, norm_no["h2"])
                    last = run(KD, P, lambda k: hT[:, k, :])
                last.then_inc(s_proj, 1)

            def norm(key):
                nk, width, N = norm_shape(key)
                i = auxi[("norm", key)]
                need_aux(i)
                rows = min(width, P)
                for k in range(nk):
                    j = sq0[key] + k
                    pe.wait_ge(s_sq, j + 1)
                    last = mm(ax[i % 2][0:rows, 0:N], ones[0:rows, 0:rows], sq[0:rows, j % 2, 0:N],
                              start=(k == 0), stop=(k == nk - 1))
                    if k < nk - 1:
                        last.then_inc(s_squsd, 1)
                last.then_inc(s_aux, 1)

            def rope(h, which):
                i = auxi[("rope", h, which)]
                need_aux(i)
                pe.wait_ge(s_norm, norm_no[f"{'qk'[which]}{h}"])
                src = (qm1, km1)[which]
                mm(ax[i % 2][0:QKD, :], rot[0:QKD, 0:QKD], src[0:QKD, h % 2, :], start=True, stop=True)\
                    .then_inc(s_aux, 1)

            def operands(a):
                if a < HEADS:
                    return qm1[:, a % 2, :], km1[:, a % 2, :], QKD, QKD + 1
                if a < 12:
                    return mq[:, a - HEADS, :], mkT[:, a - HEADS, :], P, P
                return Q2[:, (a - 12) % 4, :], K2[:, (a - 12) % 4, :], NOPE + 1, QKD + 1

            def score_bank(step):
                n = tile_no[step]
                if n >= 3:
                    was = tiles[n - 3]
                    if was[0] == "S":
                        pe.wait_ge(s_max, s_no[was])
                    else:
                        pe.wait_ge(s_P, t_no[was])
                return scb[n % 3]

            def S(a, qb):
                q, k, K, _ = operands(a)
                if qb == 0:
                    if a < HEADS:
                        pe.wait_ge(s_rope, rope_no[(a, 1)])
                    elif a < 12:
                        pe.wait_ge(s_norm, norm_no[f"mk{a - HEADS}"])
                    else:
                        p = (a - 12) // 2
                        pe.wait_ge(s_cast, 6)
                        pe.wait_ge(s_init2, 5)
                        pe.wait_ge(s_evac, pi[("qk2", 2 * p + 1)] + 1)
                        pe.wait_ge(s_kb[(a - 12) % 4], 16 * ((a - 12) // 4 + 1))
                ps = score_bank(("S", a, qb))
                N = (qb + 1) * P if a >= 12 else n_keys(a) * P
                last = mm(ps[:, 0:N], q[0:K, qb * P:(qb + 1) * P], k[0:K, 0:N], start=True, stop=(a < 12))
                if 12 <= a < 20:
                    last = mm(ps[:, qb * P:N], idb, msf, start=False, stop=True)
                elif a >= 20:
                    last = mm(ps[:, 0:N], idb, msd[:, T - N:T], start=False, stop=True)
                last.then_inc(s_S, 1)

            def M(a):
                i = auxi[("M", a)]
                need_aux(i)
                pe.wait_ge(s_max, s_no[("S", a, TB - 1)])
                for qb in range(TB):
                    last = mm(ax[i % 2][0:1, qb * P:(qb + 1) * P], mx[:, 4 * (a % 2) + qb:4 * (a % 2) + qb + 1],
                              negid, start=True, stop=True)
                last.then_inc(s_aux, 1)

            def T_(a, kb):
                q, k, _, K = operands(a)
                if kb == 0:
                    i = auxi[("M", a)]
                    pe.wait_ge(s_auxfree[i % 2], i // 2 + 1)
                ps = score_bank(("T", a, kb))
                c0 = q0(a, kb)
                kk = k[0:K, kb * P:(kb + 1) * P]
                last = mm(ps[:, c0:T], kk, q[0:K, c0:T], start=True, stop=(a < HEADS))
                if HEADS <= a < 12:
                    last = mm(ps[:, :], ones[0:1, :], mrow[0:1, :], start=False, stop=True)
                elif 12 <= a < 20:
                    last = mm(ps[:, c0:c0 + P], idb, mtf, start=False, stop=True)
                elif a >= 20:
                    last = mm(ps[:, c0:T], idb, mtd[:, 0:T - c0], start=False, stop=True)
                last.then_inc(s_T, 1)

            def PV(a, kb):
                if a >= 20:
                    pe.wait_ge(s_Pc, cnt_no[(a, kb)])
                else:
                    pe.wait_ge(s_P, t_no[("T", a, kb)])
                if kb == 0 and a > 0:
                    pe.wait_ge(s_O, O_no[a] - 1)
                c0 = q0(a, kb)
                rhs = PT[:, kb, c0:T]
                nk = n_keys(a)
                if a < HEADS:
                    v = VA[:, kb, a, :]
                elif a < 12:
                    v = mv[:, kb, (a - HEADS) * P:(a - HEADS + 1) * P]
                else:
                    v = (VA if a < 20 else VB)[:, kb, (a - 12) % 8, :]
                if kb == 0 and a in (0, HEADS, 12, 20):
                    last_v = {0: ("uv", TB - 1), HEADS: ("mv", MB - 1), 12: ("v2", TB - 1), 20: ("v2", 2 * TB - 1)}[a]
                    pe.wait_ge(s_evac, pi[last_v] + 1)
                if HEADS <= a < 12:
                    i = auxi[("den", a)]
                    if kb == 0:
                        need_aux(i)
                    den = mm(ax[i % 2][:, :], ones, rhs, start=(kb == 0), stop=(kb == nk - 1))
                    if kb == nk - 1:
                        den.then_inc(s_aux, 1)
                mm(ob[:, c0:T], v, rhs, start=(kb == 0), stop=(kb == nk - 1)).then_inc(s_PV, 1)

            pe.wait_ge(s_const, 16)
            for s in STEPS:
                if s[0] == "proj":
                    proj(s[1])
                elif s[0] == "norm":
                    norm(s[1])
                elif s[0] == "rope":
                    rope(s[1], s[2])
                elif s[0] == "S":
                    S(s[1], s[2])
                elif s[0] == "M":
                    M(s[1])
                elif s[0] == "T":
                    T_(s[1], s[2])
                elif s[0] == "PV":
                    PV(s[1], s[2])

            pe.wait_ge(s_sk, 16)
            pe.wait_ge(s_evac, len(PROJ))
            def key_scores(tb):
                for c in range(4):
                    n = 4 * tb + c
                    if n >= 4:
                        pe.wait_ge(s_qe, n - 3)
                    for u in range(4):
                        hp = 4 * c + u
                        last = mm(bank[2 + n % 4][:, u * P:(u + 1) * P], pq[:, hp, tb * P:(tb + 1) * P], sk[:, hp, :],
                                  start=True, stop=True)
                    last.then_inc(s_qs, 1)

            def lists_out(tb):
                pe.wait_ge(s_tk, tb + 1)
                if tb >= 2:
                    pe.wait_ge(s_ltc, tb - 1)
                for w in range(3):
                    last = nc.tensor.transpose(bank[tb % 2][:, w * P:(w + 1) * P], sel[:, w, :], ident)
                last.then_inc(s_lt, 1)

            key_scores(0)
            key_scores(1)
            for tb in range(TB):
                lists_out(tb)
                if tb + 2 < TB:
                    key_scores(tb + 2)
            pe.wait_ge(s_ltc, TB)
            pe.wait_ge(s_qe, 4 * TB)
            for tb in range(TB):
                for dh in range(2):
                    for k in range(4):
                        last = nc.tensor.transpose(bank[2 * tb + dh][:, k * P:(k + 1) * P],
                                                   xT[:, 4 * dh + k, tb * P:(tb + 1) * P], ident)
            last.then_inc(s_hx, 1)
            pe.wait_ge(s_hxc, 8)
            def gate_groups(it, first):
                for u in range(2):
                    pe.wait_ge(s_oh, it * 2 + (u + 1))
                    if not first:
                        pe.wait_ge(s_ge[u], it)
                    for k in range(4):
                        last = mm(bank[u][:, k * P:(k + 1) * P], ohring[:, u, 1, k, :], ohring[:, u, 0, k, :],
                                  start=True, stop=True)
                    last.then_inc(s_gm[u], 1)

            gate_groups(0, True)
            with pe.Fori(1, T // 8) as it:
                gate_groups(it, False)

            def hidden(e, slot):
                pe.wait_ge(s_ulo, e + 1)
                at_least(pe, s_gelu, e - 1)
                for k in range(KD):
                    for w, x in ((0, hh), (0, hl), (1, hh)):
                        last = mm(bank[slot % 2][:, :], U2[:, slot % 2, w, k, :], x[:, k, :],
                                  start=(k == 0 and x is hh and w == 0), stop=(k == KD - 1 and w == 1))
                last.then_inc(s_hid, 1)

            def outputs(g, half):
                pe.wait_ge(s_vlo, g * 2 + 2)
                pe.wait_ge(s_alo, g * 2 + 2)
                for u in range(8):
                    tb, dh = u // 2, u % 2
                    at_least(pe, s_ea, g * 8 + (u - 3))
                    for e in (2 * half, 2 * half + 1):
                        for wa, wv in ((0, 0), (0, 1), (1, 0)):
                            last = mm(bank[2 + u % 4][:, :], A2[:, e, wa, tb * P:(tb + 1) * P],
                                      V2[:, e, wv, dh * T:(dh + 1) * T],
                                      start=(e == 2 * half and wa == wv), stop=(e > 2 * half and wa == 1))
                    last.then_inc(s_eo, 1)

            for u in range(2):
                pe.wait_ge(s_ge[u], T // 8)
            pe.wait_ge(s_hl, KD)
            for slot in range(4):
                hidden(slot, slot)
                if slot % 2 == 1 and slot > 1:
                    outputs(0, 0)
            with pe.Fori(1, NG // 2) as it:
                hidden(it * 4, 0)
                hidden(it * 4 + 1, 1)
                outputs(it * 2 - 1, 1)
                hidden(it * 4 + 2, 2)
                hidden(it * 4 + 3, 3)
                outputs(it * 2, 0)
            outputs(NG - 1, 1)

        @block.scalar
        def _(act):
            A = nc.scalar.activation
            chain = [0]

            def link(ins):
                chain[0] += 1
                ins.then_inc(s_rc, 1)
                act.wait_ge(s_rc, chain[0])

            def cast():
              act.wait_ge(s_raw, 16)
              act.wait_ge(s_const, 16)
              for dst, name, n in ((msf, "msf", 128), (mtf, "mtf", 128), (msd, "msd", 512), (mtd, "mtd", 512),
                                 (cnt, "cnt", 512)):
                c = CN[name] - NKEEP
                nc.scalar.copy(dst, craw[:, c:c + n]).then_inc(s_cast, 1)
              nc.scalar.copy(idb, ident).then_inc(s_cast, 1)

            def evac(n):
                kind, i, _ = PROJ[n]
                act.wait_ge(s_proj, n + 1)
                ps = pj[n % 2]
                if n in TEMPS:
                    j = TEMPS[n]
                    dst = ebuf[:, j % NE, :]
                    if j >= NE:
                        act.wait_ge(s_post, POST_OF[j - NE])
                    if kind == "conv" and i == 0:
                        act.wait_ge(s_tab, 1)
                    if kind == "r" and i == 0:
                        act.wait_ge(s_par, 16)
                    if kind == "gate" or (kind == "conv" and i % 4 == 3):
                        A(dst, ps[:, :], ACT.Silu).then_inc(s_evac, 1)
                    elif kind == "r":
                        A(dst, ps[:, :], ACT.Sigmoid, bias=col("bg", i)).then_inc(s_evac, 1)
                    elif kind == "wf":
                        A(dst[0:8, :], ps[0:8, :], ACT.Identity, bias=col("bf", 0, 0, 8)).then_inc(s_evac, 1)
                    else:
                        nc.scalar.copy(dst, ps[:, :]).then_inc(s_evac, 1)
                elif kind == "lat":
                    nc.scalar.copy(lat[:, i, :], ps[:, :]).then_inc(s_evac, 1)
                elif kind == "kpe":
                    nc.scalar.copy(lat[NOPE:QKD, 5, :], ps[NOPE:QKD, :]).then_inc(s_evac, 1)
                elif kind == "uq":
                    nc.scalar.copy(qm1[0:QKD, i % 2, :], ps[0:QKD, :]).then_inc(s_evac, 1)
                elif kind == "uk":
                    if i == 0:
                        act.wait_ge(s_evac, pi[("kpe", 0)] + 1)
                    nc.scalar.copy(km1[NOPE:QKD, i % 2, :], lat[NOPE:QKD, 5, :])
                    nc.scalar.copy(km1[0:NOPE, i % 2, :], ps[0:NOPE, :]).then_inc(s_evac, 1)
                elif kind in ("uv", "v2"):
                    if kind == "uv":
                        act.wait_ge(s_init, 1)
                    if kind == "v2" and i >= TB:
                        act.wait_ge(s_init2, 5)
                    V = VB if i >= TB else VA
                    src = ps[:, :].rearrange("p (h d) -> p h d", h=HEADS)
                    nc.scalar.copy(V[:, i % TB, 0:HEADS:2, 0:DH], src[:, 0:HEADS:2, :])
                    nc.scalar.copy(V[:, i % TB, 1:HEADS:2, DH:P], src[:, 1:HEADS:2, :]).then_inc(s_evac, 1)
                elif kind == "gate":
                    A(memgate[:, i - 4, :], ps[:, :], ACT.Silu).then_inc(s_evac, 1)
                elif kind == "qm":
                    nc.scalar.copy(mq[:, i, :], ps[:, :]).then_inc(s_evac, 1)
                elif kind == "mk":
                    nc.scalar.copy(mkT[:, i, :], ps[:, 0:MEM]).then_inc(s_evac, 1)
                elif kind == "mv":
                    nc.scalar.copy(mv[:, i, :], ps[:, :]).then_inc(s_evac, 1)
                elif kind == "qk2":
                    p, s = i // 2, i % 2
                    if i == 0:
                        act.wait_ge(s_init2, 5)
                    dst = (Q2, K2)[s]
                    scale = (DH ** -0.5, 1.0)[s]
                    for u in range(2):
                        ins = A(dst[0:DH, (2 * p + u) % 4, :], ps[u * DH:(u + 1) * DH, :], ACT.Copy, scale=scale)
                    ins.then_inc(s_evac, 1)
                else:
                    assert kind == "wq"
                    nc.scalar.copy(pq[:, i, :], ps[:, :]).then_inc(s_evac, 1)

            def square_summed(j):
                key = max((k for k in sq0 if sq0[k] <= j), key=lambda k: sq0[k])
                if j == sq0[key] + norm_shape(key)[0] - 1:
                    act.wait_ge(s_aux, auxi[("norm", key)] + 1)
                else:
                    act.wait_ge(s_squsd, j + 1 - sum(1 for k in sq0 if sq0[k] + norm_shape(k)[0] - 1 <= j))

            def norm(key):
                nk, width, N = norm_shape(key)
                rows = min(width, P)
                for k in range(nk):
                    j = sq0[key] + k
                    if key == "x":
                        act.wait_ge(s_x, 16)
                        src = xT[:, k, :]
                    elif key == "x2":
                        act.wait_ge(s_post, post_no[("res", k)])
                        src = xT[:, k, :]
                    elif key == "h2":
                        act.wait_ge(s_post, post_no[("res2", k)])
                        src = xT[:, k, :]
                    elif key == "ql":
                        act.wait_ge(s_evac, pi[("lat", k)] + 1)
                        src = lat[:, k, :]
                    elif key == "kvl":
                        act.wait_ge(s_evac, pi[("lat", QL + k)] + 1)
                        src = lat[:, QL + k, :]
                    elif key == "mem":
                        act.wait_ge(s_mem, 16)
                        src = memT[:, k, :]
                    elif key.startswith("mq"):
                        act.wait_ge(s_evac, pi[("qm", int(key[2:]))] + 1)
                        src = mq[:, int(key[2:]), :]
                    elif key.startswith("mk"):
                        act.wait_ge(s_evac, pi[("mk", int(key[2:]))] + 1)
                        src = mkT[:, int(key[2:]), :]
                    else:
                        h = int(key[1:])
                        act.wait_ge(s_evac, pi[("u" + key[0], h)] + 1)
                        src = (qm1 if key[0] == "q" else km1)[0:QKD, h % 2, :]
                    if j >= 2:
                        square_summed(j - 2)
                    A(sq[0:rows, j % 2, 0:N], src, ACT.Square, scale=width ** -0.5).then_inc(s_sq, 1)
                i, j = auxi[("norm", key)], norm_no[key]
                act.wait_ge(s_aux, i + 1)
                if j > 2:
                    act.wait_ge(s_norm, j - 2)
                r = rs[0:rows, j % 2, 0:N]
                if key == "x":
                    act.wait_ge(s_par, 16)
                A(r, ax[i % 2][0:rows, 0:N], ACT.Ln, bias=col("eps", 0, 0, rows)).then_inc(s_auxfree[i % 2], 1)
                act.wait_ge(s_auxfree[i % 2], i // 2 + 1)
                A(r, r, ACT.Exp, scale=-0.5).then_inc(s_rs, 1)

            def rope_tables():
                act.wait_ge(s_cos, 1)
                A(sinT[NOPE:QKD, :], rtmp[NOPE:QKD, :], ACT.Sin).then_inc(s_tab, 1)
                act.wait_ge(s_cos, 2)
                A(cosT[NOPE:QKD, :], cosT[NOPE:QKD, :], ACT.Sin).then_inc(s_tab, 1)

            def M(a):
                i = auxi[("M", a)]
                act.wait_ge(s_aux, i + 1)
                if a == 0:
                    act.wait_ge(s_init, 2)
                if a < HEADS:
                    dst = qm1[QKD:QKD + 1, a % 2, :]
                elif a < 12:
                    dst = mrow[0:1, :]
                else:
                    dst = Q2[QKD:QKD + 1, (a - 12) % 4, :]
                nc.scalar.copy(dst, ax[i % 2][0:1, :]).then_inc(s_auxfree[i % 2], 1)

            def T_(a, kb):
                act.wait_ge(s_T, t_no[("T", a, kb)])
                if a > 0:
                    act.wait_ge(s_PV, pv_no[(a - 1, min(kb, n_keys(a - 1) - 1))])
                c0 = q0(a, kb)
                scale = QKD ** -0.5 if a < HEADS else P ** -0.5 if a < 12 else 1.0
                n = tile_no[("T", a, kb)]
                A(PT[:, kb, c0:T], scb[n % 3][:, c0:T], ACT.Exp, scale=scale).then_inc(s_P, 1)

            def forget(n):
                act.wait_ge(s_fmag, 1)
                link(A(zsm[0:8, 1, :], zsm[0:8, 1, :], ACT.Exp))
                A(zsm[0:8, 1, :], zsm[0:8, 1, :], ACT.Ln, bias=1.0).then_inc(s_fch, 1)

            for s in STEPS:
                if s[0] == "proj":
                    evac(s[1])
                elif s[0] == "norm":
                    norm(s[1])
                elif s[0] == "rope_tables":
                    rope_tables()
                elif s[0] == "cast":
                    cast()
                elif s[0] == "M":
                    M(s[1])
                elif s[0] == "T":
                    T_(s[1], s[2])
                elif s[0] == "post" and s[1] == "forget":
                    forget(s[3][0])

            def rank_exp(tb):
                act.wait_ge(s_sm, tb + 1)
                A(ee, ee, ACT.Exp).then_inc(s_ex, 1)

            def lists_out(tb):
                act.wait_ge(s_lt, tb + 1)
                nc.scalar.copy(lists[:, :, tb * P:(tb + 1) * P],
                               bank[tb % 2][:, 0:3 * P].rearrange("p (w t) -> p w t", w=3)).then_inc(s_ltc, 1)

            def scores_out(tb):
                if tb >= 2:
                    act.wait_ge(s_tk, tb - 1)
                for c in range(4):
                    n = 4 * tb + c
                    act.wait_ge(s_qs, n + 1)
                    nc.scalar.copy(sc[:, tb % 2, c * T:(c + 1) * T], bank[2 + n % 4][:, :]).then_inc(s_qe, 1)

            scores_out(0)
            scores_out(1)
            for tb in range(TB):
                rank_exp(tb)
                lists_out(tb)
                if tb + 2 < TB:
                    scores_out(tb + 2)
            act.wait_ge(s_hx, 1)
            for b in range(8):
                nc.scalar.copy(xT[:, b, :], bank[b][:, :]).then_inc(s_hxc, 1)
            for k in range(KD):
                nc.scalar.copy(hh[:, k, :], hT[:, k, :]).then_inc(s_hh, 1)
            act.wait_ge(s_tk, TB)
            for tb in range(TB):
                if tb >= 2:
                    act.wait_ge(s_gst[tb % 2], 16 * 4 * (tb // 2))
                with act.Fori(0, 16) as it:
                    for u in range(2):
                        act.wait_ge(s_gm[u], it + (16 * tb + 1))
                        dst = stage[:, tb % 2, :, bass.ds(it * 8 + 4 * u, 4)].rearrange("p i t -> p t i")
                        nc.scalar.copy(dst, bank[u][:, :].rearrange("p (t i) -> p t i", t=4)).then_inc(s_ge[u], 1)
            def high_u(e, slot, turn):
                if slot % 2 == 0:
                    act.wait_ge(s_u[slot // 2], turn * 16 + 16)
                at_least(act, s_hid, e - 1)
                nc.scalar.copy(U2[:, slot % 2, 0].rearrange("p k e -> p (k e)"), UR[:, slot, :]).then_inc(s_uhi, 1)

            def expert_tiles(turn, last):
                for u in range(4):
                    e = turn * 4 + u
                    act.wait_ge(s_hid, e + 1)
                    at_least(act, s_alo, e - 3)
                    A(AF[:, u, :], bank[u % 2][:, :], ACT.Gelu).then_inc(s_gelu, 1)
                    if not last or u < 2:
                        high_u(e + 2, (u + 2) % 4, turn + (u + 2) // 4)
                    if u % 2 == 0:
                        act.wait_ge(s_v[u // 2], turn * 16 + 16)
                    at_least(act, s_eo, turn * 16 + (8 * (u // 2) - 8))
                    nc.scalar.copy(V2[:, u, 0], VR[:, u, :]).then_inc(s_vhi, 1)
                    act.wait_ge(s_act, e + 1)
                    nc.scalar.copy(A2[:, u, 0], AF[:, u, :]).then_inc(s_ahi, 1)

            high_u(0, 0, 0)
            high_u(1, 1, 0)
            expert_tiles(0, False)
            with act.Fori(1, NG // 2 - 1) as it:
                expert_tiles(it, False)
            expert_tiles(NG // 2 - 1, True)
            for tb in range(TB):
                act.wait_ge(s_ea, NG * 8)
                A(fsq, xT[:, 2 * tb:2 * tb + 2, :].rearrange("p k n -> p (k n)"), ACT.Square,
                  scale=D ** -0.5, accum_out=fss[:, tb:tb + 1]).then_inc(s_fsq, 1)
                act.wait_ge(s_fsq, 3 * tb + 1)
                A(fss[:, 4 + tb:5 + tb], fss[:, tb:tb + 1], ACT.Ln, bias=col("eps")).then_inc(s_fsq, 1)
                act.wait_ge(s_fsq, 3 * tb + 2)
                A(fss[:, 8 + tb:9 + tb], fss[:, 4 + tb:5 + tb], ACT.Exp, scale=-0.5).then_inc(s_fsq, 1)

        @block.vector
        def _(dve):
            V = nc.vector
            chain = [0]

            def link(ins):
                chain[0] += 1
                ins.then_inc(s_d, 1)
                dve.wait_ge(s_d, chain[0])

            ended = {}

            def end(ins, s, name):
                ended[name] = (s, ended.pop(name, (s, 0))[1] + 1)
                ins.then_inc(s, 1)

            def settle():
                if ended:
                    dve.wait_ge(*list(ended.values())[-1])

            dve.wait_ge(s_par, 16)
            dve.wait_ge(s_const, 16)

            def norm(key):
                nk, width, N = norm_shape(key)
                rows = min(width, P)
                j = norm_no[key]
                dve.wait_ge(s_rs, j)
                r = rs[0:rows, j % 2, 0:N]
                for k in range(nk):
                    if key == "x":
                        dst, src, g = hT[:, k, :], xT[:, k, :], col("norm", k)
                    elif key in ("x2", "h2"):
                        dst, src, g = hT[:, k, :], xT[:, k, :], col({"x2": "norm1", "h2": "norm2"}[key], k)
                    elif key == "ql":
                        dst = src = lat[:, k, :]
                        g = col("qn", k)
                    elif key == "kvl":
                        dst = src = lat[:, QL + k, :]
                        g = col("kvn", k)
                    elif key == "mem":
                        dst = src = memT[:, k, :]
                        g = col("memn", k)
                    elif key.startswith("mq"):
                        dst = src = mq[:, int(key[2:]), :]
                        g = col("mq")
                    elif key.startswith("mk"):
                        dst = src = mkT[:, int(key[2:]), :]
                        g = col("mk")
                    else:
                        dst = src = (qm1 if key[0] == "q" else km1)[0:QKD, int(key[1:]) % 2, :]
                        g = col(key[0] + "h", 0, 0, QKD)
                    ins = V.scalar_tensor_tensor(dst, src, g, r, ALU.mult, ALU.mult)
                end(ins, s_norm, "s_norm")

            def rope_tables():
                R = slice(NOPE, QKD)
                dve.wait_ge(s_pos, 16)
                dve.wait_ge(s_cast, 6)
                ang, kk, t1, t2 = zsm[R, 0, :], zsm[R, 1, :], rtmp[R, :], cosT[R, :]
                magic = 12582912.0
                c1 = 6.28125
                c2 = float(np.float32(np.floor((2 * np.pi - c1) * 2 ** 21) / 2 ** 21))
                c3 = float(2 * np.pi - c1 - c2)
                link(V.tensor_copy(ang, pos_i[R, :]))
                link(V.tensor_scalar(ang, ang, col("invf", 0, NOPE, QKD), None, ALU.mult))
                for which, dst in ((0, t1), (1, t2)):
                    if which:
                        link(V.tensor_scalar(kk, ang, 1.0 / (2 * np.pi), 0.25, ALU.mult, ALU.add))
                    else:
                        link(V.tensor_scalar(kk, ang, 1.0 / (2 * np.pi), None, ALU.mult))
                    link(V.tensor_scalar(kk, kk, magic, None, ALU.add))
                    link(V.tensor_scalar(kk, kk, magic, None, ALU.subtract))
                    link(V.scalar_tensor_tensor(dst, kk, -c1, ang, ALU.mult, ALU.add))
                    link(V.scalar_tensor_tensor(dst, kk, -c2, dst, ALU.mult, ALU.add))
                    link(V.scalar_tensor_tensor(dst, kk, -c3, dst, ALU.mult, ALU.add))
                    if which:
                        link(V.tensor_scalar(dst, dst, np.pi / 2, None, ALU.add))
                    V.tensor_scalar(dst, dst, 3.1415925, -3.1415925, ALU.min, ALU.max).then_inc(s_cos, 1)

            def rope(h, which):
                i = auxi[("rope", h, which)]
                R = slice(NOPE, QKD)
                x = (qm1, km1)[which][R, h % 2, :]
                dve.wait_ge(s_tab, 2)
                dve.wait_ge(s_aux, i + 1)
                V.tensor_tensor(rtmp[R, :], ax[i % 2][R, :], sinT[R, :], ALU.mult).then_inc(s_auxfree[i % 2], 1)
                link(V.tensor_tensor(x, x, cosT[R, :], ALU.mult))
                end(V.tensor_tensor(x, x, rtmp[R, :], ALU.add), s_rope, "s_rope")

            def S(a, qb):
                n = tile_no[("S", a, qb)]
                dve.wait_ge(s_S, s_no[("S", a, qb)])
                N = (qb + 1) * P if a >= 12 else n_keys(a) * P
                c = 4 * (a % 2) + qb
                V.tensor_reduce(mx[:, c:c + 1], scb[n % 3][:, 0:N], AX.X, ALU.max).then_inc(s_max, 1)

            def count(a, kb):
                dve.wait_ge(s_P, t_no[("T", a, kb)])
                c0 = q0(a, kb)
                V.tensor_tensor(PT[:, kb, c0:T], PT[:, kb, c0:T], cnt[:, 0:T - c0], ALU.mult).then_inc(s_Pc, 1)

            def O(a):
                dve.wait_ge(s_PV, pv_no[(a, n_keys(a) - 1)])
                if HEADS <= a < 12:
                    i = auxi[("den", a)]
                    V.reciprocal(dtmp, ax[i % 2][:, :]).then_inc(s_auxfree[i % 2], 1)
                    dve.wait_ge(s_auxfree[i % 2], i // 2 + 1)
                    end(V.tensor_tensor(oT[:, a, :], ob[:, :], dtmp, ALU.mult), s_O, "s_O")
                    return
                h = a if a < HEADS else a - 12
                r0 = DH * (h % 2)
                d0 = DH - r0
                link(V.reciprocal(dtmp[r0:r0 + DH, :], ob[d0:d0 + DH, :]))
                end(V.tensor_tensor(oT[r0:r0 + DH, h // 2, :], ob[r0:r0 + DH, :], dtmp[r0:r0 + DH, :],
                                ALU.mult), s_O, "s_O")

            def post(kind, i, ns):
                for n in ns:
                    dve.wait_ge(s_evac, n + 1)
                e = [ebuf[:, TEMPS[n] % NE, :] for n in ns]
                if kind == "conv":
                    c, u, b, g = e
                    if i == 0:
                        dve.wait_ge(s_init, 3)
                    z, w = zc, cwork
                    link(V.tensor_tensor(z[:, 1:T + 1], c, u, ALU.mult))
                    link(V.tensor_scalar(w[:, 0, :], z[:, 0:T], col("cw", i), None, ALU.mult))
                    link(V.scalar_tensor_tensor(w[:, 0, :], z[:, 1:T + 1], col("cw", 4 + i), w[:, 0, :],
                                                ALU.mult, ALU.add))
                    link(V.scalar_tensor_tensor(w[:, 0, :], z[:, 2:T + 2], col("cw", 8 + i), w[:, 0, :],
                                                ALU.mult, ALU.add))
                    link(V.scalar_tensor_tensor(w[:, 0, :], w[:, 0, :], col("cb", i), b, ALU.add, ALU.mult))
                    end(V.tensor_tensor(oT[:, 4 + i, :], w[:, 0, :], g, ALU.mult), s_post, "s_post")
                elif kind == "gate":
                    dve.wait_ge(s_O, HEADS)
                    end(V.tensor_tensor(oT[:, i, :], oT[:, i, :], e[0], ALU.mult), s_post, "s_post")
                elif kind == "mgate":
                    dve.wait_ge(s_O, HEADS + MEM_HEADS)
                    dve.wait_ge(s_evac, pi[("gate", 7)] + 1)
                    end(V.tensor_tensor(oT[:, 8 + i, :], oT[:, 8 + i, :], memgate[:, i, :], ALU.mult), s_post, "s_post")
                elif kind == "rb":
                    f, b = i // 3, i % 3
                    if b == 0:
                        end(V.tensor_tensor(yT[:, f, :], e[0], e[1], ALU.mult), s_post, "s_post")
                    else:
                        link(V.tensor_tensor(dtmp, e[0], e[1], ALU.mult))
                        end(V.tensor_tensor(yT[:, f, :], yT[:, f, :], dtmp, ALU.add), s_post, "s_post")
                    dve.wait_ge(s_post, post_no[("rb", i)])
                elif kind in ("res", "res2"):
                    end(V.tensor_tensor(xT[:, i, :], xT[:, i, :], e[0], ALU.add), s_post, "s_post")
                else:
                    assert kind == "forget"
                    z = e[0][0:8, :]
                    z0, z1, z2 = zsm[0:8, 0, :], zsm[0:8, 1, :], zsm[0:8, 2, :]
                    link(V.tensor_scalar(z0, z, 0.0, None, ALU.max))
                    V.scalar_tensor_tensor(z1, z, 0.0, z0, ALU.min, ALU.subtract).then_inc(s_fmag, 1)
                    dve.wait_ge(s_fch, 1)
                    link(V.scalar_tensor_tensor(z0, z, 0.0, z1, ALU.min, ALU.subtract))
                    link(V.tensor_scalar(z0, z0, -1.0, None, ALU.mult))
                    link(V.memset(z1, 1.0))
                    end(V.tensor_tensor_scan(z2, z1, z0, 0.0, ALU.mult, ALU.add), s_post, "s_post")

            for s in STEPS:
                if s[0] in ("norm", "rope", "O", "post"):
                    settle()
                if s[0] == "norm":
                    norm(s[1])
                elif s[0] == "rope_tables":
                    rope_tables()
                elif s[0] == "rope":
                    rope(s[1], s[2])
                elif s[0] == "S":
                    S(s[1], s[2])
                elif s[0] == "T" and s[1] >= 20:
                    count(s[1], s[2])
                elif s[0] == "O":
                    O(s[1])
                elif s[0] == "post":
                    post(s[1], s[2], s[3])

            for tb in range(TB):
                dve.wait_ge(s_qe, 4 * (tb + 1))
                b = sc[:, tb % 2, :].rearrange("p (h k) -> p h k", h=16)
                for hp in range(16):
                    ins = V.max(tv[:, hp, 0:8], b[:, hp, :])
                link(ins)
                for hp in range(16):
                    ins = V.max_index(ti[:, hp, 0:8], tv[:, hp, 0:8], b[:, hp, :])
                link(ins)
                for hp in range(16):
                    ins = V.match_replace(b[:, hp, :], tv[:, hp, 0:8], b[:, hp, :], -BIG)
                link(ins)
                for hp in range(16):
                    ins = V.max(tv[:, hp, 8:16], b[:, hp, :])
                link(ins)
                for hp in range(16):
                    ins = V.max_index(ti[:, hp, 8:16], tv[:, hp, 8:16], b[:, hp, :])
                link(ins)
                tvh = tv.rearrange("p (h w) k -> p h w k", w=2)
                c4 = cand.rearrange("p (h a b) -> p h a b", h=8, a=16)
                ch = cand.rearrange("p (h n) -> p h n", h=8)
                link(V.tensor_tensor(c4, tvh[:, :, 0, :].unsqueeze(3).to_broadcast([P, 8, 16, 16]),
                                     tvh[:, :, 1, :].unsqueeze(2).to_broadcast([P, 8, 16, 16]), ALU.add))
                link(V.tensor_copy(tif, ti.rearrange("p h k -> p (h k)")))
                for h in range(8):
                    ins = V.max(cs[:, h, 0:8], ch[:, h, :])
                link(ins)
                for h in range(8):
                    ins = V.max_index(ci[:, h, 0:8], cs[:, h, 0:8], ch[:, h, :])
                link(ins)
                for h in range(8):
                    ins = V.match_replace(ch[:, h, :], cs[:, h, 0:8], ch[:, h, :], -BIG)
                link(ins)
                for h in range(8):
                    ins = V.max(cs[:, h, 8:16], ch[:, h, :])
                link(ins)
                for h in range(8):
                    ins = V.max_index(ci[:, h, 8:16], cs[:, h, 8:16], ch[:, h, :])
                link(ins)
                e3 = ee.rearrange("p (h k) -> p h k", h=8)
                if tb >= 1:
                    dve.wait_ge(s_lt, tb)
                V.tensor_tensor(e3, cs, cs[:, :, 0:1].to_broadcast([P, 8, 16]), ALU.subtract).then_inc(s_sm, 1)
                cif = ci.rearrange("p h k -> p (h k)")
                for w in range(2):
                    if w == 0:
                        link(V.tensor_scalar(ca, cif, 4, None, ALU.logical_shift_right))
                    else:
                        link(V.tensor_scalar(ca, cif, 15, None, ALU.bitwise_and))
                    link(V.tensor_copy(cbf[:, w, :], ca))
                    q3 = eq.rearrange("p (r m) -> p r m", m=16)
                    q4 = eq.rearrange("p (h k m) -> p h k m", h=8, k=16)
                    tf = tif.rearrange("p (h w m) -> p h w m", h=8, w=2)[:, :, w, :]
                    link(V.tensor_tensor(q3, cbf[:, w, :].unsqueeze(2).to_broadcast([P, P, 16]),
                                         iota16.unsqueeze(1).to_broadcast([P, P, 16]), ALU.is_equal))
                    link(V.tensor_tensor(q4, q4, tf.unsqueeze(2).to_broadcast([P, 8, 16, 16]), ALU.mult))
                    link(V.tensor_reduce(sel[:, w, :], q3, AX.X, ALU.add))
                dve.wait_ge(s_ex, tb + 1)
                link(V.tensor_reduce(es[:, 0:8], e3, AX.X, ALU.add))
                link(V.reciprocal(es[:, 8:16], es[:, 0:8]))
                V.tensor_tensor(sel[:, 2, :].rearrange("p (h k) -> p h k", h=8), e3,
                                es[:, 8:16].unsqueeze(2).to_broadcast([P, 8, 16]), ALU.mult).then_inc(s_tk, 1)

            for k in range(KD):
                dve.wait_ge(s_hh, k + 1)
                V.tensor_tensor(hl[:, k, :], hT[:, k, :], hh[:, k, :].bitcast(F32), ALU.subtract).then_inc(s_hl, 1)
            dve.wait_ge(s_ltc, TB)
            dve.wait_ge(s_tk, TB)
            def onehots(it, first):
                for u in range(2):
                    if not first:
                        dve.wait_ge(s_gm[u], it)
                    for k in range(4):
                        t = it * 8 + (4 * u + k)
                        V.tensor_scalar(ohring[:, u, 0, k, :], iota, lists[:, 0, bass.ds(t, 1)],
                                        lists[:, 2, bass.ds(t, 1)], ALU.is_equal, ALU.mult)
                        ins = V.tensor_scalar(ohring[:, u, 1, k, :], iota, lists[:, 1, bass.ds(t, 1)], None,
                                              ALU.is_equal)
                    ins.then_inc(s_oh, 1)

            onehots(0, True)
            with dve.Fori(1, T // 8) as it:
                onehots(it, False)

            def gated(turn, half):
                for u in (2 * half, 2 * half + 1):
                    e = turn * 4 + u
                    if u % 2 == 0:
                        dve.wait_ge(s_g[half], turn * 16 + 16)
                    dve.wait_ge(s_gelu, e + 1)
                    V.tensor_tensor(AF[:, u, :], AF[:, u, :], GR[:, u, :], ALU.mult).then_inc(s_act, 1)
                    dve.wait_ge(s_ahi, e + 1)
                    V.tensor_tensor(A2[:, u, 1], AF[:, u, :], A2[:, u, 0].bitcast(F32), ALU.subtract)\
                        .then_inc(s_alo, 1)

            def add_outputs(g):
                for u in range(8):
                    dve.wait_ge(s_eo, g * 8 + (u + 1))
                    V.tensor_tensor(xT[:, u, :], xT[:, u, :], bank[2 + u % 4][:, :], ALU.add).then_inc(s_ea, 1)

            dve.wait_ge(s_hxc, 8)
            gated(0, 0)
            gated(0, 1)
            add_outputs(0)
            with dve.Fori(1, NG // 2) as it:
                gated(it, 0)
                add_outputs(it * 2 - 1)
                gated(it, 1)
                add_outputs(it * 2)
            add_outputs(NG - 1)
            dve.wait_ge(s_gf, 16)
            for tb in range(TB):
                dve.wait_ge(s_fsq, 3 * (tb + 1))
                row = xT[:, 2 * tb:2 * tb + 2, :].rearrange("p k n -> p (k n)")
                V.scalar_tensor_tensor(row, row, fss[:, 8 + tb:9 + tb], gf, ALU.mult, ALU.mult).then_inc(s_fin, 1)


def _tiles(np_, w, cols_per_tile):
    K, F = w.shape
    t = w.reshape(K // 128, 128, F // cols_per_tile, cols_per_tile).transpose(2, 1, 0, 3)
    return np_.ascontiguousarray(t).reshape(F // cols_per_tile, 128, -1)


def _rows(np_, w, per):
    K, F = w.shape
    t = w.reshape(K // 128 // per, per, 128, F).transpose(0, 2, 1, 3)
    return np_.ascontiguousarray(t).reshape(K // 128 // per, 128, per * F)


def _cols(np_, v):
    return np_.ascontiguousarray(v.reshape(-1, 128).T)


def _pad(np_, v, n=128):
    c = np_.zeros((n, 1), v.dtype)
    c[:v.shape[0], 0] = v
    return c


def _constants(np_):
    f = np_.float32
    d = np_.arange(128)
    eye = np_.eye(128, dtype=f)
    rot = np_.zeros((128, 128), f)
    for i in range(HALF):
        rot[NOPE + HALF + i, NOPE + i] = -1.0
        rot[NOPE + i, NOPE + HALF + i] = 1.0
    iota = np_.broadcast_to(np_.arange(128, dtype=f), (128, 128))
    iota16 = iota[:, :16]
    msf = np_.where(d[None, :] <= d[:, None], 0.0, NEG).astype(f)
    mtf = np_.ascontiguousarray(msf.T)
    dq = d[:, None] - (np_.arange(512)[None, :] - 384)
    dt = np_.arange(512)[None, :] - d[:, None]

    def patterns(x):
        return ((x >= 0) & (x <= 128)).astype(int) + ((x >= 0) & (x % 4 == 0)) + ((x >= 0) & (x % 16 == 0))

    msd = np_.where(patterns(dq) > 0, 0.0, NEG).astype(f)
    mtd = np_.where(patterns(dt) > 0, 0.0, NEG).astype(f)
    return np_.ascontiguousarray(np_.concatenate(
        [eye, -eye, np_.ones((128, 128), f), rot, iota, iota16, msf, mtf, msd, mtd, patterns(dt).astype(f)], axis=1))


def kernel(**inputs):
    import numpy as _np
    import concourse.bacc as _bacc
    from concourse import mybir as _mybir
    from concourse.bass_utils import run_bass_kernel_spmd as _run

    a = {k: _np.asarray(v) for k, v in inputs.items()}
    w = a["w_in"][0]
    at = _np.cumsum([0, 384, 256, 32, 512, 512, 512, 512, 512, 512, 512, 3072])
    part = {k: w[:, at[i]:at[i + 1]] for i, k in enumerate(
        ("ql", "kvl", "kpe", "cb", "cc", "cu", "qm", "ga", "gc", "gm", "r"))}
    tl = lambda x, c=128: _tiles(_np, x, c)
    cv = _np.stack([tl(part[k]) for k in ("cc", "cu", "cb", "gc")], axis=1).reshape(16, 128, -1)
    kpe = _np.concatenate([_np.zeros((1024, 64), w.dtype), part["kpe"]], axis=1)
    ukv = a["w_ukv"][0].reshape(256, 8, 128)
    mkv = a["w_mkv"][0].reshape(1024, 4, 256)
    br = _np.stack([tl(a[k][0]) for k in ("w_br_attn", "w_br_conv", "w_br_mem")], axis=1).reshape(24, 128, -1)
    r = tl(part["r"]).reshape(3, 8, 128, -1).transpose(1, 0, 2, 3).reshape(24, 128, -1)
    w2 = a["w_in_2"][0]
    fq, fk, fv, wf, dq, dk, dv = (w2[:, i:j] for i, j in ((0, 512), (512, 1024), (1024, 1536), (1536, 1544),
                                                          (1544, 2056), (2056, 2568), (2568, 3080)))
    qk2 = _np.concatenate([_np.stack([tl(q), tl(k)], axis=1).reshape(8, 128, -1) for q, k in ((fq, fk), (dq, dk))])
    invf = (_np.float32(10000.0) ** (-_np.arange(0, 32, 2, dtype=_np.float32) / _np.float32(32))).astype(_np.float32)
    col = lambda k: _cols(_np, a[k][0])
    pad = lambda v: _pad(_np, v)
    table = _np.concatenate([
        col("norm_g"), col("q_norm_g"), col("kv_norm_g"), pad(a["q_head_g"][0]), pad(a["k_head_g"][0]),
        a["conv_w"][0].reshape(12, 128).T, col("conv_b"), col("mem_norm_g"), col("mem_q_g"), col("mem_k_g"),
        a["b_gate"][0].reshape(3, 8, 128).transpose(1, 0, 2).reshape(24, 128).T, col("norm1_g_2"),
        col("norm2_g_2"), pad(a["b_forget_2"][0]),
        pad(_np.concatenate([_np.zeros(64, _np.float32), invf, invf])),
        _np.full((128, 1), EPS, _np.float32)], axis=1)
    slopes = 2.0 ** -_np.arange(1, 9, dtype=_np.float32)
    arrays = {
        "xT": a["x"][0].T.reshape(8, 128, 512).transpose(1, 0, 2),
        "memT": a["mem"][0].T.reshape(8, 128, 256).transpose(1, 0, 2),
        "pos": a["positions"], "cols": table, "const": _constants(_np),
        "bias": (slopes[:, None] * _np.arange(512, dtype=_np.float32)[None]).astype(_np.float32),
        "lat": tl(_np.concatenate([part["ql"], part["kvl"]], axis=1)), "kpe": tl(kpe, 96),
        "conv": cv, "gate": _np.concatenate([tl(part["ga"]), tl(part["gm"])]), "qm": tl(part["qm"]),
        "uq": tl(a["w_uq"][0], 96), "uk": tl(ukv[:, :, :64].reshape(256, 512), 64),
        "uv": _rows(_np, ukv[:, :, 64:].reshape(256, 512), 2),
        "mk": tl(mkv[:, :, :128].reshape(1024, 512)), "mv": _rows(_np, mkv[:, :, 128:].reshape(1024, 512), 2),
        "rb": _np.concatenate([r, br], axis=2), "wo": tl(a["w_out"][0]),
        "wf": tl(wf, 8), "v2": _np.concatenate([_rows(_np, fv, 2), _rows(_np, dv, 2)]), "qk2": qk2,
        "wo2": tl(a["w_out_2"][0]), "wq": tl(a["peer_wq_2"][0]),
        "sk": a["peer_subkeys_2"][0].reshape(16, 128, 128).transpose(2, 0, 1),
        "uT": a["peer_u_2"][0].reshape(128, 128, 8, 128).transpose(0, 3, 2, 1).reshape(128, 128, 1024),
        "v": a["peer_v_2"][0].reshape(128, 128, 1024),
        "gf": a["normf_g_2"].reshape(1, 1024),
    }
    nc = _bacc.Bacc("TRN2", target_bir_lowering=False, num_devices=1)
    feed, t_in = {}, {}
    for name, x in arrays.items():
        x = _np.ascontiguousarray(x)
        feed[f"in_{name}"] = x
        t_in[name] = nc.dram_tensor(f"in_{name}", x.shape, _mybir.dt.from_np(x.dtype), kind="ExternalInput").ap()
    out = nc.dram_tensor("out_0", (512, 1024), _mybir.dt.float32, kind="ExternalOutput").ap()
    program(nc, t_in, out)
    res = _run(nc, [feed], core_ids=[0])
    return res.results[0]["out_0"].reshape(1, 512, 1024)
```

```python
from contextlib import ExitStack

import numpy as np

import concourse.bass as bass
from concourse import mybir

F32 = mybir.dt.float32
F32R = mybir.dt.float32r
BF16 = mybir.dt.bfloat16
U32 = mybir.dt.uint32
I32 = mybir.dt.int32
ALU = mybir.AluOpType
ACT = mybir.ActivationFunctionType
AX = mybir.AxisListType

P = 128
D = 1024
KD = D // P
T = 512
TB = T // P
MEM = 256
MB = MEM // P
HEADS = 8
QL, KVL = 3, 2
NOPE, ROPE = 64, 32
QKD = NOPE + ROPE
HALF = ROPE // 2
DH = 64
MEM_HEADS = 4
EPS = 1e-6
ATT2 = 16
TOPK = 16
NT = 128
NS = 64
FREE = (8, 6, 6, 6)
GATED = 8
START = [sum(FREE[:i]) + GATED * i for i in range(5)]
NG = NT - NS
PEER_HEADS = 8
NKEYS = 128
NEG = -1e30
BIG = 3.0e38

COLS = {}
_n = 0
for _name, _k in (("norm", 8), ("qn", 3), ("kvn", 2), ("qh", 1), ("kh", 1), ("cw", 12), ("cb", 4), ("memn", 8),
                  ("mq", 1), ("mk", 1), ("bg", 24), ("norm1", 8), ("norm2", 8), ("bf", 1), ("invf", 1), ("eps", 1)):
    COLS[_name] = _n
    _n += _k
NCOLS = _n

CN = {}
_n = 0
for _name, _k in (("ident", 128), ("negid", 128), ("ones", 128), ("rot", 128), ("iota", 128), ("iota16", 16),
                  ("msf", 128), ("mtf", 128), ("msd", 512), ("mtd", 512), ("cnt", 512)):
    CN[_name] = _n
    _n += _k
NCONST = _n
NKEEP = CN["msf"]

LOADS = []
PROJ = []
STEPS = []
TEMPS = {}
POST_OF = []


def build_schedule():
    if STEPS:
        return

    def load(kind, i, n):
        LOADS.append((kind, i, n))
        return len(LOADS) - 1

    def proj(kind, i, loads, temp=False):
        n = len(PROJ)
        PROJ.append((kind, i, loads))
        if temp:
            TEMPS[n] = len(TEMPS)
            POST_OF.append(None)
        STEPS.append(("proj", n))
        return n

    posts = [0]

    def post(kind, i, ns):
        posts[0] += 1
        for n in ns:
            POST_OF[TEMPS[n]] = posts[0]
        STEPS.append(("post", kind, i, ns, posts[0]))

    def tile(kind, i, k, m, temp=False):
        return proj(kind, i, [load(kind, i, k * m)], temp)

    def pre_q(h):
        tile("uq", h, QL, QKD)

    def pre_k(h):
        tile("uk", h, KVL, NOPE)

    conv_ns = []

    def conv_part(c):
        conv_ns.append(tile("conv", c, KD, P, True))
        if c % 4 == 3:
            post("conv", c // 4, conv_ns[-4:])

    STEPS.append(("norm", "x"))
    for i in range(QL + KVL):
        tile("lat", i, KD, P)
        if i == 0:
            STEPS.append(("cast",))
    tile("kpe", 0, KD, QKD)
    STEPS.append(("rope_tables",))
    STEPS.append(("sq", "kvl"))
    conv_part(0)
    STEPS.append(("norm", "kvl"))
    STEPS.append(("sq", "ql"))
    conv_part(1)
    STEPS.append(("norm", "ql"))
    L = load("uv", 0, KVL * 512)
    for tb in range(TB):
        proj("uv", tb, [L])
    def normed(kind, h):
        pairs = [("qm", i) for i in range(MEM_HEADS)] + [("mk", i) for i in range(MEM_HEADS)]
        n = pairs.index((kind, h)) - 1
        key = {"qm": "mq", "mk": "mk"}[pairs[n][0]] + str(pairs[n][1]) if n >= 0 else None
        if key:
            STEPS.append(("sq", key))
        tile(kind, h, KD, P)
        if key:
            STEPS.append(("norm", key))

    def mem_values():
        STEPS.append(("sq", f"mk{MEM_HEADS - 1}"))
        Ls = [load("mv", c, 1024) for c in range(4)]
        for tb in range(MB):
            proj("mv", tb, Ls)
        STEPS.append(("norm", f"mk{MEM_HEADS - 1}"))

    fill = [lambda c=c: conv_part(c) for c in range(2, 16)]
    fill += [lambda: (STEPS.append(("norm", "mem")), normed("qm", 0))]
    fill += [lambda h=h: normed("qm", h) for h in range(1, MEM_HEADS)]
    fill += [lambda h=h: normed("mk", h) for h in range(MEM_HEADS)]
    fill += [mem_values]

    def filler():
        if fill:
            fill.pop(0)()

    def prep_mla(h):
        yield lambda: (pre_q(h), pre_k(h), STEPS.append(("sq", f"q{h}")), STEPS.append(("sq", f"k{h}")))
        yield lambda: STEPS.append(("norm", f"q{h}"))
        yield lambda: STEPS.append(("norm", f"k{h}"))
        yield lambda: STEPS.append(("rope", h, 0))
        yield lambda: STEPS.append(("rope", h, 1))

    for f in prep_mla(0):
        f()
        filler()
    for qb in range(TB):
        STEPS.append(("S", 0, qb))
    filler()
    STEPS.append(("M", 0))
    for h in range(HEADS):
        nxt = prep_mla(h + 1) if h + 1 < HEADS else iter(())

        def more():
            f = next(nxt, None)
            if f:
                f()
        more()
        STEPS.append(("T", h, 0))
        STEPS.append(("T", h, 1))
        more()
        STEPS.append(("PV", h, 0))
        STEPS.append(("T", h, 2))
        more()
        STEPS.append(("PV", h, 1))
        STEPS.append(("T", h, 3))
        more()
        STEPS.append(("PV", h, 2))
        more()
        STEPS.append(("PV", h, 3))
        STEPS.append(("O", h))
        if h + 1 < HEADS:
            filler()
            for qb in range(TB):
                STEPS.append(("S", h + 1, qb))
            filler()
            STEPS.append(("M", h + 1))
    while fill:
        filler()
    def gate(i):
        n = tile("gate", i, KD, P, i < 4)
        if i < 4:
            post("gate", i, [n])

    for h in range(MEM_HEADS):
        a = HEADS + h
        for qb in range(TB):
            STEPS.append(("S", a, qb))
        gate(2 * h)
        STEPS.append(("M", a))
        for kb in range(MB):
            STEPS.append(("T", a, kb))
        for kb in range(MB):
            STEPS.append(("PV", a, kb))
        STEPS.append(("O", a))
        gate(2 * h + 1)
    for i in range(4):
        post("mgate", i, [])
    for f in range(KD):
        for b in range(3):
            L1 = load("rb", 3 * f + b, 12 * P)
            n1 = proj("r", 3 * f + b, [L1], True)
            n2 = proj("br", 3 * f + b, [L1], True)
            post("rb", 3 * f + b, [n1, n2])
    for f in range(KD):
        post("res", f, [tile("wo", f, KD, P, True)])

    STEPS.append(("norm", "x2"))
    post("forget", 0, [tile("wf", 0, KD, 8, True)])
    for g in range(2):
        if g == 0:
            Ls = [load("v2", c, 1024) for c in range(4)]
            for tb in range(TB):
                proj("v2", tb, Ls)

    def qk2(p, s):
        tile("qk2", 2 * p + s, KD, P)

    qk2(0, 0)
    qk2(0, 1)
    for qb in range(TB):
        STEPS.append(("S", 12, qb))
    qk2(1, 0)
    STEPS.append(("M", 12))
    for j in range(ATT2):
        a = 12 + j
        more = [("S", a + 1, qb) for qb in range(TB)] if j + 1 < ATT2 else []

        def between():
            if more:
                STEPS.append(more.pop(0))
        STEPS.append(("T", a, 0))
        between()
        STEPS.append(("T", a, 1))
        STEPS.append(("PV", a, 0))
        between()
        STEPS.append(("T", a, 2))
        STEPS.append(("PV", a, 1))
        between()
        STEPS.append(("T", a, 3))
        STEPS.append(("PV", a, 2))
        between()
        STEPS.append(("PV", a, 3))
        STEPS.append(("O", a))
        if j + 1 < ATT2:
            if j == 5:
                Ls = [load("v2", 4 + c, 1024) for c in range(4)]
                for tb in range(TB):
                    proj("v2", TB + tb, Ls)
            STEPS.append(("M", a + 1))
            if j % 2 == 0 and j // 2 + 1 < 8:
                qk2(j // 2 + 1, 1)
            elif j % 2 == 1 and j // 2 + 2 < 8:
                qk2(j // 2 + 2, 0)
    for f in range(KD):
        post("res2", f, [tile("wo2", f, KD, P, True)])
    STEPS.append(("norm", "h2"))
    STEPS.append(("high_h",))
    for i in range(2 * PEER_HEADS):
        tile("wq", i, KD, P)
        if i:
            STEPS.append(("keys", i - 1))
    STEPS.append(("keys", 2 * PEER_HEADS - 1))


def norm_shape(key):
    if key in ("x", "x2", "h2"):
        return KD, D, T
    if key == "mem":
        return KD, D, MEM
    if key == "ql":
        return QL, QL * P, T
    if key == "kvl":
        return KVL, KVL * P, T
    if key.startswith("mq"):
        return 1, P, T
    if key.startswith("mk"):
        return 1, P, MEM
    return 1, QKD, T


def program(nc, t_in, out):
    build_schedule()
    ctx = ExitStack()
    with ctx:
        def sem(name):
            return ctx.enter_context(nc.semaphore(name))

        SB = 52480
        LOW = 2 * KD * T + NKEEP + NCOLS + NCOLS % 2 + 960 + 3 * T

        def place(name, off, shape, dt):
            with nc.sbuf_tensor(name + "_before", [P, off], F32) if off else ExitStack():
                with nc.sbuf_tensor(name, [P] + shape, dt) as buffer:
                    return buffer

        low = place("low", 0, [LOW], F32)
        blocks = place("blocks", LOW, [SB - LOW], F32)
        TAIL = LOW + 16384 + 4096
        staged = place("staged", LOW, [16384], F32)
        v_raw = place("v_raw", LOW + 12288, [4, D], F32)
        tail = place("tail", TAIL, [SB - TAIL], F32)

        def region(off, n, k=None, of=None):
            at, base = of or ((low, 0) if off < LOW else (blocks, LOW))
            v = at[:, off - base:off - base + n]
            return v if k is None else v.rearrange("p (k n) -> p k n", k=k)

        xT = region(0, 4096, KD)
        hT = region(4096, 4096, KD)
        o = 8192
        const = region(o, NKEEP)
        o += NKEEP
        cols = region(o, NCOLS)
        o += NCOLS + NCOLS % 2
        msf = region(o, 64).bitcast(BF16)
        mtf = region(o + 64, 64).bitcast(BF16)
        msd = region(o + 128, 256).bitcast(BF16)
        mtd = region(o + 384, 256).bitcast(BF16)
        cnt = region(o + 640, 256).bitcast(BF16)
        idb = region(o + 896, 64).bitcast(BF16)
        o += 960
        lists = region(o, 3 * T, 3)
        o += 3 * T
        assert o == LOW
        NW = 5
        ring = region(o, NW * 1536, NW)
        o += NW * 1536
        NE = 6
        ebuf = region(o, NE * T, NE)
        o += NE * T
        NQ = 4
        sq = region(o, NQ * T, NQ)
        o += NQ * T
        rs = region(o, 2 * T, 2)
        o += 2 * T
        dtmp = region(o, T)
        o += T
        PT = region(o, 4 * T, 4)
        o += 4 * T
        VA = region(o, 4096).rearrange("p (t h d) -> p t h d", t=TB, h=HEADS)
        vA_off = o
        o += 4096
        oT = region(o, 12 * T, 12)
        oT_off = o
        o += 12 * T
        R1 = o
        lat = region(o, 6 * T, 6)
        o += 6 * T
        qm1 = region(o, 2 * T, 2)
        o += 2 * T
        km1 = region(o, 2 * T, 2)
        o += 2 * T
        rtmp = region(o, T)
        cosT = region(o + T, T)
        sinT = region(o + 2 * T, T)
        o += 3 * T
        memT = region(o, KD * MEM, KD)
        o += KD * MEM
        mkT = region(o, 4 * MEM, 4)
        o += 4 * MEM
        mv = region(o, MB * T, MB)
        o += MB * T
        mq = region(o, 4 * T, 4)
        o += 4 * T
        mrow = region(o, T)
        o += T
        mx = region(o, 8)
        o += 8
        zsm = lists
        memgate = lat[:, 0:4, :]
        cwork = zsm
        zc = region(o, T + 2)
        o += T + 2
        assert o <= SB, o
        yT = region(R1, 4096, KD)
        Q2 = region(R1 + 4096, 4 * T, 4)
        K2 = region(R1 + 4096 + 4 * T, 4 * T, 4)
        VB = region(R1 + 8192, 4096).rearrange("p (t h d) -> p t h d", t=TB, h=HEADS)
        assert R1 + 12288 <= o - (T + 2) - 8 - T
        def rt(off, n, k=None):
            return region(TAIL + off, n, k, (tail, TAIL))

        UR = rt(0, 4 * 1024, 4)
        AF = rt(8192, 4 * T, 4)
        pq = AF
        GR = rt(10240, 4 * T, 4)
        ohring = rt(10240, 2 * 2 * 4 * P).rearrange("p (s w u i) -> p s w u i", s=2, w=2, u=4)
        sk = rt(12288, 2048, 16)
        cand = rt(12288, 2048)
        sc = rt(14336, 4 * T, 4)
        eq = rt(14336, 2048)
        gf = rt(12288, D)
        fsq = rt(13312, D)
        fss = rt(14336, 16)
        tva = rt(16384, 1024, 4).rearrange("p t (h k) -> p t h k", h=16)
        tia = rt(17408, 1024, 4).rearrange("p t (h k) -> p t h k", h=16).bitcast(U32)
        tif = rt(18432, 256)
        cs = rt(18688, 128, 8)
        ci = rt(18816, 128, 8).bitcast(U32)
        ca = rt(18944, 128).bitcast(U32)
        cbf = rt(19072, 256, 2)
        sel = rt(19328, 384, 3)
        ee = rt(19712, 128)
        es = rt(19840, 16)
        assert TAIL + 19856 <= SB
        stage = staged[:, :].rearrange("p (i t) -> p i t", i=P)
        VR = v_raw
        U2 = place("u_split", TAIL + 4096, [2, 2, KD, P], F32R)
        V2 = place("v_split", LOW, [4, 2, D], F32R)
        A2 = place("a_split", LOW + 8192, [4, 2, T], F32R)
        hh = place("h_high", LOW + 16384, [KD, T], F32R)
        hl = place("h_low", 4096, [KD, T], F32R)
        craw = region(oT_off, NCONST - NKEEP)
        pos_i = ebuf[:, 0, :].bitcast(I32)

        ident = const[:, CN["ident"]:CN["ident"] + P]
        negid = const[:, CN["negid"]:CN["negid"] + P]
        ones = const[:, CN["ones"]:CN["ones"] + P]
        rot = const[:, CN["rot"]:CN["rot"] + P]
        iota = const[:, CN["iota"]:CN["iota"] + P]
        iota16 = const[:, CN["iota16"]:CN["iota16"] + 16]

        def col(name, i=0, p0=0, p1=P):
            return cols[p0:p1, COLS[name] + i:COLS[name] + i + 1]

        bank = [ctx.enter_context(nc.psum_tensor(f"bank{i}", [P, T], F32)) for i in range(8)]
        pj = [bank[0], bank[1]]
        ax = [bank[2], bank[7]]
        scb = [bank[3], bank[4], bank[5]]
        ob = bank[6]

        kept = nc.dram_tensor("kept_hidden", (NS, P, T), F32, kind="Internal").ap()
        gates = nc.dram_tensor("gates", (NKEYS, P, T), F32, kind="Internal").ap()

        s_x = sem("x_loaded")
        s_par = sem("params_loaded")
        s_const = sem("constants_loaded")
        s_raw = sem("masks_loaded")
        s_mem = sem("mem_loaded")
        s_pos = sem("positions_loaded")
        s_cast = sem("masks_cast")
        s_init = sem("buffers_set")
        s_init2 = sem("second_block_buffers_set")
        s_w = [sem(f"weights_in_slot{i}") for i in range(NW)]
        s_proj = sem("projections_done")
        s_evac = sem("projections_evacuated")
        s_post = sem("post_steps_done")
        s_sq = sem("squares_ready")
        s_squsd = sem("squares_used")
        s_aux = sem("aux_bank_written")
        s_auxfree = [sem("aux_bank0_read"), sem("aux_bank1_read")]
        s_hk = sem("normalised_tiles_ready")
        s_rs = sem("reciprocal_roots_done")
        s_norm = sem("norm_steps_done")
        s_tab = sem("rope_tables_done")
        s_rope = sem("rope_steps_done")
        s_S = sem("score_rows_done")
        s_max = sem("row_maxima_done")
        s_T = sem("score_columns_done")
        s_P = sem("exponentials_done")
        s_Pc = sem("exponentials_counted")
        s_PV = sem("value_products_done")
        s_O = sem("head_outputs_done")
        s_kb = [sem(f"key_bias_in_buffer{i}") for i in range(4)]
        s_fmag = sem("forget_magnitudes_ready")
        s_fch = sem("forget_logs_done")
        s_d = sem("vector_chain")
        s_rc = sem("scalar_chain")
        s_sk = sem("subkeys_loaded")
        s_cos = sem("angles_ready")
        s_qs = sem("key_scores_done")
        s_qe = sem("key_scores_copied")
        s_half = sem("halves_sorted")
        s_tk = sem("topk_blocks_done")
        s_kept = [sem(f"hidden_kept_slot{i}") for i in range(4)]
        s_h = [sem(f"hidden_back_{i}") for i in range(2)]
        s_sm = sem("rank_differences_ready")
        s_ex = sem("rank_exponentials_done")
        s_lt = sem("lists_transposed")
        s_ltc = sem("lists_copied")
        s_hx = sem("residual_transposed")
        s_hxc = sem("residual_copied")
        s_oh = sem("onehots_ready")
        s_gm = [sem(f"gate_groups_done_bank{i}") for i in range(2)]
        s_ge = [sem(f"gate_groups_copied_bank{i}") for i in range(2)]
        s_gst = sem("gates_stored")
        s_u = [sem(f"u_tile_in_slot{i}") for i in range(4)]
        s_v = [sem(f"v_tiles_{i}") for i in range(2)]
        s_g = [sem(f"g_tiles_{i}") for i in range(2)]
        s_hid = sem("hidden_done")
        s_gelu = sem("gelu_done")
        s_act = sem("gated_done")
        s_ahi = sem("gated_high_parts")
        s_alo = sem("gated_low_parts")
        s_uhi = sem("u_high_parts")
        s_ulo = sem("u_low_parts")
        s_vhi = sem("v_high_parts")
        s_vlo = sem("v_low_parts")
        s_hh = sem("h_high_parts")
        s_hl = sem("h_low_parts")
        s_eo = sem("expert_outputs_done")
        s_ea = sem("expert_outputs_added")
        s_gf = sem("final_gain_loaded")
        s_fin = sem("final_rows_ready")
        s_fsq = sem("final_squares_done")
        s_out = sem("output_stored")

        NORMS = [s[1] for s in STEPS if s[0] == "norm"]
        norm_no = {k: i + 1 for i, k in enumerate(NORMS)}
        sq0, n = {}, 0
        for k in NORMS:
            sq0[k] = n
            n += norm_shape(k)[0]
        pi = {(k, i): n for n, (k, i, _) in enumerate(PROJ)}
        auxi, n = {}, 0
        for s in STEPS:
            if s[0] == "norm":
                auxi[("norm", s[1])] = n
                n += 1
            elif s[0] == "rope":
                auxi[("rope",) + s[1:]] = n
                n += 1
            elif s[0] == "M":
                auxi[("M", s[1])] = n
                n += 1
            elif s[0] == "PV" and HEADS <= s[1] < 12 and s[2] == 0:
                auxi[("den", s[1])] = n
                n += 1
        tiles = [s for s in STEPS if s[0] in ("S", "T")]
        tile_no = {s: i for i, s in enumerate(tiles)}
        s_no = {s: i + 1 for i, s in enumerate(x for x in tiles if x[0] == "S")}
        t_no = {s: i + 1 for i, s in enumerate(x for x in tiles if x[0] == "T")}
        pv_no = {s[1:]: i + 1 for i, s in enumerate(x for x in STEPS if x[0] == "PV")}
        cnt_no = {s[1:]: i + 1 for i, s in enumerate(x for x in STEPS if x[0] == "T" and x[1] >= 20)}
        rope_no = {s[1:]: i + 1 for i, s in enumerate(x for x in STEPS if x[0] == "rope")}
        M_no = {s[1]: i + 1 for i, s in enumerate(x for x in STEPS if x[0] == "M")}
        O_no = {s[1]: i + 1 for i, s in enumerate(x for x in STEPS if x[0] == "O")}
        post_no = {s[1:3]: s[4] for s in STEPS if s[0] == "post"}
        last_use = {}
        for n, (_, _, loads) in enumerate(PROJ):
            for L in loads:
                last_use[L] = n

        def n_keys(a):
            return MB if HEADS <= a < 12 else TB

        def q0(a, kb):
            return kb * P if a >= 12 else 0

        def at_least(eng, sem, value):
            if not isinstance(value, int) or value > 0:
                eng.wait_ge(sem, value)

        def rounds(eng, n, body, first=False, last=False):
            a, b = int(first), n - int(last)
            if first:
                body(0, False)
            if b > a:
                with eng.Fori(a, b) as it:
                    body(it, False)
            if last:
                body(n - 1, True)

        block = ctx.enter_context(nc.Block())

        @block.sync
        def _(sp):
            sp.dma_start(xT, t_in["xT"]).then_inc(s_x, 16)
            sp.dma_start(cols, t_in["cols"]).then_inc(s_par, 16)
            sp.dma_start(const, t_in["const"][:, 0:NKEEP]).then_inc(s_const, 16)

            def weights(L):
                kind, i, n = LOADS[L]
                if L >= NW:
                    sp.wait_ge(s_proj, last_use[L - NW] + 1)
                sp.dma_start(ring[:, L % NW, 0:n], t_in[kind][i]).then_inc(s_w[L % NW], 16)

            for L in range(len(LOADS)):
                weights(L)
                if L == NW - 1:
                    sp.dma_start(craw, t_in["const"][:, NKEEP:NCONST]).then_inc(s_raw, 16)
                    sp.dma_start(pos_i[NOPE:QKD, :], t_in["pos"].to_broadcast([ROPE, T])).then_inc(s_pos, 16)
                    sp.dma_start(memT, t_in["memT"]).then_inc(s_mem, 16)
                if LOADS[L][:2] == ("wq", 0):
                    sp.wait_ge(s_O, len(O_no))
                    sp.dma_start(sk, t_in["sk"]).then_inc(s_sk, 16)
            def load_u(e, slot):
                at_least(sp, s_ulo, e - 3)
                sp.dma_start(UR[:, slot, :], t_in["uT"][bass.ds(e, 1)].rearrange("s p n -> p (s n)"))\
                    .then_inc(s_u[slot], 16)

            def keep(e, slot):
                sp.wait_ge(s_gelu, e + 1)
                sp.dma_start(kept[bass.ds(e, 1)].rearrange("s p n -> p (s n)"), AF[:, slot, :])\
                    .then_inc(s_kept[slot], 16)

            def tile(e, slot=None):
                slot = e % 4 if slot is None else slot
                keep(e, slot)
                load_u(e + 4, slot)

            def store_gates(tb, parts):
                for c in parts:
                    sp.dma_start(gates[16 * c:16 * c + 16, :, tb * P:(tb + 1) * P].rearrange("i j t -> j i t"),
                                 stage[:, 16 * c:16 * c + 16, :]).then_inc(s_gst, 16)

            sp.wait_ge(s_proj, pi[("wo2", KD - 1)] + 1)
            for e in range(4):
                load_u(e, e)
            for tb in range(TB):
                for i in range(FREE[tb]):
                    if tb:
                        store_gates(tb - 1, range(3 * i, min(3 * i + 3, 8)))
                    tile(START[tb] + i)

                def gated_tiles(it, _):
                    for u in range(4):
                        tile(it * 4 + (START[tb] + FREE[tb] + u), (START[tb] + FREE[tb] + u) % 4)
                rounds(sp, GATED // 4, gated_tiles)
                for u in range(2):
                    sp.wait_ge(s_ge[u], 16 * (tb + 1))
            for i, e in enumerate(range(START[TB], NS)):
                store_gates(TB - 1, range(3 * i, min(3 * i + 3, 8)))
                tile(e)
            sp.wait_ge(s_gst, 128 * TB)
            for u in range(4):
                sp.wait_ge(s_kept[u], 16 * NS // 4)

            v2w = t_in["v"].rearrange("(w g) p n -> g p w n", w=2)
            g2w = gates.rearrange("(w g) p n -> g p w n", w=2)

            def load_group(g, half):
                at_least(sp, s_vlo, g * 2 - 2)
                sp.dma_start(VR[:, 2 * half:2 * half + 2, :], v2w[bass.ds(g, 1)].rearrange("s p w n -> p (s w) n"))\
                    .then_inc(s_v[half], 16)
                at_least(sp, s_act, g * 2 - 2)
                sp.dma_start(GR[:, 2 * half:2 * half + 2, :], g2w[bass.ds(g, 1)].rearrange("s p w n -> p (s w) n"))\
                    .then_inc(s_g[half], 16)
                at_least(sp, s_alo, g * 2 - 2)
                sp.dma_start(AF[:, 2 * half, :], kept[bass.ds(g, 1)].rearrange("s p n -> p (s n)"))\
                    .then_inc(s_h[half], 16)

            for u in range(2):
                sp.wait_ge(s_ge[u], T // 8)
            load_group(0, 0)
            load_group(1, 1)
            sp.dma_start(gf, t_in["gf"].to_broadcast([P, D])).then_inc(s_gf, 16)

            def group_loads(it, last):
                for q in range(4):
                    if not last:
                        load_u(it * 4 + (NS + q + 4), q)
                    if not last or q < 2:
                        load_group(it * 4 + (q + 2), q % 2)
            rounds(sp, NG // 4, group_loads, last=True)
            for tb in range(TB):
                sp.wait_ge(s_fin, tb + 1)
                sp.dma_start(out[tb * P:(tb + 1) * P, :], xT[:, 2 * tb:2 * tb + 2, :]
                             .rearrange("p k n -> p (k n)")).then_inc(s_out, 16)
            sp.wait_ge(s_out, 16 * TB)

        @block.gpsimd
        def _(pool):
            nc.gpsimd.memset(VA, 1.0).then_inc(s_init, 1)
            pool.wait_ge(s_init, 1)
            nc.gpsimd.memset(km1[QKD:P, :, :], 1.0).then_inc(s_init, 1)
            pool.wait_ge(s_init, 2)
            nc.gpsimd.memset(zc[:, 0:T + 2], 0.0).then_inc(s_init, 1)
            pool.wait_ge(s_O, 12)
            nc.gpsimd.memset(Q2[NOPE:QKD, :, :], 0.0).then_inc(s_init2, 1)
            pool.wait_ge(s_init2, 1)
            nc.gpsimd.memset(K2[NOPE:QKD, :, :], 0.0).then_inc(s_init2, 1)
            pool.wait_ge(s_init2, 2)
            nc.gpsimd.memset(K2[QKD:P, :, :], 1.0).then_inc(s_init2, 1)
            pool.wait_ge(s_init2, 3)
            nc.gpsimd.memset(VB, 1.0).then_inc(s_init2, 1)
            pool.wait_ge(s_init2, 4)
            nc.gpsimd.memset(Q2[NOPE:NOPE + 1, :, :], 1.0).then_inc(s_init2, 1)
            for j in range(ATT2):
                a = 12 + j
                if j == 0:
                    pool.wait_ge(s_post, post_no[("forget", 0)])
                if j >= 4:
                    pool.wait_ge(s_T, t_no[("T", a - 4, TB - 1)])
                src = zsm[j:j + 1, 2, :] if j < 8 else t_in["bias"][j - 8:j - 7, :]
                pool.dma_start(K2[NOPE:NOPE + 1, j % 4, :], src).then_inc(s_kb[j % 4], 16)
            pool.wait_ge(s_kb[3], 16 * 4)

            def low_u(e, slot):
                pool.wait_ge(s_uhi, e + 1)
                nc.gpsimd.tensor_tensor(U2[:, slot % 2, 1].rearrange("p k e -> p (k e)"), UR[:, slot, :],
                                        U2[:, slot % 2, 0].rearrange("p k e -> p (k e)").bitcast(F32),
                                        ALU.subtract).then_inc(s_ulo, 1)

            def low_v(e, slot):
                pool.wait_ge(s_vhi, e + 1)
                nc.gpsimd.tensor_tensor(V2[:, slot, 1], VR[:, slot, :], V2[:, slot, 0].bitcast(F32),
                                        ALU.subtract).then_inc(s_vlo, 1)

            low_u(0, 0)
            low_u(1, 1)
            rounds(pool, NS // 4, lambda it, _: [low_u(it * 4 + (u + 2), (u + 2) % 4) for u in range(4)])

            def low_parts(it, last):
                for q in range(4):
                    if not last or q < 2:
                        low_u(it * 4 + (NS + q + 2), (q + 2) % 4)
                    for w in range(2):
                        low_v(it * 8 + (2 * q + w), 2 * (q % 2) + w)
            rounds(pool, NG // 4, low_parts, last=True)

        @block.tensor
        def _(pe):
            mm = nc.tensor.matmul

            def need_aux(i):
                if i >= 2:
                    pe.wait_ge(s_auxfree[i % 2], i // 2)

            def proj(n):
                kind, i, loads = PROJ[n]
                if n >= 2:
                    pe.wait_ge(s_evac, n - 1)
                for L in loads:
                    pe.wait_ge(s_w[L % NW], 16 * (L // NW + 1))
                ps = pj[n % 2]
                w = ring[:, loads[0] % NW, :]

                def run(nk, m, rhs, N=T, base=0):
                    for k in range(nk):
                        last = mm(ps[0:m, 0:N], w[:, base + k * m:base + (k + 1) * m], rhs(k),
                                  start=(k == 0), stop=(k == nk - 1))
                    return last

                def normalised(phase):
                    def tile(k):
                        if k < KD - 1:
                            pe.wait_ge(s_hk, (KD - 1) * phase + k + 1)
                        else:
                            pe.wait_ge(s_norm, norm_no[("x", "x2")[phase]])
                        return hT[:, k, :]
                    return tile

                def tok(lhs, nk, chunk):
                    for k in range(nk):
                        L = loads[k // chunk]
                        last = mm(ps[:, :], lhs(k), ring[:, L % NW, (k % chunk) * T:(k % chunk + 1) * T],
                                  start=(k == 0), stop=(k == nk - 1))
                    return last

                if kind in ("lat", "conv", "gate", "qm", "r"):
                    last = run(KD, P, normalised(0) if (kind, i) == ("lat", 0) else lambda k: hT[:, k, :])
                elif kind == "kpe":
                    last = run(KD, QKD, lambda k: hT[:, k, :])
                elif kind == "uq":
                    pe.wait_ge(s_norm, norm_no["ql"])
                    last = run(QL, QKD, lambda k: lat[:, k, :])
                elif kind == "uk":
                    pe.wait_ge(s_norm, norm_no["kvl"])
                    last = run(KVL, NOPE, lambda k: lat[:, QL + k, :])
                elif kind == "uv":
                    pe.wait_ge(s_norm, norm_no["kvl"])
                    last = tok(lambda k: lat[:, QL + k, i * P:(i + 1) * P], KVL, KVL)
                elif kind == "mk":
                    pe.wait_ge(s_norm, norm_no["mem"])
                    last = run(KD, P, lambda k: memT[:, k, :], N=MEM)
                elif kind == "mv":
                    pe.wait_ge(s_norm, norm_no["mem"])
                    last = tok(lambda k: memT[:, k, i * P:(i + 1) * P], KD, 2)
                elif kind == "br":
                    b = i % 3
                    pe.wait_ge(s_post, post_no[("mgate", 3)])
                    last = run(4, P, lambda k: oT[:, 4 * b + k, :], base=KD * P)
                elif kind == "wo":
                    pe.wait_ge(s_post, post_no[("rb", 3 * KD - 1)])
                    last = run(KD, P, lambda k: yT[:, k, :])
                elif kind in ("qk2", "wf"):
                    last = run(KD, P if kind == "qk2" else 8,
                               normalised(1) if kind == "wf" else lambda k: hT[:, k, :])
                elif kind == "v2":
                    tb = i % TB
                    last = tok(lambda k: hT[:, k, tb * P:(tb + 1) * P], KD, 2)
                elif kind == "wo2":
                    def heads(k):
                        if i == 0 and k >= KD - 2:
                            pe.wait_ge(s_O, len(O_no) - 2 * (KD - 1 - k))
                        return oT[:, k, :]
                    last = run(KD, P, heads)
                else:
                    assert kind == "wq"
                    pe.wait_ge(s_norm, norm_no["h2"])
                    last = run(KD, P, lambda k: hT[:, k, :])
                last.then_inc(s_proj, 1)

            def norm(key):
                nk, width, N = norm_shape(key)
                i = auxi[("norm", key)]
                need_aux(i)
                rows = min(width, P)
                for k in range(nk):
                    j = sq0[key] + k
                    pe.wait_ge(s_sq, j + 1)
                    last = mm(ax[i % 2][0:rows, 0:N], ones[0:rows, 0:rows], sq[0:rows, j % NQ, 0:N],
                              start=(k == 0), stop=(k == nk - 1))
                    if k < nk - 1:
                        last.then_inc(s_squsd, 1)
                last.then_inc(s_aux, 1)

            def rope(h, which):
                i = auxi[("rope", h, which)]
                need_aux(i)
                pe.wait_ge(s_norm, norm_no[f"{'qk'[which]}{h}"])
                src = (qm1, km1)[which]
                mm(ax[i % 2][0:QKD, :], rot[0:QKD, 0:QKD], src[0:QKD, h % 2, :], start=True, stop=True)\
                    .then_inc(s_aux, 1)

            def operands(a):
                if a < HEADS:
                    return qm1[:, a % 2, :], km1[:, a % 2, :], QKD, QKD + 1
                if a < 12:
                    return mq[:, a - HEADS, :], mkT[:, a - HEADS, :], P, P
                return Q2[:, (a - 12) % 4, :], K2[:, (a - 12) % 4, :], NOPE + 1, QKD + 1

            def score_bank(step):
                n = tile_no[step]
                if n >= 3:
                    was = tiles[n - 3]
                    if was[0] == "S":
                        pe.wait_ge(s_max, s_no[was])
                    else:
                        pe.wait_ge(s_P, t_no[was])
                return scb[n % 3]

            def S(a, qb):
                q, k, K, _ = operands(a)
                if qb == 0:
                    if a < HEADS:
                        pe.wait_ge(s_rope, rope_no[(a, 1)])
                    elif a < 12:
                        pe.wait_ge(s_norm, norm_no[f"mk{a - HEADS}"])
                    else:
                        p = (a - 12) // 2
                        pe.wait_ge(s_cast, 6)
                        pe.wait_ge(s_init2, 5)
                        pe.wait_ge(s_evac, pi[("qk2", 2 * p + 1)] + 1)
                        pe.wait_ge(s_kb[(a - 12) % 4], 16 * ((a - 12) // 4 + 1))
                ps = score_bank(("S", a, qb))
                N = (qb + 1) * P if a >= 12 else n_keys(a) * P
                last = mm(ps[:, 0:N], q[0:K, qb * P:(qb + 1) * P], k[0:K, 0:N], start=True, stop=(a < 12))
                if 12 <= a < 20:
                    last = mm(ps[:, qb * P:N], idb, msf, start=False, stop=True)
                elif a >= 20:
                    last = mm(ps[:, 0:N], idb, msd[:, T - N:T], start=False, stop=True)
                last.then_inc(s_S, 1)

            def M(a):
                i = auxi[("M", a)]
                need_aux(i)
                pe.wait_ge(s_max, s_no[("S", a, TB - 1)])
                for qb in range(TB):
                    last = mm(ax[i % 2][0:1, qb * P:(qb + 1) * P], mx[:, 4 * (a % 2) + qb:4 * (a % 2) + qb + 1],
                              negid, start=True, stop=True)
                last.then_inc(s_aux, 1)

            def T_(a, kb):
                q, k, _, K = operands(a)
                if kb == 0:
                    i = auxi[("M", a)]
                    pe.wait_ge(s_auxfree[i % 2], i // 2 + 1)
                ps = score_bank(("T", a, kb))
                c0 = q0(a, kb)
                kk = k[0:K, kb * P:(kb + 1) * P]
                last = mm(ps[:, c0:T], kk, q[0:K, c0:T], start=True, stop=(a < HEADS))
                if HEADS <= a < 12:
                    last = mm(ps[:, :], ones[0:1, :], mrow[0:1, :], start=False, stop=True)
                elif 12 <= a < 20:
                    last = mm(ps[:, c0:c0 + P], idb, mtf, start=False, stop=True)
                elif a >= 20:
                    last = mm(ps[:, c0:T], idb, mtd[:, 0:T - c0], start=False, stop=True)
                last.then_inc(s_T, 1)

            def PV(a, kb):
                if a >= 20:
                    pe.wait_ge(s_Pc, cnt_no[(a, kb)])
                else:
                    pe.wait_ge(s_P, t_no[("T", a, kb)])
                if kb == 0 and a > 0:
                    pe.wait_ge(s_O, O_no[a] - 1)
                c0 = q0(a, kb)
                rhs = PT[:, kb, c0:T]
                nk = n_keys(a)
                if a < HEADS:
                    v = VA[:, kb, a, :]
                elif a < 12:
                    v = mv[:, kb, (a - HEADS) * P:(a - HEADS + 1) * P]
                else:
                    v = (VA if a < 20 else VB)[:, kb, (a - 12) % 8, :]
                if kb == 0 and a in (0, HEADS, 12, 20):
                    last_v = {0: ("uv", TB - 1), HEADS: ("mv", MB - 1), 12: ("v2", TB - 1), 20: ("v2", 2 * TB - 1)}[a]
                    pe.wait_ge(s_evac, pi[last_v] + 1)
                if HEADS <= a < 12:
                    i = auxi[("den", a)]
                    if kb == 0:
                        need_aux(i)
                    den = mm(ax[i % 2][:, :], ones, rhs, start=(kb == 0), stop=(kb == nk - 1))
                    if kb == nk - 1:
                        den.then_inc(s_aux, 1)
                mm(ob[:, c0:T], v, rhs, start=(kb == 0), stop=(kb == nk - 1)).then_inc(s_PV, 1)

            pe.wait_ge(s_const, 16)
            for s in STEPS:
                if s[0] == "proj":
                    proj(s[1])
                elif s[0] == "norm":
                    norm(s[1])
                elif s[0] == "rope":
                    rope(s[1], s[2])
                elif s[0] == "S":
                    S(s[1], s[2])
                elif s[0] == "M":
                    M(s[1])
                elif s[0] == "T":
                    T_(s[1], s[2])
                elif s[0] == "PV":
                    PV(s[1], s[2])
                elif s[0] == "keys":
                    i = s[1]
                    if i == 0:
                        pe.wait_ge(s_sk, 16)
                    pe.wait_ge(s_evac, pi[("wq", i)] + 1)
                    if i >= 4:
                        pe.wait_ge(s_qe, i - 3)
                    for tb in range(TB):
                        last = mm(bank[3 + i % 4][:, tb * P:(tb + 1) * P], pq[:, i % 4, tb * P:(tb + 1) * P],
                                  sk[:, i, :], start=True, stop=True)
                    last.then_inc(s_qs, 1)

            pe.wait_ge(s_qe, 2 * PEER_HEADS)
            pe.wait_ge(s_evac, len(PROJ))
            for tb in range(TB):
                for dh in range(2):
                    for k in range(4):
                        last = nc.tensor.transpose(bank[2 * tb + dh][:, k * P:(k + 1) * P],
                                                   xT[:, 4 * dh + k, tb * P:(tb + 1) * P], ident)
            last.then_inc(s_hx, 1)
            pe.wait_ge(s_hxc, 8)

            def lists_out(tb):
                pe.wait_ge(s_tk, tb + 1)
                if tb >= 1:
                    pe.wait_ge(s_ltc, tb)
                for w in range(3):
                    last = nc.tensor.transpose(bank[4][:, w * P:(w + 1) * P], sel[:, w, :], ident)
                last.then_inc(s_lt, 1)

            def gate_group(n, u):
                pe.wait_ge(s_oh, n * 2 + (u + 1))
                at_least(pe, s_ge[u], n)
                for k in range(4):
                    last = mm(bank[2 + u][:, k * P:(k + 1) * P], ohring[:, u, 1, k, :], ohring[:, u, 0, k, :],
                              start=True, stop=True)
                last.then_inc(s_gm[u], 1)

            def hidden(e, slot, between=None):
                pe.wait_ge(s_ulo, e + 1)
                at_least(pe, s_gelu, e - 1)
                for k in range(KD):
                    if between and k % 2 == 0:
                        between(k // 2)
                    for w, x in ((0, hh), (0, hl), (1, hh)):
                        last = mm(bank[slot % 2][:, :], U2[:, slot % 2, w, k, :], x[:, k, :],
                                  start=(k == 0 and x is hh and w == 0), stop=(k == KD - 1 and w == 1))
                last.then_inc(s_hid, 1)

            def outputs(g, half):
                pe.wait_ge(s_vlo, g * 2 + 2)
                pe.wait_ge(s_alo, g * 2 + 2)
                for u in range(8):
                    tb, dh = u // 2, u % 2
                    at_least(pe, s_ea, g * 8 + (u - 3))
                    for e in (2 * half, 2 * half + 1):
                        for wa, wv in ((0, 0), (0, 1), (1, 0)):
                            last = mm(bank[2 + u % 4][:, :], A2[:, e, wa, tb * P:(tb + 1) * P],
                                      V2[:, e, wv, dh * T:(dh + 1) * T],
                                      start=(e == 2 * half and wa == wv), stop=(e > 2 * half and wa == 1))
                    last.then_inc(s_eo, 1)

            pe.wait_ge(s_hl, KD)
            for tb in range(TB):
                for e in range(START[tb], START[tb] + FREE[tb]):
                    hidden(e, e)
                lists_out(tb)

                def with_gates(it, _):
                    for u in range(4):
                        hidden(it * 4 + (START[tb] + FREE[tb] + u), START[tb] + FREE[tb] + u,
                               lambda k: gate_group(it * 8 + (16 * tb + 2 * u + k // 2), k % 2))
                rounds(pe, GATED // 4, with_gates, first=tb == 0)
            for e in range(START[TB], NS):
                hidden(e, e)
            for u in range(2):
                pe.wait_ge(s_ge[u], T // 8)

            def group_products(it, first):
                for q in range(4):
                    hidden(it * 4 + (NS + q), q)
                    if not first or q:
                        outputs(it * 4 + (q - 1), (q - 1) % 2)
            group_products(0, True)
            with pe.Fori(1, NG // 4) as it:
                group_products(it, False)
            outputs(NG - 1, 1)

        @block.scalar
        def _(act):
            A = nc.scalar.activation
            chain = [0]

            def link(ins):
                chain[0] += 1
                ins.then_inc(s_rc, 1)
                act.wait_ge(s_rc, chain[0])

            def cast():
              act.wait_ge(s_raw, 16)
              act.wait_ge(s_const, 16)
              for dst, name, n in ((msf, "msf", 128), (mtf, "mtf", 128), (msd, "msd", 512), (mtd, "mtd", 512),
                                 (cnt, "cnt", 512)):
                c = CN[name] - NKEEP
                nc.scalar.copy(dst, craw[:, c:c + n]).then_inc(s_cast, 1)
              nc.scalar.copy(idb, ident).then_inc(s_cast, 1)

            def evac(n):
                kind, i, _ = PROJ[n]
                act.wait_ge(s_proj, n + 1)
                ps = pj[n % 2]
                if n in TEMPS:
                    j = TEMPS[n]
                    dst = ebuf[:, j % NE, :]
                    if j >= NE:
                        act.wait_ge(s_post, POST_OF[j - NE])
                    if kind == "conv" and i == 0:
                        act.wait_ge(s_tab, 1)
                    if kind == "r" and i == 0:
                        act.wait_ge(s_par, 16)
                    if kind == "gate" or (kind == "conv" and i % 4 == 3):
                        A(dst, ps[:, :], ACT.Silu).then_inc(s_evac, 1)
                    elif kind == "r":
                        A(dst, ps[:, :], ACT.Sigmoid, bias=col("bg", i)).then_inc(s_evac, 1)
                    elif kind == "wf":
                        A(dst[0:8, :], ps[0:8, :], ACT.Identity, bias=col("bf", 0, 0, 8)).then_inc(s_evac, 1)
                    else:
                        nc.scalar.copy(dst, ps[:, :]).then_inc(s_evac, 1)
                elif kind == "lat":
                    nc.scalar.copy(lat[:, i, :], ps[:, :]).then_inc(s_evac, 1)
                elif kind == "kpe":
                    nc.scalar.copy(lat[NOPE:QKD, 5, :], ps[NOPE:QKD, :]).then_inc(s_evac, 1)
                elif kind == "uq":
                    nc.scalar.copy(qm1[0:QKD, i % 2, :], ps[0:QKD, :]).then_inc(s_evac, 1)
                elif kind == "uk":
                    if i == 0:
                        act.wait_ge(s_evac, pi[("kpe", 0)] + 1)
                    nc.scalar.copy(km1[NOPE:QKD, i % 2, :], lat[NOPE:QKD, 5, :])
                    nc.scalar.copy(km1[0:NOPE, i % 2, :], ps[0:NOPE, :]).then_inc(s_evac, 1)
                elif kind in ("uv", "v2"):
                    if kind == "uv":
                        act.wait_ge(s_init, 1)
                    if kind == "v2" and i >= TB:
                        act.wait_ge(s_init2, 5)
                    V = VB if i >= TB else VA
                    src = ps[:, :].rearrange("p (h d) -> p h d", h=HEADS)
                    nc.scalar.copy(V[:, i % TB, 0:HEADS:2, 0:DH], src[:, 0:HEADS:2, :])
                    nc.scalar.copy(V[:, i % TB, 1:HEADS:2, DH:P], src[:, 1:HEADS:2, :]).then_inc(s_evac, 1)
                elif kind == "gate":
                    A(memgate[:, i - 4, :], ps[:, :], ACT.Silu).then_inc(s_evac, 1)
                elif kind == "qm":
                    nc.scalar.copy(mq[:, i, :], ps[:, :]).then_inc(s_evac, 1)
                elif kind == "mk":
                    nc.scalar.copy(mkT[:, i, :], ps[:, 0:MEM]).then_inc(s_evac, 1)
                elif kind == "mv":
                    nc.scalar.copy(mv[:, i, :], ps[:, :]).then_inc(s_evac, 1)
                elif kind == "qk2":
                    p, s = i // 2, i % 2
                    if i == 0:
                        act.wait_ge(s_init2, 5)
                    dst = (Q2, K2)[s]
                    scale = (DH ** -0.5, 1.0)[s]
                    for u in range(2):
                        ins = A(dst[0:DH, (2 * p + u) % 4, :], ps[u * DH:(u + 1) * DH, :], ACT.Copy, scale=scale)
                    ins.then_inc(s_evac, 1)
                else:
                    assert kind == "wq"
                    if i >= 4:
                        act.wait_ge(s_qs, i - 3)
                    nc.scalar.copy(pq[:, i % 4, :], ps[:, :]).then_inc(s_evac, 1)

            def square_summed(j):
                key = max((k for k in sq0 if sq0[k] <= j), key=lambda k: sq0[k])
                if j == sq0[key] + norm_shape(key)[0] - 1:
                    act.wait_ge(s_aux, auxi[("norm", key)] + 1)
                else:
                    act.wait_ge(s_squsd, j + 1 - sum(1 for k in sq0 if sq0[k] + norm_shape(k)[0] - 1 <= j))

            def squares(key):
                nk, width, N = norm_shape(key)
                rows = min(width, P)
                for k in range(nk):
                    j = sq0[key] + k
                    if key == "x":
                        act.wait_ge(s_x, 16)
                        src = xT[:, k, :]
                    elif key == "x2":
                        act.wait_ge(s_post, post_no[("res", k)])
                        src = xT[:, k, :]
                    elif key == "h2":
                        act.wait_ge(s_post, post_no[("res2", k)])
                        src = xT[:, k, :]
                    elif key == "ql":
                        act.wait_ge(s_evac, pi[("lat", k)] + 1)
                        src = lat[:, k, :]
                    elif key == "kvl":
                        act.wait_ge(s_evac, pi[("lat", QL + k)] + 1)
                        src = lat[:, QL + k, :]
                    elif key == "mem":
                        act.wait_ge(s_mem, 16)
                        src = memT[:, k, :]
                    elif key.startswith("mq"):
                        act.wait_ge(s_evac, pi[("qm", int(key[2:]))] + 1)
                        src = mq[:, int(key[2:]), :]
                    elif key.startswith("mk"):
                        act.wait_ge(s_evac, pi[("mk", int(key[2:]))] + 1)
                        src = mkT[:, int(key[2:]), :]
                    else:
                        h = int(key[1:])
                        act.wait_ge(s_evac, pi[("u" + key[0], h)] + 1)
                        src = (qm1 if key[0] == "q" else km1)[0:QKD, h % 2, :]
                    if j >= NQ:
                        square_summed(j - NQ)
                    A(sq[0:rows, j % NQ, 0:N], src, ACT.Square, scale=width ** -0.5).then_inc(s_sq, 1)

            def norm(key):
                nk, width, N = norm_shape(key)
                rows = min(width, P)
                if ("sq", key) not in STEPS:
                    squares(key)
                i, j = auxi[("norm", key)], norm_no[key]
                act.wait_ge(s_aux, i + 1)
                if j > 2:
                    act.wait_ge(s_norm, j - 2)
                r = rs[0:rows, j % 2, 0:N]
                if key == "x":
                    act.wait_ge(s_par, 16)
                A(r, ax[i % 2][0:rows, 0:N], ACT.Ln, bias=col("eps", 0, 0, rows)).then_inc(s_auxfree[i % 2], 1)
                act.wait_ge(s_auxfree[i % 2], i // 2 + 1)
                A(r, r, ACT.Exp, scale=-0.5).then_inc(s_rs, 1)

            def rope_tables():
                act.wait_ge(s_cos, 1)
                A(sinT[NOPE:QKD, :], rtmp[NOPE:QKD, :], ACT.Sin).then_inc(s_tab, 1)
                act.wait_ge(s_cos, 2)
                A(cosT[NOPE:QKD, :], cosT[NOPE:QKD, :], ACT.Sin).then_inc(s_tab, 1)

            def M(a):
                i = auxi[("M", a)]
                act.wait_ge(s_aux, i + 1)
                if a == 0:
                    act.wait_ge(s_init, 2)
                if a < HEADS:
                    dst = qm1[QKD:QKD + 1, a % 2, :]
                elif a < 12:
                    dst = mrow[0:1, :]
                else:
                    dst = Q2[QKD:QKD + 1, (a - 12) % 4, :]
                nc.scalar.copy(dst, ax[i % 2][0:1, :]).then_inc(s_auxfree[i % 2], 1)

            def T_(a, kb):
                act.wait_ge(s_T, t_no[("T", a, kb)])
                if a > 0:
                    act.wait_ge(s_PV, pv_no[(a - 1, min(kb, n_keys(a - 1) - 1))])
                c0 = q0(a, kb)
                scale = QKD ** -0.5 if a < HEADS else P ** -0.5 if a < 12 else 1.0
                n = tile_no[("T", a, kb)]
                A(PT[:, kb, c0:T], scb[n % 3][:, c0:T], ACT.Exp, scale=scale).then_inc(s_P, 1)

            def forget(n):
                act.wait_ge(s_fmag, 1)
                link(A(zsm[0:8, 1, :], zsm[0:8, 1, :], ACT.Exp))
                A(zsm[0:8, 1, :], zsm[0:8, 1, :], ACT.Ln, bias=1.0).then_inc(s_fch, 1)

            for s in STEPS:
                if s[0] == "proj":
                    evac(s[1])
                elif s[0] == "sq":
                    squares(s[1])
                elif s[0] == "norm":
                    norm(s[1])
                elif s[0] == "rope_tables":
                    rope_tables()
                elif s[0] == "cast":
                    cast()
                elif s[0] == "M":
                    M(s[1])
                elif s[0] == "T":
                    T_(s[1], s[2])
                elif s[0] == "post" and s[1] == "forget":
                    forget(s[3][0])
                elif s[0] == "high_h":
                    act.wait_ge(s_norm, norm_no["h2"])
                    for k in range(KD):
                        nc.scalar.copy(hh[:, k, :], hT[:, k, :]).then_inc(s_hh, 1)
                elif s[0] == "keys":
                    i = s[1]
                    act.wait_ge(s_qs, i + 1)
                    if i >= 4:
                        act.wait_ge(s_half, i - 3)
                    nc.scalar.copy(sc[:, i % 4, :], bank[3 + i % 4][:, :]).then_inc(s_qe, 1)

            act.wait_ge(s_hx, 1)
            for b in range(8):
                nc.scalar.copy(xT[:, b, :], bank[b][:, :]).then_inc(s_hxc, 1)

            def high_u(e, slot):
                act.wait_ge(s_u[slot], (e - slot) * 4 + 16)
                at_least(act, s_hid, e - 1)
                nc.scalar.copy(U2[:, slot % 2, 0].rearrange("p k e -> p (k e)"), UR[:, slot, :]).then_inc(s_uhi, 1)

            def kept_tile(e, slot):
                act.wait_ge(s_hid, e + 1)
                at_least(act, s_kept[slot], (e - slot) * 4)
                A(AF[:, slot, :], bank[slot % 2][:, :], ACT.Gelu).then_inc(s_gelu, 1)
                high_u(e + 2, (slot + 2) % 4)

            def copy_group(tb, n, u, t):
                act.wait_ge(s_gm[u], n + 1)
                nc.scalar.copy(stage[:, :, bass.ds(t, 4)].rearrange("p i t -> p t i"),
                               bank[2 + u][:, :].rearrange("p (t i) -> p t i", t=4)).then_inc(s_ge[u], 1)

            high_u(0, 0)
            high_u(1, 1)
            for tb in range(TB):
                for i in range(FREE[tb]):
                    if i == 4:
                        act.wait_ge(s_sm, tb + 1)
                        A(ee, ee, ACT.Exp).then_inc(s_ex, 1)
                    kept_tile(START[tb] + i, (START[tb] + i) % 4)
                act.wait_ge(s_lt, tb + 1)
                nc.scalar.copy(lists[:, :, tb * P:(tb + 1) * P],
                               bank[4][:, 0:3 * P].rearrange("p (w t) -> p w t", w=3)).then_inc(s_ltc, 1)
                if tb:
                    act.wait_ge(s_gst, 128 * tb)

                def with_gates(it, _):
                    for u in range(4):
                        for k in range(4):
                            copy_group(tb, it * 8 + (16 * tb + 2 * u + k // 2), k % 2, it * 64 + (16 * u + 4 * k))
                        kept_tile(it * 4 + (START[tb] + FREE[tb] + u), (START[tb] + FREE[tb] + u) % 4)
                rounds(act, GATED // 4, with_gates, first=tb == 0)
            for e in range(START[TB], NS):
                kept_tile(e, e % 4)

            for u in range(4):
                act.wait_ge(s_kept[u], 16 * NS // 4)
            act.wait_ge(s_gst, 128 * TB)

            def expert_groups(it, last):
                for q in range(4):
                    g, half = it * 4 + q, q % 2
                    act.wait_ge(s_v[half], it * 32 + (16 * (q // 2) + 16))
                    at_least(act, s_eo, g * 8 - 8)
                    for w in range(2):
                        nc.scalar.copy(V2[:, 2 * half + w, 0], VR[:, 2 * half + w, :]).then_inc(s_vhi, 1)
                    act.wait_ge(s_act, g * 2 + 1)
                    nc.scalar.copy(A2[:, 2 * half, 0], AF[:, 2 * half, :]).then_inc(s_ahi, 1)
                    act.wait_ge(s_hid, g + (NS + 1))
                    at_least(act, s_alo, g * 2 - 2)
                    A(AF[:, 2 * half + 1, :], bank[q % 2][:, :], ACT.Gelu).then_inc(s_gelu, 1)
                    if not last or q < 2:
                        high_u(g + (NS + 2), (q + 2) % 4)
                    act.wait_ge(s_act, g * 2 + 2)
                    nc.scalar.copy(A2[:, 2 * half + 1, 0], AF[:, 2 * half + 1, :]).then_inc(s_ahi, 1)
            rounds(act, NG // 4, expert_groups, first=True, last=True)
            for tb in range(TB):
                act.wait_ge(s_ea, NG * 8)
                A(fsq, xT[:, 2 * tb:2 * tb + 2, :].rearrange("p k n -> p (k n)"), ACT.Square,
                  scale=D ** -0.5, accum_out=fss[:, tb:tb + 1]).then_inc(s_fsq, 1)
                act.wait_ge(s_fsq, 3 * tb + 1)
                A(fss[:, 4 + tb:5 + tb], fss[:, tb:tb + 1], ACT.Ln, bias=col("eps")).then_inc(s_fsq, 1)
                act.wait_ge(s_fsq, 3 * tb + 2)
                A(fss[:, 8 + tb:9 + tb], fss[:, 4 + tb:5 + tb], ACT.Exp, scale=-0.5).then_inc(s_fsq, 1)

        @block.vector
        def _(dve):
            V = nc.vector
            chain = [0]

            def link(ins):
                chain[0] += 1
                ins.then_inc(s_d, 1)
                dve.wait_ge(s_d, chain[0])

            ended = {}

            def end(ins, s, name):
                ended[name] = (s, ended.pop(name, (s, 0))[1] + 1)
                ins.then_inc(s, 1)

            def settle():
                if ended:
                    dve.wait_ge(*list(ended.values())[-1])

            dve.wait_ge(s_par, 16)
            dve.wait_ge(s_const, 16)

            def norm(key):
                nk, width, N = norm_shape(key)
                rows = min(width, P)
                j = norm_no[key]
                dve.wait_ge(s_rs, j)
                r = rs[0:rows, j % 2, 0:N]
                for k in range(nk):
                    if key == "x":
                        dst, src, g = hT[:, k, :], xT[:, k, :], col("norm", k)
                    elif key in ("x2", "h2"):
                        dst, src, g = hT[:, k, :], xT[:, k, :], col({"x2": "norm1", "h2": "norm2"}[key], k)
                    elif key == "ql":
                        dst = src = lat[:, k, :]
                        g = col("qn", k)
                    elif key == "kvl":
                        dst = src = lat[:, QL + k, :]
                        g = col("kvn", k)
                    elif key == "mem":
                        dst = src = memT[:, k, :]
                        g = col("memn", k)
                    elif key.startswith("mq"):
                        dst = src = mq[:, int(key[2:]), :]
                        g = col("mq")
                    elif key.startswith("mk"):
                        dst = src = mkT[:, int(key[2:]), :]
                        g = col("mk")
                    else:
                        dst = src = (qm1 if key[0] == "q" else km1)[0:QKD, int(key[1:]) % 2, :]
                        g = col(key[0] + "h", 0, 0, QKD)
                    ins = V.scalar_tensor_tensor(dst, src, g, r, ALU.mult, ALU.mult)
                    if key in ("x", "x2") and k < KD - 1:
                        ins.then_inc(s_hk, 1)
                end(ins, s_norm, "s_norm")

            def rope_tables():
                R = slice(NOPE, QKD)
                dve.wait_ge(s_pos, 16)
                dve.wait_ge(s_cast, 6)
                ang, kk, t1, t2 = zsm[R, 0, :], zsm[R, 1, :], rtmp[R, :], cosT[R, :]
                magic = 12582912.0
                c1 = 6.28125
                c2 = float(np.float32(np.floor((2 * np.pi - c1) * 2 ** 21) / 2 ** 21))
                c3 = float(2 * np.pi - c1 - c2)
                link(V.tensor_copy(ang, pos_i[R, :]))
                link(V.tensor_scalar(ang, ang, col("invf", 0, NOPE, QKD), None, ALU.mult))
                for which, dst in ((0, t1), (1, t2)):
                    if which:
                        link(V.tensor_scalar(kk, ang, 1.0 / (2 * np.pi), 0.25, ALU.mult, ALU.add))
                    else:
                        link(V.tensor_scalar(kk, ang, 1.0 / (2 * np.pi), None, ALU.mult))
                    link(V.tensor_scalar(kk, kk, magic, None, ALU.add))
                    link(V.tensor_scalar(kk, kk, magic, None, ALU.subtract))
                    link(V.scalar_tensor_tensor(dst, kk, -c1, ang, ALU.mult, ALU.add))
                    link(V.scalar_tensor_tensor(dst, kk, -c2, dst, ALU.mult, ALU.add))
                    link(V.scalar_tensor_tensor(dst, kk, -c3, dst, ALU.mult, ALU.add))
                    if which:
                        link(V.tensor_scalar(dst, dst, np.pi / 2, None, ALU.add))
                    V.tensor_scalar(dst, dst, 3.1415925, -3.1415925, ALU.min, ALU.max).then_inc(s_cos, 1)

            def rope(h, which):
                i = auxi[("rope", h, which)]
                R = slice(NOPE, QKD)
                x = (qm1, km1)[which][R, h % 2, :]
                dve.wait_ge(s_tab, 2)
                dve.wait_ge(s_aux, i + 1)
                V.tensor_tensor(rtmp[R, :], ax[i % 2][R, :], sinT[R, :], ALU.mult).then_inc(s_auxfree[i % 2], 1)
                link(V.tensor_tensor(x, x, cosT[R, :], ALU.mult))
                end(V.tensor_tensor(x, x, rtmp[R, :], ALU.add), s_rope, "s_rope")

            def S(a, qb):
                n = tile_no[("S", a, qb)]
                dve.wait_ge(s_S, s_no[("S", a, qb)])
                N = (qb + 1) * P if a >= 12 else n_keys(a) * P
                c = 4 * (a % 2) + qb
                V.tensor_reduce(mx[:, c:c + 1], scb[n % 3][:, 0:N], AX.X, ALU.max).then_inc(s_max, 1)

            def count(a, kb):
                dve.wait_ge(s_P, t_no[("T", a, kb)])
                c0 = q0(a, kb)
                V.tensor_tensor(PT[:, kb, c0:T], PT[:, kb, c0:T], cnt[:, 0:T - c0], ALU.mult).then_inc(s_Pc, 1)

            def O(a):
                dve.wait_ge(s_PV, pv_no[(a, n_keys(a) - 1)])
                if HEADS <= a < 12:
                    i = auxi[("den", a)]
                    V.reciprocal(dtmp, ax[i % 2][:, :]).then_inc(s_auxfree[i % 2], 1)
                    dve.wait_ge(s_auxfree[i % 2], i // 2 + 1)
                    end(V.tensor_tensor(oT[:, a, :], ob[:, :], dtmp, ALU.mult), s_O, "s_O")
                    return
                h = a if a < HEADS else a - 12
                r0 = DH * (h % 2)
                d0 = DH - r0
                link(V.reciprocal(dtmp[r0:r0 + DH, :], ob[d0:d0 + DH, :]))
                end(V.tensor_tensor(oT[r0:r0 + DH, h // 2, :], ob[r0:r0 + DH, :], dtmp[r0:r0 + DH, :],
                                ALU.mult), s_O, "s_O")

            def post(kind, i, ns):
                for n in ns:
                    dve.wait_ge(s_evac, n + 1)
                e = [ebuf[:, TEMPS[n] % NE, :] for n in ns]
                if kind == "conv":
                    c, u, b, g = e
                    if i == 0:
                        dve.wait_ge(s_init, 3)
                    z, w = zc, cwork
                    link(V.tensor_tensor(z[:, 1:T + 1], c, u, ALU.mult))
                    link(V.tensor_scalar(w[:, 0, :], z[:, 0:T], col("cw", i), None, ALU.mult))
                    link(V.scalar_tensor_tensor(w[:, 0, :], z[:, 1:T + 1], col("cw", 4 + i), w[:, 0, :],
                                                ALU.mult, ALU.add))
                    link(V.scalar_tensor_tensor(w[:, 0, :], z[:, 2:T + 2], col("cw", 8 + i), w[:, 0, :],
                                                ALU.mult, ALU.add))
                    link(V.scalar_tensor_tensor(w[:, 0, :], w[:, 0, :], col("cb", i), b, ALU.add, ALU.mult))
                    end(V.tensor_tensor(oT[:, 4 + i, :], w[:, 0, :], g, ALU.mult), s_post, "s_post")
                elif kind == "gate":
                    dve.wait_ge(s_O, HEADS)
                    end(V.tensor_tensor(oT[:, i, :], oT[:, i, :], e[0], ALU.mult), s_post, "s_post")
                elif kind == "mgate":
                    dve.wait_ge(s_O, HEADS + MEM_HEADS)
                    dve.wait_ge(s_evac, pi[("gate", 7)] + 1)
                    end(V.tensor_tensor(oT[:, 8 + i, :], oT[:, 8 + i, :], memgate[:, i, :], ALU.mult), s_post, "s_post")
                elif kind == "rb":
                    f, b = i // 3, i % 3
                    if b == 0:
                        end(V.tensor_tensor(yT[:, f, :], e[0], e[1], ALU.mult), s_post, "s_post")
                    else:
                        link(V.tensor_tensor(dtmp, e[0], e[1], ALU.mult))
                        end(V.tensor_tensor(yT[:, f, :], yT[:, f, :], dtmp, ALU.add), s_post, "s_post")
                    dve.wait_ge(s_post, post_no[("rb", i)])
                elif kind in ("res", "res2"):
                    end(V.tensor_tensor(xT[:, i, :], xT[:, i, :], e[0], ALU.add), s_post, "s_post")
                else:
                    assert kind == "forget"
                    z = e[0][0:8, :]
                    z0, z1, z2 = zsm[0:8, 0, :], zsm[0:8, 1, :], zsm[0:8, 2, :]
                    link(V.tensor_scalar(z0, z, 0.0, None, ALU.max))
                    V.scalar_tensor_tensor(z1, z, 0.0, z0, ALU.min, ALU.subtract).then_inc(s_fmag, 1)
                    dve.wait_ge(s_fch, 1)
                    link(V.scalar_tensor_tensor(z0, z, 0.0, z1, ALU.min, ALU.subtract))
                    link(V.tensor_scalar(z0, z0, -1.0, None, ALU.mult))
                    link(V.memset(z1, 1.0))
                    end(V.tensor_tensor_scan(z2, z1, z0, 0.0, ALU.mult, ALU.add), s_post, "s_post")

            def sorted_half(i):
                dve.wait_ge(s_qe, i + 1)
                b = sc[:, i % 4, :].rearrange("p (t k) -> p t k", t=TB)
                for tb in range(TB):
                    ins = V.max(tva[:, tb, i, 0:8], b[:, tb, :])
                link(ins)
                for tb in range(TB):
                    ins = V.max_index(tia[:, tb, i, 0:8], tva[:, tb, i, 0:8], b[:, tb, :])
                link(ins)
                for tb in range(TB):
                    ins = V.match_replace(b[:, tb, :], tva[:, tb, i, 0:8], b[:, tb, :], -BIG)
                link(ins)
                for tb in range(TB):
                    ins = V.max(tva[:, tb, i, 8:16], b[:, tb, :])
                link(ins)
                for tb in range(TB):
                    ins = V.max_index(tia[:, tb, i, 8:16], tva[:, tb, i, 8:16], b[:, tb, :])
                end(ins, s_half, "s_half")

            for s in STEPS:
                if s[0] in ("norm", "rope", "O", "post", "keys"):
                    settle()
                if s[0] == "norm":
                    norm(s[1])
                elif s[0] == "rope_tables":
                    rope_tables()
                elif s[0] == "rope":
                    rope(s[1], s[2])
                elif s[0] == "S":
                    S(s[1], s[2])
                elif s[0] == "T" and s[1] >= 20:
                    count(s[1], s[2])
                elif s[0] == "O":
                    O(s[1])
                elif s[0] == "post":
                    post(s[1], s[2], s[3])
                elif s[0] == "keys":
                    sorted_half(s[1])

            for k in range(KD):
                dve.wait_ge(s_hh, k + 1)
                dve.wait_ge(s_proj, len(PROJ))
                V.tensor_tensor(hl[:, k, :], hT[:, k, :], hh[:, k, :].bitcast(F32), ALU.subtract).then_inc(s_hl, 1)

            def retrieve(tb):
                tv, ti = tva[:, tb], tia[:, tb]
                tvh = tv.rearrange("p (h w) k -> p h w k", w=2)
                c4 = cand.rearrange("p (h a b) -> p h a b", h=8, a=16)
                ch = cand.rearrange("p (h n) -> p h n", h=8)
                link(V.tensor_tensor(c4, tvh[:, :, 0, :].unsqueeze(3).to_broadcast([P, 8, 16, 16]),
                                     tvh[:, :, 1, :].unsqueeze(2).to_broadcast([P, 8, 16, 16]), ALU.add))
                link(V.tensor_copy(tif, ti.rearrange("p h k -> p (h k)")))
                for h in range(8):
                    ins = V.max(cs[:, h, 0:8], ch[:, h, :])
                link(ins)
                for h in range(8):
                    ins = V.max_index(ci[:, h, 0:8], cs[:, h, 0:8], ch[:, h, :])
                link(ins)
                for h in range(8):
                    ins = V.match_replace(ch[:, h, :], cs[:, h, 0:8], ch[:, h, :], -BIG)
                link(ins)
                for h in range(8):
                    ins = V.max(cs[:, h, 8:16], ch[:, h, :])
                link(ins)
                for h in range(8):
                    ins = V.max_index(ci[:, h, 8:16], cs[:, h, 8:16], ch[:, h, :])
                link(ins)
                e3 = ee.rearrange("p (h k) -> p h k", h=8)
                if tb >= 1:
                    dve.wait_ge(s_lt, tb)
                V.tensor_tensor(e3, cs, cs[:, :, 0:1].to_broadcast([P, 8, 16]), ALU.subtract).then_inc(s_sm, 1)
                cif = ci.rearrange("p h k -> p (h k)")
                for w in range(2):
                    if w == 0:
                        link(V.tensor_scalar(ca, cif, 4, None, ALU.logical_shift_right))
                    else:
                        link(V.tensor_scalar(ca, cif, 15, None, ALU.bitwise_and))
                    link(V.tensor_copy(cbf[:, w, :], ca))
                    q3 = eq.rearrange("p (r m) -> p r m", m=16)
                    q4 = eq.rearrange("p (h k m) -> p h k m", h=8, k=16)
                    tf = tif.rearrange("p (h w m) -> p h w m", h=8, w=2)[:, :, w, :]
                    link(V.tensor_tensor(q3, cbf[:, w, :].unsqueeze(2).to_broadcast([P, P, 16]),
                                         iota16.unsqueeze(1).to_broadcast([P, P, 16]), ALU.is_equal))
                    link(V.tensor_tensor(q4, q4, tf.unsqueeze(2).to_broadcast([P, 8, 16, 16]), ALU.mult))
                    link(V.tensor_reduce(sel[:, w, :], q3, AX.X, ALU.add))
                dve.wait_ge(s_ex, tb + 1)
                link(V.tensor_reduce(es[:, 0:8], e3, AX.X, ALU.add))
                link(V.reciprocal(es[:, 8:16], es[:, 0:8]))
                V.tensor_tensor(sel[:, 2, :].rearrange("p (h k) -> p h k", h=8), e3,
                                es[:, 8:16].unsqueeze(2).to_broadcast([P, 8, 16]), ALU.mult).then_inc(s_tk, 1)

            def onehots(n, u, t):
                at_least(dve, s_gm[u], n)
                for k in range(4):
                    V.tensor_scalar(ohring[:, u, 0, k, :], iota, lists[:, 0, bass.ds(t + k, 1)],
                                    lists[:, 2, bass.ds(t + k, 1)], ALU.is_equal, ALU.mult)
                    ins = V.tensor_scalar(ohring[:, u, 1, k, :], iota, lists[:, 1, bass.ds(t + k, 1)], None,
                                          ALU.is_equal)
                ins.then_inc(s_oh, 1)

            for tb in range(TB):
                retrieve(tb)
                dve.wait_ge(s_ltc, tb + 1)
                rounds(dve, P // 8, lambda it, _: [
                    onehots(it + 16 * tb, u, it * 8 + (P * tb + 4 * u)) for u in range(2)], first=tb == 0)

            def gated(g, half, it, q):
                for w in range(2):
                    slot = 2 * half + w
                    if w == 0:
                        dve.wait_ge(s_g[half], it * 32 + (16 * (q // 2) + 16))
                        dve.wait_ge(s_h[half], it * 32 + (16 * (q // 2) + 16))
                    else:
                        dve.wait_ge(s_gelu, g + (NS + 1))
                    V.tensor_tensor(AF[:, slot, :], AF[:, slot, :], GR[:, slot, :], ALU.mult).then_inc(s_act, 1)
                    dve.wait_ge(s_ahi, g * 2 + (w + 1))
                    V.tensor_tensor(A2[:, slot, 1], AF[:, slot, :], A2[:, slot, 0].bitcast(F32), ALU.subtract)\
                        .then_inc(s_alo, 1)

            def add_outputs(g):
                for u in range(8):
                    dve.wait_ge(s_eo, g * 8 + (u + 1))
                    V.tensor_tensor(xT[:, u, :], xT[:, u, :], bank[2 + u % 4][:, :], ALU.add).then_inc(s_ea, 1)

            dve.wait_ge(s_hxc, 8)

            def expert_groups(it, first):
                for q in range(4):
                    gated(it * 4 + q, q % 2, it, q)
                    if not first or q:
                        add_outputs(it * 4 + (q - 1))
            expert_groups(0, True)
            with dve.Fori(1, NG // 4) as it:
                expert_groups(it, False)
            add_outputs(NG - 1)
            dve.wait_ge(s_gf, 16)
            for tb in range(TB):
                dve.wait_ge(s_fsq, 3 * (tb + 1))
                row = xT[:, 2 * tb:2 * tb + 2, :].rearrange("p k n -> p (k n)")
                V.scalar_tensor_tensor(row, row, fss[:, 8 + tb:9 + tb], gf, ALU.mult, ALU.mult).then_inc(s_fin, 1)


def _tiles(np_, w, cols_per_tile):
    K, F = w.shape
    t = w.reshape(K // 128, 128, F // cols_per_tile, cols_per_tile).transpose(2, 1, 0, 3)
    return np_.ascontiguousarray(t).reshape(F // cols_per_tile, 128, -1)


def _rows(np_, w, per):
    K, F = w.shape
    t = w.reshape(K // 128 // per, per, 128, F).transpose(0, 2, 1, 3)
    return np_.ascontiguousarray(t).reshape(K // 128 // per, 128, per * F)


def _cols(np_, v):
    return np_.ascontiguousarray(v.reshape(-1, 128).T)


def _pad(np_, v, n=128):
    c = np_.zeros((n, 1), v.dtype)
    c[:v.shape[0], 0] = v
    return c


def _constants(np_):
    f = np_.float32
    d = np_.arange(128)
    eye = np_.eye(128, dtype=f)
    rot = np_.zeros((128, 128), f)
    for i in range(HALF):
        rot[NOPE + HALF + i, NOPE + i] = -1.0
        rot[NOPE + i, NOPE + HALF + i] = 1.0
    iota = np_.broadcast_to(np_.arange(128, dtype=f), (128, 128))
    iota16 = iota[:, :16]
    msf = np_.where(d[None, :] <= d[:, None], 0.0, NEG).astype(f)
    mtf = np_.ascontiguousarray(msf.T)
    dq = d[:, None] - (np_.arange(512)[None, :] - 384)
    dt = np_.arange(512)[None, :] - d[:, None]

    def patterns(x):
        return ((x >= 0) & (x <= 128)).astype(int) + ((x >= 0) & (x % 4 == 0)) + ((x >= 0) & (x % 16 == 0))

    msd = np_.where(patterns(dq) > 0, 0.0, NEG).astype(f)
    mtd = np_.where(patterns(dt) > 0, 0.0, NEG).astype(f)
    return np_.ascontiguousarray(np_.concatenate(
        [eye, -eye, np_.ones((128, 128), f), rot, iota, iota16, msf, mtf, msd, mtd, patterns(dt).astype(f)], axis=1))


def kernel(**inputs):
    import numpy as _np
    import concourse.bacc as _bacc
    from concourse import mybir as _mybir
    from concourse.bass_utils import run_bass_kernel_spmd as _run

    a = {k: _np.asarray(v) for k, v in inputs.items()}
    w = a["w_in"][0]
    at = _np.cumsum([0, 384, 256, 32, 512, 512, 512, 512, 512, 512, 512, 3072])
    part = {k: w[:, at[i]:at[i + 1]] for i, k in enumerate(
        ("ql", "kvl", "kpe", "cb", "cc", "cu", "qm", "ga", "gc", "gm", "r"))}
    tl = lambda x, c=128: _tiles(_np, x, c)
    cv = _np.stack([tl(part[k]) for k in ("cc", "cu", "cb", "gc")], axis=1).reshape(16, 128, -1)
    kpe = _np.concatenate([_np.zeros((1024, 64), w.dtype), part["kpe"]], axis=1)
    ukv = a["w_ukv"][0].reshape(256, 8, 128)
    mkv = a["w_mkv"][0].reshape(1024, 4, 256)
    br = _np.stack([tl(a[k][0]) for k in ("w_br_attn", "w_br_conv", "w_br_mem")], axis=1).reshape(24, 128, -1)
    r = tl(part["r"]).reshape(3, 8, 128, -1).transpose(1, 0, 2, 3).reshape(24, 128, -1)
    w2 = a["w_in_2"][0]
    fq, fk, fv, wf, dq, dk, dv = (w2[:, i:j] for i, j in ((0, 512), (512, 1024), (1024, 1536), (1536, 1544),
                                                          (1544, 2056), (2056, 2568), (2568, 3080)))
    qk2 = _np.concatenate([_np.stack([tl(q), tl(k)], axis=1).reshape(8, 128, -1) for q, k in ((fq, fk), (dq, dk))])
    invf = (_np.float32(10000.0) ** (-_np.arange(0, 32, 2, dtype=_np.float32) / _np.float32(32))).astype(_np.float32)
    col = lambda k: _cols(_np, a[k][0])
    pad = lambda v: _pad(_np, v)
    table = _np.concatenate([
        col("norm_g"), col("q_norm_g"), col("kv_norm_g"), pad(a["q_head_g"][0]), pad(a["k_head_g"][0]),
        a["conv_w"][0].reshape(12, 128).T, col("conv_b"), col("mem_norm_g"), col("mem_q_g"), col("mem_k_g"),
        a["b_gate"][0].reshape(3, 8, 128).transpose(1, 0, 2).reshape(24, 128).T, col("norm1_g_2"),
        col("norm2_g_2"), pad(a["b_forget_2"][0]),
        pad(_np.concatenate([_np.zeros(64, _np.float32), invf, invf])),
        _np.full((128, 1), EPS, _np.float32)], axis=1)
    slopes = 2.0 ** -_np.arange(1, 9, dtype=_np.float32)
    arrays = {
        "xT": a["x"][0].T.reshape(8, 128, 512).transpose(1, 0, 2),
        "memT": a["mem"][0].T.reshape(8, 128, 256).transpose(1, 0, 2),
        "pos": a["positions"], "cols": table, "const": _constants(_np),
        "bias": (slopes[:, None] * _np.arange(512, dtype=_np.float32)[None]).astype(_np.float32),
        "lat": tl(_np.concatenate([part["ql"], part["kvl"]], axis=1)), "kpe": tl(kpe, 96),
        "conv": cv, "gate": _np.concatenate([tl(part["ga"]), tl(part["gm"])]), "qm": tl(part["qm"]),
        "uq": tl(a["w_uq"][0], 96), "uk": tl(ukv[:, :, :64].reshape(256, 512), 64),
        "uv": _rows(_np, ukv[:, :, 64:].reshape(256, 512), 2),
        "mk": tl(mkv[:, :, :128].reshape(1024, 512)), "mv": _rows(_np, mkv[:, :, 128:].reshape(1024, 512), 2),
        "rb": _np.concatenate([r, br], axis=2), "wo": tl(a["w_out"][0]),
        "wf": tl(wf, 8), "v2": _np.concatenate([_rows(_np, fv, 2), _rows(_np, dv, 2)]), "qk2": qk2,
        "wo2": tl(a["w_out_2"][0]), "wq": tl(a["peer_wq_2"][0]),
        "sk": a["peer_subkeys_2"][0].reshape(16, 128, 128).transpose(2, 0, 1),
        "uT": a["peer_u_2"][0].reshape(128, 128, 8, 128).transpose(0, 3, 2, 1).reshape(128, 128, 1024),
        "v": a["peer_v_2"][0].reshape(128, 128, 1024),
        "gf": a["normf_g_2"].reshape(1, 1024),
    }
    nc = _bacc.Bacc("TRN2", target_bir_lowering=False, num_devices=1)
    feed, t_in = {}, {}
    for name, x in arrays.items():
        x = _np.ascontiguousarray(x)
        feed[f"in_{name}"] = x
        t_in[name] = nc.dram_tensor(f"in_{name}", x.shape, _mybir.dt.from_np(x.dtype), kind="ExternalInput").ap()
    out = nc.dram_tensor("out_0", (512, 1024), _mybir.dt.float32, kind="ExternalOutput").ap()
    program(nc, t_in, out)
    res = _run(nc, [feed], core_ids=[0])
    return res.results[0]["out_0"].reshape(1, 512, 1024)
```

```python
from contextlib import ExitStack

import numpy as np

import concourse.bass as bass
from concourse import mybir

F32 = mybir.dt.float32
F32R = mybir.dt.float32r
BF16 = mybir.dt.bfloat16
U32 = mybir.dt.uint32
I32 = mybir.dt.int32
ALU = mybir.AluOpType
ACT = mybir.ActivationFunctionType
AX = mybir.AxisListType

P = 128
D = 1024
KD = D // P
T = 512
TB = T // P
MEM = 256
MB = MEM // P
HEADS = 8
QL, KVL = 3, 2
NOPE, ROPE = 64, 32
QKD = NOPE + ROPE
HALF = ROPE // 2
DH = 64
MEM_HEADS = 4
EPS = 1e-6
ATT2 = 16
TOPK = 16
NT = 128
NS = 64
FREE = (8, 7, 7, 7)
GATED = 8
START = [sum(FREE[:i]) + GATED * i for i in range(5)]
NG = NT - NS
PEER_HEADS = 8
NKEYS = 128
NEG = -1e30
BIG = 3.0e38

COLS = {}
_n = 0
for _name, _k in (("norm", 8), ("qn", 3), ("kvn", 2), ("qh", 1), ("kh", 1), ("cw", 12), ("cb", 4), ("memn", 8),
                  ("mq", 1), ("mk", 1), ("bg", 24), ("norm1", 8), ("norm2", 8), ("bf", 1), ("invf", 1), ("eps", 1)):
    COLS[_name] = _n
    _n += _k
NCOLS = _n

CN = {}
_n = 0
for _name, _k in (("ident", 128), ("negid", 128), ("ones", 128), ("rot", 128), ("iota", 128), ("iota16", 16),
                  ("msf", 128), ("mtf", 128), ("msd", 512), ("mtd", 512), ("cnt", 512)):
    CN[_name] = _n
    _n += _k
NCONST = _n
NKEEP = CN["msf"]

LOADS = []
PROJ = []
STEPS = []
TEMPS = {}
POST_OF = []


def build_schedule():
    if STEPS:
        return

    def load(kind, i, n):
        LOADS.append((kind, i, n))
        return len(LOADS) - 1

    def proj(kind, i, loads, temp=False):
        n = len(PROJ)
        PROJ.append((kind, i, loads))
        if temp:
            TEMPS[n] = len(TEMPS)
            POST_OF.append(None)
        STEPS.append(("proj", n))
        return n

    posts = [0]

    def post(kind, i, ns):
        posts[0] += 1
        for n in ns:
            POST_OF[TEMPS[n]] = posts[0]
        STEPS.append(("post", kind, i, ns, posts[0]))

    def tile(kind, i, k, m, temp=False):
        return proj(kind, i, [load(kind, i, k * m)], temp)

    def pre_q(h):
        tile("uq", h, QL, QKD)

    def pre_k(h):
        tile("uk", h, KVL, NOPE)

    conv_ns = []

    def conv_part(c):
        conv_ns.append(tile("conv", c, KD, P, True))
        if c % 4 == 3:
            post("conv", c // 4, conv_ns[-4:])

    STEPS.append(("norm", "x"))
    STEPS.append(("high_h", "x"))
    for i in range(QL + KVL):
        tile("lat", i, KD, P)
        if i == 0:
            STEPS.append(("cast",))
    tile("kpe", 0, KD, QKD)
    STEPS.append(("rope_tables",))
    STEPS.append(("sq", "kvl"))
    conv_part(0)
    STEPS.append(("norm", "kvl"))
    STEPS.append(("sq", "ql"))
    conv_part(1)
    STEPS.append(("norm", "ql"))
    L = load("uv", 0, KVL * 512)
    for tb in range(TB):
        proj("uv", tb, [L])
    def normed(kind, h):
        pairs = [("qm", i) for i in range(MEM_HEADS)] + [("mk", i) for i in range(MEM_HEADS)]
        n = pairs.index((kind, h)) - 1
        key = {"qm": "mq", "mk": "mk"}[pairs[n][0]] + str(pairs[n][1]) if n >= 0 else None
        if key:
            STEPS.append(("sq", key))
        tile(kind, h, KD, P)
        if key:
            STEPS.append(("norm", key))

    def mem_values():
        STEPS.append(("sq", f"mk{MEM_HEADS - 1}"))
        Ls = [load("mv", c, 1024) for c in range(4)]
        for tb in range(MB):
            proj("mv", tb, Ls)
        STEPS.append(("norm", f"mk{MEM_HEADS - 1}"))

    fill = [lambda c=c: conv_part(c) for c in range(2, 16)]
    fill += [lambda: (STEPS.append(("norm", "mem")), normed("qm", 0))]
    fill += [lambda h=h: normed("qm", h) for h in range(1, MEM_HEADS)]
    fill += [lambda h=h: normed("mk", h) for h in range(MEM_HEADS)]
    fill += [mem_values]

    def filler():
        if fill:
            fill.pop(0)()

    def prep_mla(h):
        yield lambda: (pre_q(h), pre_k(h), STEPS.append(("sq", f"q{h}")), STEPS.append(("sq", f"k{h}")))
        yield lambda: STEPS.append(("norm", f"q{h}"))
        yield lambda: STEPS.append(("norm", f"k{h}"))
        yield lambda: STEPS.append(("rope", h, 0))
        yield lambda: STEPS.append(("rope", h, 1))

    for f in prep_mla(0):
        f()
        filler()
    for qb in range(TB):
        STEPS.append(("S", 0, qb))
    filler()
    STEPS.append(("M", 0))
    for h in range(HEADS):
        nxt = prep_mla(h + 1) if h + 1 < HEADS else iter(())

        def more():
            f = next(nxt, None)
            if f:
                f()
        more()
        STEPS.append(("T", h, 0))
        STEPS.append(("T", h, 1))
        more()
        STEPS.append(("PV", h, 0))
        STEPS.append(("T", h, 2))
        more()
        STEPS.append(("PV", h, 1))
        if h + 1 < HEADS:
            filler()
        more()
        more()
        STEPS.append(("T", h, 3))
        STEPS.append(("PV", h, 2))
        STEPS.append(("PV", h, 3))
        if h + 1 < HEADS:
            for qb in range(TB):
                STEPS.append(("S", h + 1, qb))
        STEPS.append(("O", h))
        if h + 1 < HEADS:
            filler()
            STEPS.append(("M", h + 1))
    while fill:
        filler()
    def gate(i):
        n = tile("gate", i, KD, P, i < 4)
        if i < 4:
            post("gate", i, [n])

    for h in range(MEM_HEADS):
        a = HEADS + h
        for qb in range(TB):
            STEPS.append(("S", a, qb))
        STEPS.append(("M", a))
        gate(2 * h)
        if h >= 2:
            STEPS.append(("split", "b", 4 * (h - 2), 4 * (h - 1)))
        for kb in range(MB):
            STEPS.append(("T", a, kb))
        for kb in range(MB):
            STEPS.append(("PV", a, kb))
        STEPS.append(("O", a))
        gate(2 * h + 1)
    for i in range(4):
        post("mgate", i, [])
    STEPS.append(("split", "b", 8, 12))
    for f in range(KD):
        for b in range(3):
            n1 = tile("r", 3 * f + b, KD, P, True)
            n2 = tile("br", 3 * f + b, 4, P, True)
            post("rb", 3 * f + b, [n1, n2])
    STEPS.append(("split", "y", 0, KD))
    for f in range(KD):
        post("res", f, [tile("wo", f, KD, P, True)])

    STEPS.append(("norm", "x2"))
    post("forget", 0, [tile("wf", 0, KD, 8, True)])
    STEPS.append(("high_h", "x2"))
    for g in range(2):
        Ls = [load("v2", 4 * g + c, 1024) for c in range(4)]
        for tb in range(TB):
            proj("v2", TB * g + tb, Ls)
    STEPS.append(("low_h",))

    def qk2(p, s):
        tile("qk2", 2 * p + s, KD, P)

    qk2(0, 0)
    qk2(0, 1)
    for qb in range(TB):
        STEPS.append(("S", 12, qb))
    qk2(1, 0)
    STEPS.append(("M", 12))
    for j in range(ATT2):
        a = 12 + j
        more = [("S", a + 1, qb) for qb in range(TB)] if j + 1 < ATT2 else []

        def between():
            if more:
                STEPS.append(more.pop(0))
        STEPS.append(("T", a, 0))
        between()
        STEPS.append(("T", a, 1))
        between()
        STEPS.append(("PV", a, 0))
        STEPS.append(("T", a, 2))
        between()
        STEPS.append(("PV", a, 1))
        STEPS.append(("T", a, 3))
        between()
        STEPS.append(("PV", a, 2))
        STEPS.append(("PV", a, 3))
        STEPS.append(("O", a))
        if j >= 13:
            STEPS.append(("split", "o", *((0, 3), (3, 6), (6, KD))[j - 13]))
        if j + 1 < ATT2:
            STEPS.append(("M", a + 1))
            if j % 2 == 0 and j // 2 + 1 < 8:
                qk2(j // 2 + 1, 1)
            elif j % 2 == 1 and j // 2 + 2 < 8:
                qk2(j // 2 + 2, 0)
    for f in range(KD):
        post("res2", f, [tile("wo2", f, KD, P, True)])
    STEPS.append(("norm", "h2"))
    STEPS.append(("high_h", "h2"))
    for i in range(2 * PEER_HEADS):
        tile("wq", i, KD, P)
        if i:
            STEPS.append(("keys", i - 1))
    STEPS.append(("keys", 2 * PEER_HEADS - 1))


SPLIT = ("lat", "kpe", "conv", "gate", "qm", "r", "br", "wo", "qk2", "wo2", "wq")
PHASES = (("x", KD), ("b", 12), ("y", KD), ("x2", KD), ("o", KD), ("h2", KD))


def norm_shape(key):
    if key in ("x", "x2", "h2"):
        return KD, D, T
    if key == "mem":
        return KD, D, MEM
    if key == "ql":
        return QL, QL * P, T
    if key == "kvl":
        return KVL, KVL * P, T
    if key.startswith("mq"):
        return 1, P, T
    if key.startswith("mk"):
        return 1, P, MEM
    return 1, QKD, T


def program(nc, t_in, out):
    build_schedule()
    ctx = ExitStack()
    with ctx:
        def sem(name):
            return ctx.enter_context(nc.semaphore(name))

        LOW = 2 * KD * T + NKEEP + NCOLS + NCOLS % 2 + 960 + 3 * T + 8
        HH = LOW + 16384
        SB = HH + 12288 + 24 * T

        def place(name, off, shape, dt):
            with nc.sbuf_tensor(name + "_before", [P, off], F32) if off else ExitStack():
                with nc.sbuf_tensor(name, [P] + shape, dt) as buffer:
                    return buffer

        low = place("low", 0, [LOW], F32)
        blocks = place("blocks", LOW, [SB - LOW], F32)
        TAIL = LOW + 16384 + 4096
        staged = place("staged", LOW, [16384], F32)
        v_raw = place("v_raw", LOW + 12288, [4, D], F32)
        tail = place("tail", TAIL, [SB - TAIL], F32)

        def region(off, n, k=None, of=None):
            at, base = of or ((low, 0) if off < LOW else (blocks, LOW))
            v = at[:, off - base:off - base + n]
            return v if k is None else v.rearrange("p (k n) -> p k n", k=k)

        xT = region(0, 4096, KD)
        hT = region(4096, 4096, KD)
        o = 8192
        const = region(o, NKEEP)
        o += NKEEP
        cols = region(o, NCOLS)
        o += NCOLS + NCOLS % 2
        msf = region(o, 64).bitcast(BF16)
        mtf = region(o + 64, 64).bitcast(BF16)
        msd = region(o + 128, 256).bitcast(BF16)
        mtd = region(o + 384, 256).bitcast(BF16)
        cnt = region(o + 640, 256).bitcast(BF16)
        idb = region(o + 896, 64).bitcast(BF16)
        o += 960
        mx = region(LOW - 8, 8)
        lists_off = o
        lists = region(o, 3 * T, 3)
        o += 3 * T + 8
        assert o == LOW
        NW = 5
        ring = region(o, NW * 1024, NW)
        o += NW * 1024
        NE = 5
        ebuf = region(o, NE * T, NE)
        o += NE * T
        NQ = 3
        sq = region(o, NQ * T, NQ)
        o += NQ * T
        rs = region(o, T)
        o += T
        dtmp = region(o, T)
        o += T
        PT_off = o
        PT = region(o, 4 * T, 4)
        o += 4 * T
        mkT_off = o
        mkT = region(o, 4 * MEM, 4)
        o += 4 * MEM
        mrow = region(o, T)
        o += T
        Q2 = region(o, 4 * T, 4)
        rtmp = region(o, T)
        cosT = region(o + T, T)
        sinT = region(o + 2 * T, T)
        qm1 = region(o + 3 * T, 2 * T, 2)
        mv = region(o + 3 * T, MB * T, MB)
        o += 5 * T
        assert o <= HH
        VA = region(HH + 4096, 4096).rearrange("p (t h d) -> p t h d", t=TB, h=HEADS)
        o = HH + 12288
        oT = region(o, 12 * T, 12)
        oT_off = o
        memT = region(o + 8 * T, KD * MEM, KD)
        o += 12 * T
        R1 = o
        lat = region(o, 6 * T, 6)
        o += 6 * T
        km1 = region(o, 2 * T, 2)
        o += 2 * T
        mq = region(o, 4 * T, 4)
        K2 = region(o, 4 * T, 4)
        o += 4 * T
        zsm = lists
        memgate = lat[:, 0:4, :]
        cwork = zsm
        zc = region(LOW - 8 - (T + 2), T + 2)
        assert o <= SB, o
        yT = region(R1, 4096, KD)
        VB = region(R1, 4096).rearrange("p (t h d) -> p t h d", t=TB, h=HEADS)
        def rt(off, n, k=None):
            return region(TAIL + off, n, k, (tail, TAIL))

        UR = rt(0, 4 * 1024, 4)
        AF = rt(8192, 4 * T, 4)
        pq = AF
        GR = rt(10240, 4 * T, 4)
        ohring = rt(10240, 2 * 2 * 4 * P).rearrange("p (s w u i) -> p s w u i", s=2, w=2, u=4)
        sk = rt(12288, 2048, 16)
        cand = rt(12288, 2048)
        sc = rt(14336, 4 * T, 4)
        eq = rt(14336, 2048)
        gf = rt(12288, D)
        fsq = rt(13312, D)
        fss = rt(14336, 16)
        tva = rt(16384, 1024, 4).rearrange("p t (h k) -> p t h k", h=16)
        tia = rt(17408, 1024, 4).rearrange("p t (h k) -> p t h k", h=16).bitcast(U32)
        tif = rt(18432, 256)
        cs = rt(18688, 128, 8)
        ci = rt(18816, 128, 8).bitcast(U32)
        ca = rt(18944, 128).bitcast(U32)
        cbf = rt(19072, 256, 2)
        sel = rt(19328, 384, 3)
        ee = rt(19712, 128)
        es = rt(19840, 16)
        assert TAIL + 19856 <= SB
        stage = staged[:, :].rearrange("p (i t) -> p i t", i=P)
        VR = v_raw
        U2 = place("u_split", TAIL + 4096, [2, 2, KD, P], F32R)
        V2 = place("v_split", LOW, [4, 2, D], F32R)
        A2 = place("a_split", LOW + 8192, [4, 2, T], F32R)
        hh = place("h_high", HH, [KD, T], F32R)
        hl = place("h_low", 4096, [KD, T], F32R)

        B2 = [place("branch_weights0", lists_off, [2, 4 * P], F32R), place("branch_weights1", mkT_off, [2, 4 * P], F32R)]
        yl = place("y_low", R1, [KD, T], F32R)
        ol = place("o_low", oT_off, [12, T], F32R)
        oh = (place("o_high", HH + 4096, [8, T], F32R), place("o_high_mem", PT_off, [4, T], F32R))
        craw = region(oT_off, NCONST - NKEEP)
        pos_i = ebuf[:, 0, :].bitcast(I32)

        ident = const[:, CN["ident"]:CN["ident"] + P]
        negid = const[:, CN["negid"]:CN["negid"] + P]
        ones = const[:, CN["ones"]:CN["ones"] + P]
        rot = const[:, CN["rot"]:CN["rot"] + P]
        iota = const[:, CN["iota"]:CN["iota"] + P]
        iota16 = const[:, CN["iota16"]:CN["iota16"] + 16]

        def col(name, i=0, p0=0, p1=P):
            return cols[p0:p1, COLS[name] + i:COLS[name] + i + 1]

        bank = [ctx.enter_context(nc.psum_tensor(f"bank{i}", [P, T], F32)) for i in range(8)]
        pj = [bank[0], bank[1]]
        ax = [bank[2], bank[7]]
        scb = [bank[3], bank[4], bank[5]]
        ob = bank[6]

        kept = nc.dram_tensor("kept_hidden", (NS, P, T), F32, kind="Internal").ap()
        gates = nc.dram_tensor("gates", (NKEYS, P, T), F32, kind="Internal").ap()

        s_x = [sem(f"x_tiles_{c}_loaded") for c in range(4)]
        s_par = sem("params_loaded")
        s_const = sem("constants_loaded")
        s_raw = sem("masks_loaded")
        s_mem = sem("mem_loaded")
        s_pos = sem("positions_loaded")
        s_cast = sem("masks_cast")
        s_init = sem("buffers_set")
        s_init2 = sem("second_block_buffers_set")
        s_w = [sem(f"weights_in_slot{i}") for i in range(NW)]
        s_proj = sem("projections_done")
        s_evac = sem("projections_evacuated")
        s_post = sem("post_steps_done")
        s_sq = sem("squares_ready")
        s_squsd = sem("squares_used")
        s_aux = sem("aux_bank_written")
        s_auxfree = [sem("aux_bank0_read"), sem("aux_bank1_read")]
        s_whi = sem("weight_high_parts")
        s_wlo = sem("weight_low_parts")
        s_hk = sem("normalised_tiles_ready")
        s_chunk = sem("value_weight_chunks_done")
        s_rs = sem("reciprocal_roots_done")
        s_norm = sem("norm_steps_done")
        s_tab = sem("rope_tables_done")
        s_rope = sem("rope_steps_done")
        s_S = sem("score_rows_done")
        s_max = sem("row_maxima_done")
        s_T = sem("score_columns_done")
        s_P = sem("exponentials_done")
        s_Pc = sem("exponentials_counted")
        s_PV = sem("value_products_done")
        s_O = sem("head_outputs_done")
        s_kb = [sem(f"key_bias_in_buffer{i}") for i in range(4)]
        s_fmag = sem("forget_magnitudes_ready")
        s_fch = sem("forget_logs_done")
        s_d = sem("vector_chain")
        s_rc = sem("scalar_chain")
        s_sk = sem("subkeys_loaded")
        s_cos = sem("angles_ready")
        s_qs = sem("key_scores_done")
        s_qe = sem("key_scores_copied")
        s_half = sem("halves_sorted")
        s_tk = sem("topk_blocks_done")
        s_kept = [sem(f"hidden_kept_slot{i}") for i in range(4)]
        s_h = [sem(f"hidden_back_{i}") for i in range(2)]
        s_sm = sem("rank_differences_ready")
        s_ex = sem("rank_exponentials_done")
        s_lt = sem("lists_transposed")
        s_ltc = sem("lists_copied")
        s_hx = sem("residual_transposed")
        s_hxc = sem("residual_copied")
        s_oh = sem("onehots_ready")
        s_gm = [sem(f"gate_groups_done_bank{i}") for i in range(2)]
        s_ge = [sem(f"gate_groups_copied_bank{i}") for i in range(2)]
        s_gst = sem("gates_stored")
        s_gst_first = sem("last_gates_stored_first_part")
        s_u = [sem(f"u_tile_in_slot{i}") for i in range(4)]
        s_v = [sem(f"v_tiles_{i}") for i in range(2)]
        s_g = [sem(f"g_tiles_{i}") for i in range(2)]
        s_hid = sem("hidden_done")
        s_gelu = sem("gelu_done")
        s_act = sem("gated_done")
        s_ahi = sem("gated_high_parts")
        s_alo = sem("gated_low_parts")
        s_uhi = sem("u_high_parts")
        s_ulo = sem("u_low_parts")
        s_vhi = sem("v_high_parts")
        s_vlo = sem("v_low_parts")
        s_hh = sem("h_high_parts")
        s_hl = sem("h_low_parts")
        s_eo = sem("expert_outputs_done")
        s_ea = sem("expert_outputs_added")
        s_gf = sem("final_gain_loaded")
        s_fin = sem("final_rows_ready")
        s_fsq = sem("final_squares_done")
        s_out = sem("output_stored")

        NORMS = [s[1] for s in STEPS if s[0] == "norm"]
        norm_no = {k: i + 1 for i, k in enumerate(NORMS)}
        sq0, n = {}, 0
        for k in NORMS:
            sq0[k] = n
            n += norm_shape(k)[0]
        pi = {(k, i): n for n, (k, i, _) in enumerate(PROJ)}
        auxi, n = {}, 0
        for s in STEPS:
            if s[0] == "norm":
                auxi[("norm", s[1])] = n
                n += 1
            elif s[0] == "rope":
                auxi[("rope",) + s[1:]] = n
                n += 1
            elif s[0] == "M":
                auxi[("M", s[1])] = n
                n += 1
            elif s[0] == "PV" and HEADS <= s[1] < 12 and s[2] == 0:
                auxi[("den", s[1])] = n
                n += 1
        tiles = [s for s in STEPS if s[0] in ("S", "T")]
        tile_no = {s: i for i, s in enumerate(tiles)}
        s_no = {s: i + 1 for i, s in enumerate(x for x in tiles if x[0] == "S")}
        t_no = {s: i + 1 for i, s in enumerate(x for x in tiles if x[0] == "T")}
        pv_no = {s[1:]: i + 1 for i, s in enumerate(x for x in STEPS if x[0] == "PV")}
        cnt_no = {s[1:]: i + 1 for i, s in enumerate(x for x in STEPS if x[0] == "T" and x[1] >= 20)}
        rope_no = {s[1:]: i + 1 for i, s in enumerate(x for x in STEPS if x[0] == "rope")}
        M_no = {s[1]: i + 1 for i, s in enumerate(x for x in STEPS if x[0] == "M")}
        O_no = {s[1]: i + 1 for i, s in enumerate(x for x in STEPS if x[0] == "O")}
        post_no = {s[1:3]: s[4] for s in STEPS if s[0] == "post"}
        last_use = {}
        for n, (_, _, loads) in enumerate(PROJ):
            for L in loads:
                last_use[L] = n

        slots, came_before, place_after = {}, {}, {}
        users = {True: [], False: []}
        for n, (kind, _, loads) in enumerate(PROJ):
            if kind in SPLIT:
                same = users[kind == "br"]
                slots[n] = len(same) % 2
                came_before[n] = same[-2] if len(same) >= 2 else None
                after = came_before[n] if len(same) >= 2 else -1 if kind != "br" else n - 2
                if loads[0] >= NW:
                    after = max(after, min(last_use[loads[0] - NW] + 1, n - 1))
                place_after[n] = after
                same.append(n)
        UNITS = sorted(place_after, key=lambda n: (place_after[n], n))
        unit = {n: u for u, n in enumerate(UNITS)}
        split_after = {}
        for u, n in enumerate(UNITS):
            split_after.setdefault(place_after[n], []).append(u)
        assert split_after[-1] == [0, 1]

        def flat(u, part):
            n = UNITS[u]
            if PROJ[n][0] == "br":
                return B2[slots[n]][:, part]
            return U2[:, slots[n], part].rearrange("p k e -> p (k e)")

        H_NO = {"x": 0, "x2": 1, "h2": 2}
        parts0 = {key: sum(n for _, n in PHASES[:i]) for i, (key, _) in enumerate(PHASES)}

        def unit_size(u):
            kind = PROJ[UNITS[u]][0]
            return KD * QKD if kind == "kpe" else 4 * P if kind == "br" else KD * P

        def n_keys(a):
            return MB if HEADS <= a < 12 else TB

        def q0(a, kb):
            return kb * P if a >= 12 else 0

        def at_least(eng, sem, value):
            if not isinstance(value, int) or value > 0:
                eng.wait_ge(sem, value)

        def rounds(eng, n, body, first=False, last=False):
            a, b = int(first), n - int(last)
            if first:
                body(0, False)
            if b > a:
                with eng.Fori(a, b) as it:
                    body(it, False)
            if last:
                body(n - 1, True)

        block = ctx.enter_context(nc.Block())

        @block.sync
        def _(sp):
            for c in range(4):
                sp.dma_start(xT[:, 2 * c:2 * c + 2, :], t_in["xT"][:, 2 * c:2 * c + 2, :]).then_inc(s_x[c], 16)
                if c == 0:
                    sp.dma_start(const, t_in["const"][:, 0:NKEEP]).then_inc(s_const, 16)
                    sp.dma_start(cols, t_in["cols"]).then_inc(s_par, 16)

            def weights(L):
                kind, i, n = LOADS[L]
                if L >= NW:
                    was, c, _ = LOADS[L - NW]
                    if was == "v2" and c % 4 < 3:
                        sp.wait_ge(s_chunk, 3 * (c // 4) + c % 4 + 1)
                    else:
                        sp.wait_ge(s_proj, last_use[L - NW] + 1)
                sp.dma_start(ring[:, L % NW, 0:n], t_in[kind][i]).then_inc(s_w[L % NW], 16)

            for L in range(len(LOADS)):
                weights(L)
                if L == NW - 1:
                    sp.dma_start(craw, t_in["const"][:, NKEEP:NCONST]).then_inc(s_raw, 16)
                    sp.dma_start(pos_i[NOPE:QKD, :], t_in["pos"].to_broadcast([ROPE, T])).then_inc(s_pos, 16)
                    sp.dma_start(memT, t_in["memT"]).then_inc(s_mem, 16)
                if LOADS[L][:2] == ("wq", 3):
                    sp.wait_ge(s_proj, pi[("wo2", KD - 1)] + 1)
                    sp.dma_start(sk, t_in["sk"]).then_inc(s_sk, 16)
            def load_u(e, slot):
                at_least(sp, s_ulo, e - 3)
                sp.dma_start(UR[:, slot, :], t_in["uT"][bass.ds(e, 1)].rearrange("s p n -> p (s n)"))\
                    .then_inc(s_u[slot], 16)

            def keep(e, slot):
                sp.wait_ge(s_gelu, e + 1)
                sp.dma_start(kept[bass.ds(e, 1)].rearrange("s p n -> p (s n)"), AF[:, slot, :])\
                    .then_inc(s_kept[slot], 16)

            def tile(e, slot=None):
                slot = e % 4 if slot is None else slot
                keep(e, slot)
                load_u(e + 4, slot)

            v2w = t_in["v"].rearrange("(w g) p n -> g p w n", w=2)
            g2w = gates.rearrange("(w g) p n -> g p w n", w=2)

            def load_values(g, half):
                if isinstance(g, int) and g == 0:
                    sp.wait_ge(s_gst_first, 64)
                at_least(sp, s_vlo, g * 2 - 2)
                sp.dma_start(VR[:, 2 * half:2 * half + 2, :], v2w[bass.ds(g, 1)].rearrange("s p w n -> p (s w) n"))\
                    .then_inc(s_v[half], 16)

            def load_gates(g, half):
                if isinstance(g, int) and g == 0:
                    sp.wait_ge(s_gst, 128 * (TB - 1))
                at_least(sp, s_act, g * 2 - 2)
                sp.dma_start(GR[:, 2 * half:2 * half + 2, :], g2w[bass.ds(g, 1)].rearrange("s p w n -> p (s w) n"))\
                    .then_inc(s_g[half], 16)

            def load_kept(g, half):
                at_least(sp, s_alo, g * 2 - 2)
                sp.dma_start(AF[:, 2 * half, :], kept[bass.ds(g, 1)].rearrange("s p n -> p (s n)"))\
                    .then_inc(s_h[half], 16)

            def load_group(g, half):
                load_values(g, half)
                load_gates(g, half)
                load_kept(g, half)

            def store_gates(tb, parts, done=s_gst):
                for c in parts:
                    sp.dma_start(gates[16 * c:16 * c + 16, :, tb * P:(tb + 1) * P].rearrange("i j t -> j i t"),
                                 stage[:, 16 * c:16 * c + 16, :]).then_inc(done, 16)

            PIECES = [[0], [1], [2, 3], [4, 5], [6, 7]] + [[]] * 3

            sp.wait_ge(s_proj, pi[("wo2", KD - 1)] + 1)
            for e in range(4):
                load_u(e, e)
            for tb in range(TB):
                for i in range(FREE[tb]):
                    if tb:
                        store_gates(tb - 1, PIECES[i])
                    tile(START[tb] + i)

                def gated_tiles(it, _):
                    for u in range(4):
                        tile(it * 4 + (START[tb] + FREE[tb] + u), (START[tb] + FREE[tb] + u) % 4)
                rounds(sp, GATED // 4, gated_tiles)
                for u in range(2):
                    sp.wait_ge(s_ge[u], 16 * (tb + 1))
            for i, e in enumerate(range(START[TB], NS)):
                if i == 0:
                    store_gates(TB - 1, [6, 0, 1, 4], s_gst_first)
                tile(e)
                if e == NS - 2:
                    load_values(0, 0)
                    load_gates(0, 0)
                    sp.wait_ge(s_kept[0], 16 * NS // 4)
                    load_kept(0, 0)
            store_gates(TB - 1, [7, 2, 3, 5])
            for u in range(4):
                sp.wait_ge(s_kept[u], 16 * NS // 4)

            sp.wait_ge(s_gst, 128 * TB - 64)
            load_group(1, 1)
            sp.dma_start(gf, t_in["gf"].to_broadcast([P, D])).then_inc(s_gf, 16)

            def group_loads(it, last):
                for q in range(4):
                    if not last:
                        load_u(it * 4 + (NS + q + 4), q)
                    if not last or q < 2:
                        load_group(it * 4 + (q + 2), q % 2)
            rounds(sp, NG // 4, group_loads, last=True)
            for tb in range(TB):
                sp.wait_ge(s_fin, tb + 1)
                sp.dma_start(out[tb * P:(tb + 1) * P, :], xT[:, 2 * tb:2 * tb + 2, :]
                             .rearrange("p k n -> p (k n)")).then_inc(s_out, 16)
            sp.wait_ge(s_out, 16 * TB)

        @block.gpsimd
        def _(pool):
            nc.gpsimd.memset(VA, 1.0).then_inc(s_init, 1)
            pool.wait_ge(s_init, 1)
            nc.gpsimd.memset(km1[QKD:P, :, :], 1.0).then_inc(s_init, 1)
            pool.wait_ge(s_init, 2)
            nc.gpsimd.memset(zc[:, 0:T + 2], 0.0).then_inc(s_init, 1)

            buffers_set = [0]

            def low_weights(u):
                kind, _, loads = PROJ[UNITS[u]]
                n = unit_size(u)
                pool.wait_ge(s_whi, u + 1)
                if u:
                    pool.wait_ge(s_wlo, u)
                if buffers_set[0]:
                    pool.wait_ge(s_init2, buffers_set[0])
                nc.gpsimd.tensor_tensor(flat(u, 1)[:, 0:n], ring[:, loads[0] % NW, 0:n],
                                        flat(u, 0)[:, 0:n].bitcast(F32), ALU.subtract).then_inc(s_wlo, 1)

            def key_bias(j):
                if j == 0:
                    pool.wait_ge(s_post, post_no[("forget", 0)])
                    pool.wait_ge(s_init2, 6)
                if j >= 4:
                    pool.wait_ge(s_T, t_no[("T", 12 + j - 4, TB - 1)])
                src = zsm[j:j + 1, 2, :] if j < 8 else t_in["bias"][j - 8:j - 7, :]
                pool.dma_start(K2[NOPE:NOPE + 1, j % 4, :], src).then_inc(s_kb[j % 4], 16)

            def second_block_buffers(n, lows):
                pool.wait_ge(s_wlo, lows)
                buffers_set[0] = n + 1
                if n == 0:
                    pool.wait_ge(s_O, 12)
                else:
                    pool.wait_ge(s_init2, n)
                if n == 4:
                    pool.wait_ge(s_proj, pi[("br", 3 * KD - 1)] + 1)
                if n == 5:
                    pool.wait_ge(s_proj, pi[("wo", KD - 1)] + 1)
                what, value = ((Q2[NOPE:QKD, :, :], 0.0), (K2[NOPE:QKD, :, :], 0.0), (K2[QKD:P, :, :], 1.0),
                               (Q2[NOPE:NOPE + 1, :, :], 1.0), (VA, 1.0), (VB, 1.0))[n]
                nc.gpsimd.memset(what, value).then_inc(s_init2, 1)

            lows = 2
            for s in STEPS:
                if s[0] == "high_h" and s[1] == "x":
                    low_weights(0)
                    low_weights(1)
                elif s[0] == "proj":
                    for u in split_after.get(s[1], []):
                        low_weights(u)
                        lows = u + 1
                elif s[0] == "post" and s[1] == "rb" and 3 <= s[2] < 7:
                    second_block_buffers(s[2] - 3, lows)
                elif s[0] == "post" and s[1] == "res" and s[2] in (0, KD - 1):
                    second_block_buffers(4 if s[2] == 0 else 5, lows)
                elif s[0] == "low_h":
                    for j in range(4):
                        key_bias(j)
                elif s[0] == "T" and 12 <= s[1] < 24 and s[2] == TB - 1:
                    key_bias(s[1] - 12 + 4)
            pool.wait_ge(s_kb[3], 16 * 4)

            def low_u(e, slot):
                pool.wait_ge(s_uhi, e + 1)
                nc.gpsimd.tensor_tensor(U2[:, slot % 2, 1].rearrange("p k e -> p (k e)"), UR[:, slot, :],
                                        U2[:, slot % 2, 0].rearrange("p k e -> p (k e)").bitcast(F32),
                                        ALU.subtract).then_inc(s_ulo, 1)

            def low_v(e, slot):
                pool.wait_ge(s_vhi, e + 1)
                nc.gpsimd.tensor_tensor(V2[:, slot, 1], VR[:, slot, :], V2[:, slot, 0].bitcast(F32),
                                        ALU.subtract).then_inc(s_vlo, 1)

            pool.wait_ge(s_wlo, len(UNITS))
            low_u(0, 0)
            low_u(1, 1)
            rounds(pool, NS // 4, lambda it, _: [low_u(it * 4 + (u + 2), (u + 2) % 4) for u in range(4)])

            def low_parts(it, last):
                for q in range(4):
                    if not last or q < 2:
                        low_u(it * 4 + (NS + q + 2), (q + 2) % 4)
                    for w in range(2):
                        low_v(it * 8 + (2 * q + w), 2 * (q % 2) + w)
            rounds(pool, NG // 4, low_parts, last=True)

        @block.tensor
        def _(pe):
            mm = nc.tensor.matmul

            def need_aux(i):
                if i >= 2:
                    pe.wait_ge(s_auxfree[i % 2], i // 2)

            def proj(n):
                kind, i, loads = PROJ[n]
                if n >= 2:
                    pe.wait_ge(s_evac, n - 1)
                if kind in SPLIT:
                    pe.wait_ge(s_wlo, unit[n] + 1)
                else:
                    for L in loads:
                        pe.wait_ge(s_w[L % NW], 16 * (L // NW + 1))
                ps = pj[n % 2]
                w = ring[:, loads[0] % NW, :]

                def run(nk, m, rhs, N=T):
                    for k in range(nk):
                        last = mm(ps[0:m, 0:N], w[:, k * m:(k + 1) * m], rhs(k),
                                  start=(k == 0), stop=(k == nk - 1))
                    return last

                def split(m, nk=KD):
                    u = unit[n]
                    phase = {"lat": "x", "br": "b", "wo": "y", "qk2": "x2", "wo2": "o", "wq": "h2"}.get(kind)
                    first = i < 3 if kind == "br" else i == 0
                    x_low = {"br": ol, "wo": yl, "wo2": ol}.get(kind, hl)
                    for k in range(nk):
                        t = 4 * (i % 3) + k if kind == "br" else k
                        if first and phase is not None:
                            pe.wait_ge(s_hl, parts0[phase] + t + 1)
                        high = oh[t // 8][:, t % 8, :] if kind == "br" else hh[:, t, :]
                        for j, (part, x) in enumerate(((0, high), (0, x_low[:, t, :]), (1, high))):
                            last = mm(ps[0:m, :], flat(u, part)[:, k * m:(k + 1) * m], x,
                                      start=(k == 0 and j == 0), stop=(k == nk - 1 and j == 2))
                    return last

                def normalised(k):
                    if k < KD - 1:
                        pe.wait_ge(s_hk, KD - 1 + k + 1)
                    else:
                        pe.wait_ge(s_norm, norm_no["x2"])
                    return hT[:, k, :]

                def tok(lhs, nk, chunk):
                    for k in range(nk):
                        L = loads[k // chunk]
                        last = mm(ps[:, :], lhs(k), ring[:, L % NW, (k % chunk) * T:(k % chunk + 1) * T],
                                  start=(k == 0), stop=(k == nk - 1))
                        if kind == "v2" and i % TB == TB - 1 and k % chunk == chunk - 1 and k < nk - 1:
                            last.then_inc(s_chunk, 1)
                    return last

                if kind in SPLIT:
                    last = split(QKD if kind == "kpe" else P, 4 if kind == "br" else KD)
                elif kind == "uq":
                    pe.wait_ge(s_norm, norm_no["ql"])
                    last = run(QL, QKD, lambda k: lat[:, k, :])
                elif kind == "uk":
                    pe.wait_ge(s_norm, norm_no["kvl"])
                    last = run(KVL, NOPE, lambda k: lat[:, QL + k, :])
                elif kind == "uv":
                    pe.wait_ge(s_norm, norm_no["kvl"])
                    last = tok(lambda k: lat[:, QL + k, i * P:(i + 1) * P], KVL, KVL)
                elif kind == "mk":
                    pe.wait_ge(s_norm, norm_no["mem"])
                    last = run(KD, P, lambda k: memT[:, k, :], N=MEM)
                elif kind == "mv":
                    pe.wait_ge(s_norm, norm_no["mem"])
                    last = tok(lambda k: memT[:, k, i * P:(i + 1) * P], KD, 2)
                elif kind == "wf":
                    last = run(KD, 8, normalised)
                elif kind == "v2":
                    tb = i % TB
                    last = tok(lambda k: hT[:, k, tb * P:(tb + 1) * P], KD, 2)
                last.then_inc(s_proj, 1)

            def norm(key):
                nk, width, N = norm_shape(key)
                i = auxi[("norm", key)]
                need_aux(i)
                rows = min(width, P)
                for k in range(nk):
                    j = sq0[key] + k
                    pe.wait_ge(s_sq, j + 1)
                    last = mm(ax[i % 2][0:rows, 0:N], ones[0:rows, 0:rows], sq[0:rows, j % NQ, 0:N],
                              start=(k == 0), stop=(k == nk - 1))
                    if k < nk - 1:
                        last.then_inc(s_squsd, 1)
                last.then_inc(s_aux, 1)

            def rope(h, which):
                i = auxi[("rope", h, which)]
                need_aux(i)
                pe.wait_ge(s_norm, norm_no[f"{'qk'[which]}{h}"])
                src = (qm1, km1)[which]
                mm(ax[i % 2][0:QKD, :], rot[0:QKD, 0:QKD], src[0:QKD, h % 2, :], start=True, stop=True)\
                    .then_inc(s_aux, 1)

            def operands(a):
                if a < HEADS:
                    return qm1[:, a % 2, :], km1[:, a % 2, :], QKD, QKD + 1
                if a < 12:
                    return mq[:, a - HEADS, :], mkT[:, a - HEADS, :], P, P
                return Q2[:, (a - 12) % 4, :], K2[:, (a - 12) % 4, :], NOPE + 1, QKD + 1

            def score_bank(step):
                n = tile_no[step]
                if n >= 3:
                    was = tiles[n - 3]
                    if was[0] == "S":
                        pe.wait_ge(s_max, s_no[was])
                    else:
                        pe.wait_ge(s_P, t_no[was])
                return scb[n % 3]

            def S(a, qb):
                q, k, K, _ = operands(a)
                if qb == 0:
                    if a < HEADS:
                        pe.wait_ge(s_rope, rope_no[(a, 1)])
                    elif a < 12:
                        pe.wait_ge(s_norm, norm_no[f"mk{a - HEADS}"])
                    else:
                        p = (a - 12) // 2
                        pe.wait_ge(s_cast, 6)
                        pe.wait_ge(s_init2, 6)
                        pe.wait_ge(s_evac, pi[("qk2", 2 * p + 1)] + 1)
                        pe.wait_ge(s_kb[(a - 12) % 4], 16 * ((a - 12) // 4 + 1))
                ps = score_bank(("S", a, qb))
                N = (qb + 1) * P if a >= 12 else n_keys(a) * P
                last = mm(ps[:, 0:N], q[0:K, qb * P:(qb + 1) * P], k[0:K, 0:N], start=True, stop=(a < 12))
                if 12 <= a < 20:
                    last = mm(ps[:, qb * P:N], idb, msf, start=False, stop=True)
                elif a >= 20:
                    last = mm(ps[:, 0:N], idb, msd[:, T - N:T], start=False, stop=True)
                last.then_inc(s_S, 1)

            def M(a):
                i = auxi[("M", a)]
                need_aux(i)
                pe.wait_ge(s_max, s_no[("S", a, TB - 1)])
                for qb in range(TB):
                    last = mm(ax[i % 2][0:1, qb * P:(qb + 1) * P], mx[:, 4 * (a % 2) + qb:4 * (a % 2) + qb + 1],
                              negid, start=True, stop=True)
                last.then_inc(s_aux, 1)

            def T_(a, kb):
                q, k, _, K = operands(a)
                if kb == 0:
                    i = auxi[("M", a)]
                    pe.wait_ge(s_auxfree[i % 2], i // 2 + 1)
                ps = score_bank(("T", a, kb))
                c0 = q0(a, kb)
                kk = k[0:K, kb * P:(kb + 1) * P]
                last = mm(ps[:, c0:T], kk, q[0:K, c0:T], start=True, stop=(a < HEADS))
                if HEADS <= a < 12:
                    last = mm(ps[:, :], ones[0:1, :], mrow[0:1, :], start=False, stop=True)
                elif 12 <= a < 20:
                    last = mm(ps[:, c0:c0 + P], idb, mtf, start=False, stop=True)
                elif a >= 20:
                    last = mm(ps[:, c0:T], idb, mtd[:, 0:T - c0], start=False, stop=True)
                last.then_inc(s_T, 1)

            def PV(a, kb):
                if a >= 20:
                    pe.wait_ge(s_Pc, cnt_no[(a, kb)])
                else:
                    pe.wait_ge(s_P, t_no[("T", a, kb)])
                if kb == 0 and a > 0:
                    pe.wait_ge(s_O, O_no[a] - 1)
                c0 = q0(a, kb)
                rhs = PT[:, kb, c0:T]
                nk = n_keys(a)
                if a < HEADS:
                    v = VA[:, kb, a, :]
                elif a < 12:
                    v = mv[:, kb, (a - HEADS) * P:(a - HEADS + 1) * P]
                else:
                    v = (VA if a < 20 else VB)[:, kb, (a - 12) % 8, :]
                if kb == 0 and a in (0, HEADS, 12, 20):
                    last_v = {0: ("uv", TB - 1), HEADS: ("mv", MB - 1), 12: ("v2", TB - 1), 20: ("v2", 2 * TB - 1)}[a]
                    pe.wait_ge(s_evac, pi[last_v] + 1)
                if HEADS <= a < 12:
                    i = auxi[("den", a)]
                    if kb == 0:
                        need_aux(i)
                    den = mm(ax[i % 2][:, :], ones, rhs, start=(kb == 0), stop=(kb == nk - 1))
                    if kb == nk - 1:
                        den.then_inc(s_aux, 1)
                mm(ob[:, c0:T], v, rhs, start=(kb == 0), stop=(kb == nk - 1)).then_inc(s_PV, 1)

            pe.wait_ge(s_const, 16)
            for s in STEPS:
                if s[0] == "proj":
                    proj(s[1])
                elif s[0] == "norm":
                    norm(s[1])
                elif s[0] == "rope":
                    rope(s[1], s[2])
                elif s[0] == "S":
                    S(s[1], s[2])
                elif s[0] == "M":
                    M(s[1])
                elif s[0] == "T":
                    T_(s[1], s[2])
                elif s[0] == "PV":
                    PV(s[1], s[2])
                elif s[0] == "keys":
                    i = s[1]
                    if i == 0:
                        pe.wait_ge(s_sk, 16)
                    pe.wait_ge(s_evac, pi[("wq", i)] + 1)
                    if i >= 4:
                        pe.wait_ge(s_qe, i - 3)
                    for tb in range(TB):
                        last = mm(bank[3 + i % 4][:, tb * P:(tb + 1) * P], pq[:, i % 4, tb * P:(tb + 1) * P],
                                  sk[:, i, :], start=True, stop=True)
                    last.then_inc(s_qs, 1)

            pe.wait_ge(s_qe, 2 * PEER_HEADS)
            pe.wait_ge(s_evac, len(PROJ))
            for tb in range(TB):
                for dh in range(2):
                    for k in range(4):
                        last = nc.tensor.transpose(bank[2 * tb + dh][:, k * P:(k + 1) * P],
                                                   xT[:, 4 * dh + k, tb * P:(tb + 1) * P], ident)
            last.then_inc(s_hx, 1)
            pe.wait_ge(s_hxc, 2)

            def lists_out(tb):
                if tb == 0:
                    pe.wait_ge(s_hxc, 8)
                pe.wait_ge(s_tk, tb + 1)
                if tb >= 1:
                    pe.wait_ge(s_ltc, tb)
                for w in range(3):
                    last = nc.tensor.transpose(bank[4][:, w * P:(w + 1) * P], sel[:, w, :], ident)
                last.then_inc(s_lt, 1)

            def gate_group(n, u):
                pe.wait_ge(s_oh, n * 2 + (u + 1))
                at_least(pe, s_ge[u], n)
                for k in range(4):
                    last = mm(bank[2 + u][:, k * P:(k + 1) * P], ohring[:, u, 1, k, :], ohring[:, u, 0, k, :],
                              start=True, stop=True)
                last.then_inc(s_gm[u], 1)

            def hidden(e, slot, between=None):
                pe.wait_ge(s_ulo, e + 1)
                at_least(pe, s_gelu, e - 1)
                for k in range(KD):
                    if between and k % 2 == 0:
                        between(k // 2)
                    for w, x in ((0, hh), (0, hl), (1, hh)):
                        last = mm(bank[slot % 2][:, :], U2[:, slot % 2, w, k, :], x[:, k, :],
                                  start=(k == 0 and x is hh and w == 0), stop=(k == KD - 1 and w == 1))
                last.then_inc(s_hid, 1)

            def outputs(g, half):
                pe.wait_ge(s_vlo, g * 2 + 2)
                pe.wait_ge(s_alo, g * 2 + 2)
                for u in range(8):
                    tb, dh = u // 2, u % 2
                    at_least(pe, s_ea, g * 8 + (u - 3))
                    for e in (2 * half, 2 * half + 1):
                        for wa, wv in ((0, 0), (0, 1), (1, 0)):
                            last = mm(bank[2 + u % 4][:, :], A2[:, e, wa, tb * P:(tb + 1) * P],
                                      V2[:, e, wv, dh * T:(dh + 1) * T],
                                      start=(e == 2 * half and wa == wv), stop=(e > 2 * half and wa == 1))
                    last.then_inc(s_eo, 1)

            for tb in range(TB):
                for e in range(START[tb], START[tb] + FREE[tb]):
                    if e == START[tb] + FREE[tb] - 1:
                        lists_out(tb)
                    hidden(e, e)

                def with_gates(it, _):
                    for u in range(4):
                        hidden(it * 4 + (START[tb] + FREE[tb] + u), START[tb] + FREE[tb] + u,
                               lambda k: gate_group(it * 8 + (16 * tb + 2 * u + k // 2), k % 2))
                rounds(pe, GATED // 4, with_gates, first=tb == 0)
            for e in range(START[TB], NS):
                hidden(e, e)
            for u in range(2):
                pe.wait_ge(s_ge[u], T // 8)

            def group_products(it, first):
                for q in range(4):
                    hidden(it * 4 + (NS + q), q)
                    if not first or q:
                        outputs(it * 4 + (q - 1), (q - 1) % 2)
            group_products(0, True)
            with pe.Fori(1, NG // 4) as it:
                group_products(it, False)
            outputs(NG - 1, 1)

        @block.scalar
        def _(act):
            A = nc.scalar.activation
            chain = [0]

            def link(ins):
                chain[0] += 1
                ins.then_inc(s_rc, 1)
                act.wait_ge(s_rc, chain[0])

            def cast():
              act.wait_ge(s_raw, 16)
              act.wait_ge(s_const, 16)
              for dst, name, n in ((msf, "msf", 128), (mtf, "mtf", 128), (msd, "msd", 512), (mtd, "mtd", 512),
                                 (cnt, "cnt", 512)):
                c = CN[name] - NKEEP
                nc.scalar.copy(dst, craw[:, c:c + n]).then_inc(s_cast, 1)
              nc.scalar.copy(idb, ident).then_inc(s_cast, 1)

            def evac(n):
                kind, i, _ = PROJ[n]
                act.wait_ge(s_proj, n + 1)
                ps = pj[n % 2]
                if n in TEMPS:
                    j = TEMPS[n]
                    dst = ebuf[:, j % NE, :]
                    if j >= NE:
                        act.wait_ge(s_post, POST_OF[j - NE])
                    if kind == "conv" and i == 0:
                        act.wait_ge(s_tab, 1)
                    if kind == "r" and i == 0:
                        act.wait_ge(s_par, 16)
                    if kind == "gate" or (kind == "conv" and i % 4 == 3):
                        A(dst, ps[:, :], ACT.Silu).then_inc(s_evac, 1)
                    elif kind == "r":
                        A(dst, ps[:, :], ACT.Sigmoid, bias=col("bg", i)).then_inc(s_evac, 1)
                    elif kind == "wf":
                        A(dst[0:8, :], ps[0:8, :], ACT.Identity, bias=col("bf", 0, 0, 8)).then_inc(s_evac, 1)
                    else:
                        nc.scalar.copy(dst, ps[:, :]).then_inc(s_evac, 1)
                elif kind == "lat":
                    nc.scalar.copy(lat[:, i, :], ps[:, :]).then_inc(s_evac, 1)
                elif kind == "kpe":
                    nc.scalar.copy(lat[NOPE:QKD, 5, :], ps[NOPE:QKD, :]).then_inc(s_evac, 1)
                elif kind == "uq":
                    nc.scalar.copy(qm1[0:QKD, i % 2, :], ps[0:QKD, :]).then_inc(s_evac, 1)
                elif kind == "uk":
                    if i == 0:
                        act.wait_ge(s_evac, pi[("kpe", 0)] + 1)
                    nc.scalar.copy(km1[NOPE:QKD, i % 2, :], lat[NOPE:QKD, 5, :])
                    nc.scalar.copy(km1[0:NOPE, i % 2, :], ps[0:NOPE, :]).then_inc(s_evac, 1)
                elif kind in ("uv", "v2"):
                    if kind == "uv":
                        act.wait_ge(s_init, 1)
                    if kind == "v2":
                        act.wait_ge(s_init2, 6 if i >= TB else 5)
                    V = VB if i >= TB else VA
                    src = ps[:, :].rearrange("p (h d) -> p h d", h=HEADS)
                    nc.scalar.copy(V[:, i % TB, 0:HEADS:2, 0:DH], src[:, 0:HEADS:2, :])
                    nc.scalar.copy(V[:, i % TB, 1:HEADS:2, DH:P], src[:, 1:HEADS:2, :]).then_inc(s_evac, 1)
                elif kind == "gate":
                    A(memgate[:, i - 4, :], ps[:, :], ACT.Silu).then_inc(s_evac, 1)
                elif kind == "qm":
                    nc.scalar.copy(mq[:, i, :], ps[:, :]).then_inc(s_evac, 1)
                elif kind == "mk":
                    nc.scalar.copy(mkT[:, i, :], ps[:, 0:MEM]).then_inc(s_evac, 1)
                elif kind == "mv":
                    nc.scalar.copy(mv[:, i, :], ps[:, :]).then_inc(s_evac, 1)
                elif kind == "qk2":
                    p, s = i // 2, i % 2
                    if i == 0:
                        act.wait_ge(s_init2, 6)
                    dst = (Q2, K2)[s]
                    scale = (DH ** -0.5, 1.0)[s]
                    for u in range(2):
                        ins = A(dst[0:DH, (2 * p + u) % 4, :], ps[u * DH:(u + 1) * DH, :], ACT.Copy, scale=scale)
                    ins.then_inc(s_evac, 1)
                else:
                    assert kind == "wq"
                    if i >= 4:
                        act.wait_ge(s_qs, i - 3)
                    nc.scalar.copy(pq[:, i % 4, :], ps[:, :]).then_inc(s_evac, 1)

            def high_weights(u):
                kind, _, loads = PROJ[UNITS[u]]
                n = unit_size(u)
                L = loads[0]
                act.wait_ge(s_w[L % NW], 16 * (L // NW + 1))
                if came_before[UNITS[u]] is not None:
                    act.wait_ge(s_proj, came_before[UNITS[u]] + 1)
                nc.scalar.copy(flat(u, 0)[:, 0:n], ring[:, L % NW, 0:n]).then_inc(s_whi, 1)

            def square_summed(j):
                key = max((k for k in sq0 if sq0[k] <= j), key=lambda k: sq0[k])
                if j == sq0[key] + norm_shape(key)[0] - 1:
                    act.wait_ge(s_aux, auxi[("norm", key)] + 1)
                else:
                    act.wait_ge(s_squsd, j + 1 - sum(1 for k in sq0 if sq0[k] + norm_shape(k)[0] - 1 <= j))

            def squares(key):
                nk, width, N = norm_shape(key)
                rows = min(width, P)
                for k in range(nk):
                    j = sq0[key] + k
                    if key == "x":
                        act.wait_ge(s_x[k // 2], 16)
                        src = xT[:, k, :]
                    elif key == "x2":
                        act.wait_ge(s_post, post_no[("res", k)])
                        src = xT[:, k, :]
                    elif key == "h2":
                        act.wait_ge(s_post, post_no[("res2", k)])
                        src = xT[:, k, :]
                    elif key == "ql":
                        act.wait_ge(s_evac, pi[("lat", k)] + 1)
                        src = lat[:, k, :]
                    elif key == "kvl":
                        act.wait_ge(s_evac, pi[("lat", QL + k)] + 1)
                        src = lat[:, QL + k, :]
                    elif key == "mem":
                        act.wait_ge(s_mem, 16)
                        src = memT[:, k, :]
                    elif key.startswith("mq"):
                        act.wait_ge(s_evac, pi[("qm", int(key[2:]))] + 1)
                        src = mq[:, int(key[2:]), :]
                    elif key.startswith("mk"):
                        act.wait_ge(s_evac, pi[("mk", int(key[2:]))] + 1)
                        src = mkT[:, int(key[2:]), :]
                    else:
                        h = int(key[1:])
                        act.wait_ge(s_evac, pi[("u" + key[0], h)] + 1)
                        src = (qm1 if key[0] == "q" else km1)[0:QKD, h % 2, :]
                    if j >= NQ:
                        square_summed(j - NQ)
                    A(sq[0:rows, j % NQ, 0:N], src, ACT.Square, scale=width ** -0.5).then_inc(s_sq, 1)

            def norm(key):
                nk, width, N = norm_shape(key)
                rows = min(width, P)
                if ("sq", key) not in STEPS:
                    squares(key)
                i, j = auxi[("norm", key)], norm_no[key]
                act.wait_ge(s_aux, i + 1)
                if j > 1:
                    act.wait_ge(s_norm, j - 1)
                r = rs[0:rows, 0:N]
                if key == "x":
                    act.wait_ge(s_par, 16)
                A(r, ax[i % 2][0:rows, 0:N], ACT.Ln, bias=col("eps", 0, 0, rows)).then_inc(s_auxfree[i % 2], 1)
                act.wait_ge(s_auxfree[i % 2], i // 2 + 1)
                A(r, r, ACT.Exp, scale=-0.5).then_inc(s_rs, 1)

            def rope_tables():
                act.wait_ge(s_cos, 1)
                A(sinT[NOPE:QKD, :], rtmp[NOPE:QKD, :], ACT.Sin).then_inc(s_tab, 1)
                act.wait_ge(s_cos, 2)
                A(cosT[NOPE:QKD, :], cosT[NOPE:QKD, :], ACT.Sin).then_inc(s_tab, 1)

            def M(a):
                i = auxi[("M", a)]
                act.wait_ge(s_aux, i + 1)
                if a == 0:
                    act.wait_ge(s_init, 2)
                if a < HEADS:
                    dst = qm1[QKD:QKD + 1, a % 2, :]
                elif a < 12:
                    dst = mrow[0:1, :]
                else:
                    dst = Q2[QKD:QKD + 1, (a - 12) % 4, :]
                nc.scalar.copy(dst, ax[i % 2][0:1, :]).then_inc(s_auxfree[i % 2], 1)

            def T_(a, kb):
                act.wait_ge(s_T, t_no[("T", a, kb)])
                if a > 0:
                    act.wait_ge(s_PV, pv_no[(a - 1, min(kb, n_keys(a - 1) - 1))])
                c0 = q0(a, kb)
                scale = QKD ** -0.5 if a < HEADS else P ** -0.5 if a < 12 else 1.0
                n = tile_no[("T", a, kb)]
                A(PT[:, kb, c0:T], scb[n % 3][:, c0:T], ACT.Exp, scale=scale).then_inc(s_P, 1)

            def forget(n):
                act.wait_ge(s_fmag, 1)
                link(A(zsm[0:8, 1, :], zsm[0:8, 1, :], ACT.Exp))
                A(zsm[0:8, 1, :], zsm[0:8, 1, :], ACT.Ln, bias=1.0).then_inc(s_fch, 1)

            for s in STEPS:
                if s[0] == "proj":
                    evac(s[1])
                    for u in split_after.get(s[1], []):
                        high_weights(u)
                elif s[0] == "sq":
                    squares(s[1])
                elif s[0] == "norm":
                    norm(s[1])
                elif s[0] == "rope_tables":
                    rope_tables()
                elif s[0] == "cast":
                    cast()
                elif s[0] == "M":
                    M(s[1])
                elif s[0] == "T":
                    T_(s[1], s[2])
                elif s[0] == "post" and s[1] == "forget":
                    forget(s[3][0])
                elif s[0] == "split":
                    for k in range(s[2], s[3]):
                        if s[1] == "b":
                            act.wait_ge(s_post, post_no[(("gate", "conv", "mgate")[k // 4], k % 4)])
                            nc.scalar.copy(oh[k // 8][:, k % 8, :], oT[:, k, :]).then_inc(s_hh, 1)
                            continue
                        if s[1] == "y":
                            act.wait_ge(s_post, post_no[("rb", 3 * k + 2)])
                            act.wait_ge(s_proj, pi[("r", 3 * KD - 1)] + 1)
                        else:
                            act.wait_ge(s_O, O_no[12 + 2 * k + 1])
                            act.wait_ge(s_proj, pi[("qk2", ATT2 - 1)] + 1)
                        nc.scalar.copy(hh[:, k, :], (yT if s[1] == "y" else oT)[:, k, :]).then_inc(s_hh, 1)
                elif s[0] == "high_h":
                    if s[1] == "x":
                        high_weights(0)
                    for k in range(KD):
                        if k < KD - 1:
                            act.wait_ge(s_hk, (KD - 1) * H_NO[s[1]] + k + 1)
                        else:
                            act.wait_ge(s_norm, norm_no[s[1]])
                        nc.scalar.copy(hh[:, k, :], hT[:, k, :]).then_inc(s_hh, 1)
                    if s[1] == "x":
                        high_weights(1)
                elif s[0] == "keys":
                    i = s[1]
                    act.wait_ge(s_qs, i + 1)
                    if i >= 4:
                        act.wait_ge(s_half, i - 3)
                    nc.scalar.copy(sc[:, i % 4, :], bank[3 + i % 4][:, :]).then_inc(s_qe, 1)

            def high_u(e, slot):
                act.wait_ge(s_u[slot], (e - slot) * 4 + 16)
                at_least(act, s_hid, e - 1)
                nc.scalar.copy(U2[:, slot % 2, 0].rearrange("p k e -> p (k e)"), UR[:, slot, :]).then_inc(s_uhi, 1)

            def kept_tile(e, slot):
                act.wait_ge(s_hid, e + 1)
                at_least(act, s_kept[slot], (e - slot) * 4)
                A(AF[:, slot, :], bank[slot % 2][:, :], ACT.Gelu).then_inc(s_gelu, 1)
                high_u(e + 2, (slot + 2) % 4)

            def copy_group(tb, n, u, t):
                act.wait_ge(s_gm[u], n + 1)
                nc.scalar.copy(stage[:, :, bass.ds(t, 4)].rearrange("p i t -> p t i"),
                               bank[2 + u][:, :].rearrange("p (t i) -> p t i", t=4)).then_inc(s_ge[u], 1)

            high_u(0, 0)
            high_u(1, 1)
            act.wait_ge(s_hx, 1)
            for b in range(8):
                nc.scalar.copy(xT[:, b, :], bank[b][:, :]).then_inc(s_hxc, 1)
            for tb in range(TB):
                for i in range(FREE[tb]):
                    if i == 5:
                        act.wait_ge(s_sm, tb + 1)
                        A(ee, ee, ACT.Exp).then_inc(s_ex, 1)
                    if i == FREE[tb] - 1:
                        act.wait_ge(s_lt, tb + 1)
                        nc.scalar.copy(lists[:, :, tb * P:(tb + 1) * P],
                                       bank[4][:, 0:3 * P].rearrange("p (w t) -> p w t", w=3)).then_inc(s_ltc, 1)
                    kept_tile(START[tb] + i, (START[tb] + i) % 4)
                if tb:
                    act.wait_ge(s_gst, 128 * tb)

                def with_gates(it, _):
                    for u in range(4):
                        for k in range(4):
                            copy_group(tb, it * 8 + (16 * tb + 2 * u + k // 2), k % 2, it * 64 + (16 * u + 4 * k))
                        kept_tile(it * 4 + (START[tb] + FREE[tb] + u), (START[tb] + FREE[tb] + u) % 4)
                rounds(act, GATED // 4, with_gates, first=tb == 0)
            for e in range(START[TB], NS):
                kept_tile(e, e % 4)

            for u in range(2):
                act.wait_ge(s_kept[u], 16 * NS // 4)
            act.wait_ge(s_gst_first, 64)

            def expert_groups(it, last):
                for q in range(4):
                    g, half = it * 4 + q, q % 2
                    if isinstance(g, int) and g == 1:
                        for u in range(2, 4):
                            act.wait_ge(s_kept[u], 16 * NS // 4)
                        act.wait_ge(s_gst, 128 * TB - 64)
                    act.wait_ge(s_v[half], it * 32 + (16 * (q // 2) + 16))
                    at_least(act, s_eo, g * 8 - 8)
                    for w in range(2):
                        nc.scalar.copy(V2[:, 2 * half + w, 0], VR[:, 2 * half + w, :]).then_inc(s_vhi, 1)
                    act.wait_ge(s_act, g * 2 + 1)
                    nc.scalar.copy(A2[:, 2 * half, 0], AF[:, 2 * half, :]).then_inc(s_ahi, 1)
                    act.wait_ge(s_hid, g + (NS + 1))
                    at_least(act, s_alo, g * 2 - 2)
                    A(AF[:, 2 * half + 1, :], bank[q % 2][:, :], ACT.Gelu).then_inc(s_gelu, 1)
                    if not last or q < 2:
                        high_u(g + (NS + 2), (q + 2) % 4)
                    act.wait_ge(s_act, g * 2 + 2)
                    nc.scalar.copy(A2[:, 2 * half + 1, 0], AF[:, 2 * half + 1, :]).then_inc(s_ahi, 1)
            rounds(act, NG // 4, expert_groups, first=True, last=True)
            for tb in range(TB):
                act.wait_ge(s_ea, (NG - 1) * 8 + 2 * tb + 2)
                if tb:
                    act.wait_ge(s_fsq, tb)
                A(fsq, xT[:, 2 * tb:2 * tb + 2, :].rearrange("p k n -> p (k n)"), ACT.Square,
                  scale=D ** -0.5, accum_out=fss[:, tb:tb + 1]).then_inc(s_fsq, 1)
            act.wait_ge(s_fsq, TB)
            A(fss[:, 4:4 + TB], fss[:, 0:TB], ACT.Ln, bias=col("eps")).then_inc(s_fsq, 1)
            act.wait_ge(s_fsq, TB + 1)
            A(fss[:, 8:8 + TB], fss[:, 4:4 + TB], ACT.Exp, scale=-0.5).then_inc(s_fsq, 1)

        @block.vector
        def _(dve):
            V = nc.vector
            chain = [0]

            def link(ins):
                chain[0] += 1
                ins.then_inc(s_d, 1)
                dve.wait_ge(s_d, chain[0])

            ended = {}

            def end(ins, s, name):
                ended[name] = (s, ended.pop(name, (s, 0))[1] + 1)
                ins.then_inc(s, 1)

            def settle():
                if ended:
                    dve.wait_ge(*list(ended.values())[-1])

            dve.wait_ge(s_par, 16)
            dve.wait_ge(s_const, 16)

            def norm(key):
                nk, width, N = norm_shape(key)
                rows = min(width, P)
                j = norm_no[key]
                dve.wait_ge(s_rs, j)
                r = rs[0:rows, 0:N]
                for k in range(nk):
                    if key == "x":
                        dst, src, g = hT[:, k, :], xT[:, k, :], col("norm", k)
                    elif key in ("x2", "h2"):
                        dst, src, g = hT[:, k, :], xT[:, k, :], col({"x2": "norm1", "h2": "norm2"}[key], k)
                    elif key == "ql":
                        dst = src = lat[:, k, :]
                        g = col("qn", k)
                    elif key == "kvl":
                        dst = src = lat[:, QL + k, :]
                        g = col("kvn", k)
                    elif key == "mem":
                        dst = src = memT[:, k, :]
                        g = col("memn", k)
                    elif key.startswith("mq"):
                        dst = src = mq[:, int(key[2:]), :]
                        g = col("mq")
                    elif key.startswith("mk"):
                        dst = src = mkT[:, int(key[2:]), :]
                        g = col("mk")
                    else:
                        dst = src = (qm1 if key[0] == "q" else km1)[0:QKD, int(key[1:]) % 2, :]
                        g = col(key[0] + "h", 0, 0, QKD)
                    ins = V.scalar_tensor_tensor(dst, src, g, r, ALU.mult, ALU.mult)
                    if key in H_NO and k < KD - 1:
                        ins.then_inc(s_hk, 1)
                    if key in ("x", "h2") and k == KD - 1:
                        end(ins, s_norm, "s_norm")
                    if key in ("x", "h2") and k > 0:
                        low_h(key, k - 1)
                if key in ("x", "h2"):
                    low_h(key, KD - 1)
                else:
                    end(ins, s_norm, "s_norm")

            def low_part(key, k):
                src, low, high = {"b": (oT, ol, oh[k // 8][:, k % 8, :]), "y": (yT, yl, hh[:, k % 8, :]),
                                  "o": (oT, ol, hh[:, k % 8, :])}[key]
                dve.wait_ge(s_hh, parts0[key] + k + 1)
                V.tensor_tensor(low[:, k, :], src[:, k, :], high.bitcast(F32), ALU.subtract).then_inc(s_hl, 1)

            def low_h(phase, k):
                dve.wait_ge(s_hh, parts0[phase] + k + 1)
                V.tensor_tensor(hl[:, k, :], hT[:, k, :], hh[:, k, :].bitcast(F32), ALU.subtract).then_inc(s_hl, 1)

            def rope_tables():
                R = slice(NOPE, QKD)
                dve.wait_ge(s_pos, 16)
                dve.wait_ge(s_cast, 6)
                ang, kk, t1, t2 = zsm[R, 0, :], dtmp[R, :], rtmp[R, :], cosT[R, :]
                magic = 12582912.0
                c1 = 6.28125
                c2 = float(np.float32(np.floor((2 * np.pi - c1) * 2 ** 21) / 2 ** 21))
                c3 = float(2 * np.pi - c1 - c2)
                link(V.tensor_copy(ang, pos_i[R, :]))
                link(V.tensor_scalar(ang, ang, col("invf", 0, NOPE, QKD), None, ALU.mult))
                for which, dst in ((0, t1), (1, t2)):
                    if which:
                        link(V.tensor_scalar(kk, ang, 1.0 / (2 * np.pi), 0.25, ALU.mult, ALU.add))
                    else:
                        link(V.tensor_scalar(kk, ang, 1.0 / (2 * np.pi), None, ALU.mult))
                    link(V.tensor_scalar(kk, kk, magic, None, ALU.add))
                    link(V.tensor_scalar(kk, kk, magic, None, ALU.subtract))
                    link(V.scalar_tensor_tensor(dst, kk, -c1, ang, ALU.mult, ALU.add))
                    link(V.scalar_tensor_tensor(dst, kk, -c2, dst, ALU.mult, ALU.add))
                    link(V.scalar_tensor_tensor(dst, kk, -c3, dst, ALU.mult, ALU.add))
                    if which:
                        link(V.tensor_scalar(dst, dst, np.pi / 2, None, ALU.add))
                    V.tensor_scalar(dst, dst, 3.1415925, -3.1415925, ALU.min, ALU.max).then_inc(s_cos, 1)

            def rope(h, which):
                i = auxi[("rope", h, which)]
                R = slice(NOPE, QKD)
                x = (qm1, km1)[which][R, h % 2, :]
                dve.wait_ge(s_tab, 2)
                dve.wait_ge(s_aux, i + 1)
                V.tensor_tensor(rtmp[R, :], ax[i % 2][R, :], sinT[R, :], ALU.mult).then_inc(s_auxfree[i % 2], 1)
                link(V.tensor_tensor(x, x, cosT[R, :], ALU.mult))
                end(V.tensor_tensor(x, x, rtmp[R, :], ALU.add), s_rope, "s_rope")

            def S(a, qb):
                n = tile_no[("S", a, qb)]
                dve.wait_ge(s_S, s_no[("S", a, qb)])
                N = (qb + 1) * P if a >= 12 else n_keys(a) * P
                c = 4 * (a % 2) + qb
                V.tensor_reduce(mx[:, c:c + 1], scb[n % 3][:, 0:N], AX.X, ALU.max).then_inc(s_max, 1)

            def count(a, kb):
                dve.wait_ge(s_P, t_no[("T", a, kb)])
                c0 = q0(a, kb)
                V.tensor_tensor(PT[:, kb, c0:T], PT[:, kb, c0:T], cnt[:, 0:T - c0], ALU.mult).then_inc(s_Pc, 1)

            def O(a):
                dve.wait_ge(s_PV, pv_no[(a, n_keys(a) - 1)])
                if HEADS <= a < 12:
                    i = auxi[("den", a)]
                    V.reciprocal(dtmp, ax[i % 2][:, :]).then_inc(s_auxfree[i % 2], 1)
                    dve.wait_ge(s_auxfree[i % 2], i // 2 + 1)
                    end(V.tensor_tensor(oT[:, a, :], ob[:, :], dtmp, ALU.mult), s_O, "s_O")
                    return
                h = a if a < HEADS else a - 12
                r0 = DH * (h % 2)
                d0 = DH - r0
                link(V.reciprocal(dtmp[r0:r0 + DH, :], ob[d0:d0 + DH, :]))
                end(V.tensor_tensor(oT[r0:r0 + DH, h // 2, :], ob[r0:r0 + DH, :], dtmp[r0:r0 + DH, :],
                                ALU.mult), s_O, "s_O")

            def post(kind, i, ns):
                for n in ns:
                    dve.wait_ge(s_evac, n + 1)
                e = [ebuf[:, TEMPS[n] % NE, :] for n in ns]
                if kind == "conv":
                    c, u, b, g = e
                    if i == 0:
                        dve.wait_ge(s_init, 3)
                    z, w = zc, cwork
                    link(V.tensor_tensor(z[:, 1:T + 1], c, u, ALU.mult))
                    link(V.tensor_scalar(w[:, 0, :], z[:, 0:T], col("cw", i), None, ALU.mult))
                    link(V.scalar_tensor_tensor(w[:, 0, :], z[:, 1:T + 1], col("cw", 4 + i), w[:, 0, :],
                                                ALU.mult, ALU.add))
                    link(V.scalar_tensor_tensor(w[:, 0, :], z[:, 2:T + 2], col("cw", 8 + i), w[:, 0, :],
                                                ALU.mult, ALU.add))
                    link(V.scalar_tensor_tensor(w[:, 0, :], w[:, 0, :], col("cb", i), b, ALU.add, ALU.mult))
                    end(V.tensor_tensor(oT[:, 4 + i, :], w[:, 0, :], g, ALU.mult), s_post, "s_post")
                elif kind == "gate":
                    dve.wait_ge(s_O, HEADS)
                    end(V.tensor_tensor(oT[:, i, :], oT[:, i, :], e[0], ALU.mult), s_post, "s_post")
                elif kind == "mgate":
                    dve.wait_ge(s_O, HEADS + MEM_HEADS)
                    dve.wait_ge(s_evac, pi[("gate", 7)] + 1)
                    end(V.tensor_tensor(oT[:, 8 + i, :], oT[:, 8 + i, :], memgate[:, i, :], ALU.mult), s_post, "s_post")
                elif kind == "rb":
                    f, b = i // 3, i % 3
                    if b == 0:
                        end(V.tensor_tensor(yT[:, f, :], e[0], e[1], ALU.mult), s_post, "s_post")
                    else:
                        link(V.tensor_tensor(dtmp, e[0], e[1], ALU.mult))
                        end(V.tensor_tensor(yT[:, f, :], yT[:, f, :], dtmp, ALU.add), s_post, "s_post")
                    dve.wait_ge(s_post, post_no[("rb", i)])
                elif kind in ("res", "res2"):
                    end(V.tensor_tensor(xT[:, i, :], xT[:, i, :], e[0], ALU.add), s_post, "s_post")
                else:
                    assert kind == "forget"
                    z = e[0][0:8, :]
                    z0, z1, z2 = zsm[0:8, 0, :], zsm[0:8, 1, :], zsm[0:8, 2, :]
                    link(V.tensor_scalar(z0, z, 0.0, None, ALU.max))
                    V.scalar_tensor_tensor(z1, z, 0.0, z0, ALU.min, ALU.subtract).then_inc(s_fmag, 1)
                    dve.wait_ge(s_fch, 1)
                    link(V.scalar_tensor_tensor(z0, z, 0.0, z1, ALU.min, ALU.subtract))
                    link(V.tensor_scalar(z0, z0, -1.0, None, ALU.mult))
                    link(V.memset(z1, 1.0))
                    end(V.tensor_tensor_scan(z2, z1, z0, 0.0, ALU.mult, ALU.add), s_post, "s_post")

            def sorted_half(i):
                dve.wait_ge(s_qe, i + 1)
                b = sc[:, i % 4, :].rearrange("p (t k) -> p t k", t=TB)
                for tb in range(TB):
                    ins = V.max(tva[:, tb, i, 0:8], b[:, tb, :])
                link(ins)
                for tb in range(TB):
                    ins = V.max_index(tia[:, tb, i, 0:8], tva[:, tb, i, 0:8], b[:, tb, :])
                link(ins)
                for tb in range(TB):
                    ins = V.match_replace(b[:, tb, :], tva[:, tb, i, 0:8], b[:, tb, :], -BIG)
                link(ins)
                for tb in range(TB):
                    ins = V.max(tva[:, tb, i, 8:16], b[:, tb, :])
                link(ins)
                for tb in range(TB):
                    ins = V.max_index(tia[:, tb, i, 8:16], tva[:, tb, i, 8:16], b[:, tb, :])
                end(ins, s_half, "s_half")

            for s in STEPS:
                if s[0] in ("norm", "rope", "O", "post", "keys"):
                    settle()
                if s[0] == "norm":
                    norm(s[1])
                elif s[0] == "split":
                    for k in range(s[2], s[3]):
                        low_part(s[1], k)
                elif s[0] == "low_h":
                    for k in range(KD):
                        if k < KD - 2:
                            dve.wait_ge(s_chunk, 3 + k // 2 + 1)
                        else:
                            dve.wait_ge(s_proj, pi[("v2", 2 * TB - 1)] + 1)
                        low_h("x2", k)
                elif s[0] == "rope_tables":
                    rope_tables()
                elif s[0] == "rope":
                    rope(s[1], s[2])
                elif s[0] == "S":
                    S(s[1], s[2])
                elif s[0] == "T" and s[1] >= 20:
                    count(s[1], s[2])
                elif s[0] == "O":
                    O(s[1])
                elif s[0] == "post":
                    post(s[1], s[2], s[3])
                elif s[0] == "keys":
                    sorted_half(s[1])

            def retrieve(tb):
                tv, ti = tva[:, tb], tia[:, tb]
                tvh = tv.rearrange("p (h w) k -> p h w k", w=2)
                c4 = cand.rearrange("p (h a b) -> p h a b", h=8, a=16)
                ch = cand.rearrange("p (h n) -> p h n", h=8)
                link(V.tensor_tensor(c4, tvh[:, :, 0, :].unsqueeze(3).to_broadcast([P, 8, 16, 16]),
                                     tvh[:, :, 1, :].unsqueeze(2).to_broadcast([P, 8, 16, 16]), ALU.add))
                link(V.tensor_copy(tif, ti.rearrange("p h k -> p (h k)")))
                for h in range(8):
                    ins = V.max(cs[:, h, 0:8], ch[:, h, :])
                link(ins)
                for h in range(8):
                    ins = V.max_index(ci[:, h, 0:8], cs[:, h, 0:8], ch[:, h, :])
                link(ins)
                for h in range(8):
                    ins = V.match_replace(ch[:, h, :], cs[:, h, 0:8], ch[:, h, :], -BIG)
                link(ins)
                for h in range(8):
                    ins = V.max(cs[:, h, 8:16], ch[:, h, :])
                link(ins)
                for h in range(8):
                    ins = V.max_index(ci[:, h, 8:16], cs[:, h, 8:16], ch[:, h, :])
                link(ins)
                e3 = ee.rearrange("p (h k) -> p h k", h=8)
                if tb >= 1:
                    dve.wait_ge(s_lt, tb)
                V.tensor_tensor(e3, cs, cs[:, :, 0:1].to_broadcast([P, 8, 16]), ALU.subtract).then_inc(s_sm, 1)
                cif = ci.rearrange("p h k -> p (h k)")
                for w in range(2):
                    if w == 0:
                        link(V.tensor_scalar(ca, cif, 4, None, ALU.logical_shift_right))
                    else:
                        link(V.tensor_scalar(ca, cif, 15, None, ALU.bitwise_and))
                    link(V.tensor_copy(cbf[:, w, :], ca))
                    q3 = eq.rearrange("p (r m) -> p r m", m=16)
                    q4 = eq.rearrange("p (h k m) -> p h k m", h=8, k=16)
                    tf = tif.rearrange("p (h w m) -> p h w m", h=8, w=2)[:, :, w, :]
                    link(V.tensor_tensor(q3, cbf[:, w, :].unsqueeze(2).to_broadcast([P, P, 16]),
                                         iota16.unsqueeze(1).to_broadcast([P, P, 16]), ALU.is_equal))
                    link(V.tensor_tensor(q4, q4, tf.unsqueeze(2).to_broadcast([P, 8, 16, 16]), ALU.mult))
                    link(V.tensor_reduce(sel[:, w, :], q3, AX.X, ALU.add))
                dve.wait_ge(s_ex, tb + 1)
                link(V.tensor_reduce(es[:, 0:8], e3, AX.X, ALU.add))
                link(V.reciprocal(es[:, 8:16], es[:, 0:8]))
                V.tensor_tensor(sel[:, 2, :].rearrange("p (h k) -> p h k", h=8), e3,
                                es[:, 8:16].unsqueeze(2).to_broadcast([P, 8, 16]), ALU.mult).then_inc(s_tk, 1)

            def onehots(n, u, t):
                at_least(dve, s_gm[u], n)
                for k in range(4):
                    V.tensor_scalar(ohring[:, u, 0, k, :], iota, lists[:, 0, bass.ds(t + k, 1)],
                                    lists[:, 2, bass.ds(t + k, 1)], ALU.is_equal, ALU.mult)
                    ins = V.tensor_scalar(ohring[:, u, 1, k, :], iota, lists[:, 1, bass.ds(t + k, 1)], None,
                                          ALU.is_equal)
                ins.then_inc(s_oh, 1)

            for tb in range(TB):
                retrieve(tb)
                dve.wait_ge(s_ltc, tb + 1)
                rounds(dve, P // 8, lambda it, _: [
                    onehots(it + 16 * tb, u, it * 8 + (P * tb + 4 * u)) for u in range(2)], first=tb == 0)

            def gated(g, half, it, q):
                for w in range(2):
                    slot = 2 * half + w
                    if w == 0:
                        dve.wait_ge(s_g[half], it * 32 + (16 * (q // 2) + 16))
                        dve.wait_ge(s_h[half], it * 32 + (16 * (q // 2) + 16))
                    else:
                        dve.wait_ge(s_gelu, g + (NS + 1))
                    V.tensor_tensor(AF[:, slot, :], AF[:, slot, :], GR[:, slot, :], ALU.mult).then_inc(s_act, 1)
                    dve.wait_ge(s_ahi, g * 2 + (w + 1))
                    V.tensor_tensor(A2[:, slot, 1], AF[:, slot, :], A2[:, slot, 0].bitcast(F32), ALU.subtract)\
                        .then_inc(s_alo, 1)

            def add_outputs(g):
                for u in range(8):
                    dve.wait_ge(s_eo, g * 8 + (u + 1))
                    V.tensor_tensor(xT[:, u, :], xT[:, u, :], bank[2 + u % 4][:, :], ALU.add).then_inc(s_ea, 1)

            dve.wait_ge(s_hxc, 8)

            def expert_groups(it, first):
                for q in range(4):
                    gated(it * 4 + q, q % 2, it, q)
                    if not first or q:
                        add_outputs(it * 4 + (q - 1))
            expert_groups(0, True)
            with dve.Fori(1, NG // 4) as it:
                expert_groups(it, False)
            add_outputs(NG - 1)
            dve.wait_ge(s_gf, 16)
            for tb in range(TB):
                dve.wait_ge(s_fsq, TB + 2)
                row = xT[:, 2 * tb:2 * tb + 2, :].rearrange("p k n -> p (k n)")
                V.scalar_tensor_tensor(row, row, fss[:, 8 + tb:9 + tb], gf, ALU.mult, ALU.mult).then_inc(s_fin, 1)


def _tiles(np_, w, cols_per_tile):
    K, F = w.shape
    t = w.reshape(K // 128, 128, F // cols_per_tile, cols_per_tile).transpose(2, 1, 0, 3)
    return np_.ascontiguousarray(t).reshape(F // cols_per_tile, 128, -1)


def _rows(np_, w, per):
    K, F = w.shape
    t = w.reshape(K // 128 // per, per, 128, F).transpose(0, 2, 1, 3)
    return np_.ascontiguousarray(t).reshape(K // 128 // per, 128, per * F)


def _cols(np_, v):
    return np_.ascontiguousarray(v.reshape(-1, 128).T)


def _pad(np_, v, n=128):
    c = np_.zeros((n, 1), v.dtype)
    c[:v.shape[0], 0] = v
    return c


def _constants(np_):
    f = np_.float32
    d = np_.arange(128)
    eye = np_.eye(128, dtype=f)
    rot = np_.zeros((128, 128), f)
    for i in range(HALF):
        rot[NOPE + HALF + i, NOPE + i] = -1.0
        rot[NOPE + i, NOPE + HALF + i] = 1.0
    iota = np_.broadcast_to(np_.arange(128, dtype=f), (128, 128))
    iota16 = iota[:, :16]
    msf = np_.where(d[None, :] <= d[:, None], 0.0, NEG).astype(f)
    mtf = np_.ascontiguousarray(msf.T)
    dq = d[:, None] - (np_.arange(512)[None, :] - 384)
    dt = np_.arange(512)[None, :] - d[:, None]

    def patterns(x):
        return ((x >= 0) & (x <= 128)).astype(int) + ((x >= 0) & (x % 4 == 0)) + ((x >= 0) & (x % 16 == 0))

    msd = np_.where(patterns(dq) > 0, 0.0, NEG).astype(f)
    mtd = np_.where(patterns(dt) > 0, 0.0, NEG).astype(f)
    return np_.ascontiguousarray(np_.concatenate(
        [eye, -eye, np_.ones((128, 128), f), rot, iota, iota16, msf, mtf, msd, mtd, patterns(dt).astype(f)], axis=1))


def kernel(**inputs):
    import numpy as _np
    import concourse.bacc as _bacc
    from concourse import mybir as _mybir
    from concourse.bass_utils import run_bass_kernel_spmd as _run

    a = {k: _np.asarray(v) for k, v in inputs.items()}
    w = a["w_in"][0]
    at = _np.cumsum([0, 384, 256, 32, 512, 512, 512, 512, 512, 512, 512, 3072])
    part = {k: w[:, at[i]:at[i + 1]] for i, k in enumerate(
        ("ql", "kvl", "kpe", "cb", "cc", "cu", "qm", "ga", "gc", "gm", "r"))}
    tl = lambda x, c=128: _tiles(_np, x, c)
    cv = _np.stack([tl(part[k]) for k in ("cc", "cu", "cb", "gc")], axis=1).reshape(16, 128, -1)
    kpe = _np.concatenate([_np.zeros((1024, 64), w.dtype), part["kpe"]], axis=1)
    ukv = a["w_ukv"][0].reshape(256, 8, 128)
    mkv = a["w_mkv"][0].reshape(1024, 4, 256)
    br = _np.stack([tl(a[k][0]) for k in ("w_br_attn", "w_br_conv", "w_br_mem")], axis=1).reshape(24, 128, -1)
    r = tl(part["r"]).reshape(3, 8, 128, -1).transpose(1, 0, 2, 3).reshape(24, 128, -1)
    w2 = a["w_in_2"][0]
    fq, fk, fv, wf, dq, dk, dv = (w2[:, i:j] for i, j in ((0, 512), (512, 1024), (1024, 1536), (1536, 1544),
                                                          (1544, 2056), (2056, 2568), (2568, 3080)))
    qk2 = _np.concatenate([_np.stack([tl(q), tl(k)], axis=1).reshape(8, 128, -1) for q, k in ((fq, fk), (dq, dk))])
    invf = (_np.float32(10000.0) ** (-_np.arange(0, 32, 2, dtype=_np.float32) / _np.float32(32))).astype(_np.float32)
    col = lambda k: _cols(_np, a[k][0])
    pad = lambda v: _pad(_np, v)
    table = _np.concatenate([
        col("norm_g"), col("q_norm_g"), col("kv_norm_g"), pad(a["q_head_g"][0]), pad(a["k_head_g"][0]),
        a["conv_w"][0].reshape(12, 128).T, col("conv_b"), col("mem_norm_g"), col("mem_q_g"), col("mem_k_g"),
        a["b_gate"][0].reshape(3, 8, 128).transpose(1, 0, 2).reshape(24, 128).T, col("norm1_g_2"),
        col("norm2_g_2"), pad(a["b_forget_2"][0]),
        pad(_np.concatenate([_np.zeros(64, _np.float32), invf, invf])),
        _np.full((128, 1), EPS, _np.float32)], axis=1)
    slopes = 2.0 ** -_np.arange(1, 9, dtype=_np.float32)
    arrays = {
        "xT": a["x"][0].T.reshape(8, 128, 512).transpose(1, 0, 2),
        "memT": a["mem"][0].T.reshape(8, 128, 256).transpose(1, 0, 2),
        "pos": a["positions"], "cols": table, "const": _constants(_np),
        "bias": (slopes[:, None] * _np.arange(512, dtype=_np.float32)[None]).astype(_np.float32),
        "lat": tl(_np.concatenate([part["ql"], part["kvl"]], axis=1)), "kpe": tl(kpe, 96),
        "conv": cv, "gate": _np.concatenate([tl(part["ga"]), tl(part["gm"])]), "qm": tl(part["qm"]),
        "uq": tl(a["w_uq"][0], 96), "uk": tl(ukv[:, :, :64].reshape(256, 512), 64),
        "uv": _rows(_np, ukv[:, :, 64:].reshape(256, 512), 2),
        "mk": tl(mkv[:, :, :128].reshape(1024, 512)), "mv": _rows(_np, mkv[:, :, 128:].reshape(1024, 512), 2),
        "r": r, "br": br, "wo": tl(a["w_out"][0]),
        "wf": tl(wf, 8), "v2": _np.concatenate([_rows(_np, fv, 2), _rows(_np, dv, 2)]), "qk2": qk2,
        "wo2": tl(a["w_out_2"][0]), "wq": tl(a["peer_wq_2"][0]),
        "sk": a["peer_subkeys_2"][0].reshape(16, 128, 128).transpose(2, 0, 1),
        "uT": a["peer_u_2"][0].reshape(128, 128, 8, 128).transpose(0, 3, 2, 1).reshape(128, 128, 1024),
        "v": a["peer_v_2"][0].reshape(128, 128, 1024),
        "gf": a["normf_g_2"].reshape(1, 1024),
    }
    nc = _bacc.Bacc("TRN2", target_bir_lowering=False, num_devices=1)
    feed, t_in = {}, {}
    for name, x in arrays.items():
        x = _np.ascontiguousarray(x)
        feed[f"in_{name}"] = x
        t_in[name] = nc.dram_tensor(f"in_{name}", x.shape, _mybir.dt.from_np(x.dtype), kind="ExternalInput").ap()
    out = nc.dram_tensor("out_0", (512, 1024), _mybir.dt.float32, kind="ExternalOutput").ap()
    program(nc, t_in, out)
    res = _run(nc, [feed], core_ids=[0])
    return res.results[0]["out_0"].reshape(1, 512, 1024)
```
